# Optimizing a Trainium2 kernel written in Bass

```python
import jax
import jax.numpy as jnp
from jax import lax
import numpy as np

D_MODEL = 1024
BATCH = 1
SEQ = 512
DEPTH = 2

CTX_LEN = 256
GRID_W = 64
D_MIX = D_MODEL
CONV_CH = D_MIX // 2
RET_HEADS = 4
RET_DK = (D_MIX - CONV_CH) // RET_HEADS
RET_DV = RET_DK
RET_W = RET_HEADS * RET_DV
N_PROJ = 3 * CONV_CH + 4 * RET_W
CHUNK = 128
ROPE_BASE = 10000.0
PEER_HEADS = 8
N_KEYS = 128
N_EXPERTS = N_KEYS * N_KEYS
PEER_TOPK = 16
PEER_DK = 256
PEER_HALF = PEER_DK // 2
PEER_BLOCK = 128
ALPHA = float((2 * DEPTH) ** 0.25)
BETA = float((8 * DEPTH) ** -0.25)
LN_EPS = 1e-5
GN_EPS = 1e-5

kernel_name = 'hybrid_conv_retention_peer_dit'

def _layer_norm(x, g, b):
    xf = x.astype(jnp.float32)
    mu = jnp.mean(xf, -1, keepdims=True)
    var = jnp.mean(jnp.square(xf - mu), -1, keepdims=True)
    return ((xf - mu) * lax.rsqrt(var + LN_EPS)).astype(x.dtype) * g + b

def _modulate(x, shift, scale):
    return x * (1 + scale) + shift

def _conv3_grid(z, w):
    b, length, ch = z.shape
    rows = length // GRID_W
    zp = jnp.pad(z.reshape(b, rows, GRID_W, ch), ((0, 0), (0, 0), (1, 1), (0, 0)))
    y = zp[:, :, :-2] * w[:, 0] + zp[:, :, 1:-1] * w[:, 1] + zp[:, :, 2:] * w[:, 2]
    return y.reshape(b, length, ch)

def _conv3_seq(z, w):
    zp = jnp.pad(z, ((0, 0), (1, 1), (0, 0)))
    return zp[:, :-2] * w[:, 0] + zp[:, 1:-1] * w[:, 1] + zp[:, 2:] * w[:, 2]

def _rope_2d(t):
    length = t.shape[1]
    pos = jnp.arange(length)
    nf = RET_DK // 4
    inv = ROPE_BASE ** (-jnp.arange(nf, dtype=jnp.float32) / nf)

    def rot(u, p):
        ang = p.astype(jnp.float32)[:, None] * inv[None, :]
        cos = jnp.cos(ang)[None, :, None, :].astype(u.dtype)
        sin = jnp.sin(ang)[None, :, None, :].astype(u.dtype)
        u1, u2 = u[..., :nf], u[..., nf:]
        return jnp.concatenate([u1 * cos - u2 * sin, u1 * sin + u2 * cos], -1)

    half = RET_DK // 2
    return jnp.concatenate([rot(t[..., :half], pos // GRID_W), rot(t[..., half:], pos % GRID_W)], -1)

def _heads(t):
    return t.reshape(t.shape[:-1] + (RET_HEADS, RET_DK))

def _bhld(t):
    return jnp.transpose(t, (0, 2, 1, 3)).astype(jnp.float32)

def _log_gammas(offset):
    h = jnp.arange(RET_HEADS, dtype=jnp.float32)
    return jnp.log1p(-jnp.exp2(-(5.0 + offset + h)))

def _final_state(k, v, lg):
    length = k.shape[2]
    w = jnp.exp((length - 1 - jnp.arange(length, dtype=jnp.float32))[None, :] * lg[:, None])
    return jnp.einsum('bhld,bhle->bhde', k * w[None, :, :, None], v)

def _chunk_retention(q, k, v, lg, state0, inclusive):
    b, h, length, dk = q.shape
    dv = v.shape[-1]
    n = length // CHUNK
    qc = q.reshape(b, h, n, CHUNK, dk)
    kc = k.reshape(b, h, n, CHUNK, dk)
    vc = v.reshape(b, h, n, CHUNK, dv)
    pos = jnp.arange(CHUNK, dtype=jnp.float32)
    diff = pos[:, None] - pos[None, :]
    mask = diff >= 0 if inclusive else diff > 0
    dmat = jnp.where(mask[None], jnp.exp(jnp.where(mask, diff, 0.0)[None] * lg[:, None, None]), 0.0)
    scores = jnp.einsum('bhncd,bhnsd->bhncs', qc, kc) * dmat[None, :, None]
    o_intra = jnp.einsum('bhncs,bhnse->bhnce', scores, vc)
    k_w = kc * jnp.exp((CHUNK - 1 - pos)[None, :] * lg[:, None])[None, :, None, :, None]
    upd = jnp.einsum('bhnsd,bhnse->bhnde', k_w, vc)
    chunk_decay = jnp.exp(CHUNK * lg)[None, :, None, None]

    def step(s, u):
        return chunk_decay * s + u, s

    _, s_prev = lax.scan(step, state0, jnp.moveaxis(upd, 2, 0))
    s_prev = jnp.moveaxis(s_prev, 0, 2)
    q_w = qc * jnp.exp((pos + 1)[None, :] * lg[:, None])[None, :, None, :, None]
    o_cross = jnp.einsum('bhncd,bhnde->bhnce', q_w, s_prev)
    return (o_intra + o_cross).reshape(b, h, length, dv)

def _retention_bidir(q, k, v, s_f, s_b):
    o_f = _chunk_retention(q, k, v, _log_gammas(0.0), s_f, True)
    o_b = jnp.flip(_chunk_retention(jnp.flip(q, 2), jnp.flip(k, 2), jnp.flip(v, 2),
                                    _log_gammas(0.5), s_b, False), 2)
    return o_f + o_b

def _retention_out(o, g):
    mu = jnp.mean(o, -1, keepdims=True)
    var = jnp.mean(jnp.square(o - mu), -1, keepdims=True)
    on = (o - mu) * lax.rsqrt(var + GN_EPS)
    b, h, length, dv = o.shape
    on = jnp.transpose(on, (0, 2, 1, 3)).reshape(b, length, h * dv).astype(g.dtype)
    return jax.nn.silu(g) * on

def _token_mixer(h_lat, h_ctx, w_in, conv_w, w_out, with_ctx_out):
    scale_k = RET_DK ** -0.5
    bg, cg, hx, q, k, v, g = jnp.split(h_lat @ w_in, 7, axis=-1)
    conv_lat = bg * _conv3_grid(cg * hx, conv_w)
    q_l = _bhld(_rope_2d(_heads(q)))
    k_l = _bhld(_rope_2d(_heads(k))) * scale_k
    v_l = _bhld(_heads(v))
    k0 = 3 * CONV_CH + RET_W
    if with_ctx_out:
        bgc, cgc, hxc, qc, kc, vc, gc = jnp.split(h_ctx @ w_in, 7, axis=-1)
    else:
        kc, vc = jnp.split(h_ctx @ w_in[:, k0:k0 + 2 * RET_W], 2, axis=-1)
    k_c = _bhld(_heads(kc)) * scale_k
    v_c = _bhld(_heads(vc))
    s_f = _final_state(k_c, v_c, _log_gammas(0.0))
    s_b = _final_state(jnp.flip(k_c, 2), jnp.flip(v_c, 2), _log_gammas(0.5))
    ret_lat = _retention_out(_retention_bidir(q_l, k_l, v_l, s_f, s_b), g)
    y_lat = jnp.concatenate([conv_lat, ret_lat], -1) @ w_out
    if not with_ctx_out:
        return y_lat, None
    conv_ctx = bgc * _conv3_seq(cgc * hxc, conv_w)
    zero = jnp.zeros_like(s_f)
    ret_ctx = _retention_out(_retention_bidir(_bhld(_heads(qc)), k_c, v_c, zero, zero), gc)
    y_ctx = jnp.concatenate([conv_ctx, ret_ctx], -1) @ w_out
    return y_lat, y_ctx

def _peer_ffn(h, wq, keys, u, v):
    b, length, d = h.shape
    blocks = h.reshape(-1, PEER_BLOCK, d)

    def one(hb):
        q = (hb @ wq).reshape(PEER_BLOCK, PEER_HEADS, 2, PEER_HALF)
        s = jnp.einsum('thpd,pnd->thpn', q, keys).astype(jnp.float32)
        sv, si = lax.top_k(s, PEER_TOPK)
        cand = sv[:, :, 0, :, None] + sv[:, :, 1, None, :]
        cv, ci = lax.top_k(cand.reshape(PEER_BLOCK, PEER_HEADS, PEER_TOPK * PEER_TOPK), PEER_TOPK)
        i1 = jnp.take_along_axis(si[:, :, 0], ci // PEER_TOPK, axis=-1)
        i2 = jnp.take_along_axis(si[:, :, 1], ci % PEER_TOPK, axis=-1)
        e = i1 * N_KEYS + i2
        gate = jax.nn.softmax(cv, axis=-1)
        act = jax.nn.gelu(jnp.einsum('thkd,td->thk', jnp.take(u, e, axis=0), hb), approximate=False)
        return jnp.einsum('thk,thkd->td', (gate * act).astype(hb.dtype), jnp.take(v, e, axis=0))

    return lax.map(one, blocks).reshape(b, length, d)

def setup_inputs(seed: int = 0) -> dict:
    key = jax.random.key(seed)
    ks = jax.random.split(key, 17)
    n = jax.random.normal
    f32 = jnp.float32
    col_scale = jnp.concatenate([
        jnp.ones((2 * CONV_CH,), f32), jnp.full((CONV_CH,), BETA, f32),
        jnp.ones((2 * RET_W,), f32), jnp.full((RET_W,), BETA, f32),
        jnp.ones((RET_W,), f32)])
    return {
        'x': n(ks[0], (BATCH, SEQ, D_MODEL), f32),
        'c': n(ks[1], (BATCH, D_MODEL), f32),
        'ctx': n(ks[2], (BATCH, CTX_LEN, D_MODEL), f32),
        'c_ctx': n(ks[3], (D_MODEL,), f32),
        'w_mod': n(ks[4], (DEPTH, D_MODEL, 6 * D_MODEL), f32) * D_MODEL ** -0.5,
        'b_mod': 0.02 * n(ks[5], (DEPTH, 6 * D_MODEL), f32),
        'w_in': n(ks[6], (DEPTH, D_MODEL, N_PROJ), f32) * (D_MODEL ** -0.5) * col_scale,
        'conv_w': n(ks[7], (DEPTH, CONV_CH, 3), f32) * 3 ** -0.5,
        'w_out': n(ks[8], (DEPTH, D_MIX, D_MODEL), f32) * (D_MIX ** -0.5) * BETA,
        'ln1_g': 1.0 + 0.02 * n(ks[9], (DEPTH, D_MODEL), f32),
        'ln1_b': 0.02 * n(ks[10], (DEPTH, D_MODEL), f32),
        'peer_wq': n(ks[11], (DEPTH, D_MODEL, PEER_HEADS * PEER_DK), f32) * D_MODEL ** -0.5,
        'peer_keys': n(ks[12], (DEPTH, 2, N_KEYS, PEER_HALF), f32) * PEER_HALF ** -0.5,
        'peer_u': n(ks[13], (DEPTH, N_EXPERTS, D_MODEL), f32) * D_MODEL ** -0.5,
        'peer_v': n(ks[14], (DEPTH, N_EXPERTS, D_MODEL), f32) * BETA,
        'ln2_g': 1.0 + 0.02 * n(ks[15], (DEPTH, D_MODEL), f32),
        'ln2_b': 0.02 * n(ks[16], (DEPTH, D_MODEL), f32),
    }

def reference(x, c, ctx, c_ctx, w_mod, b_mod, w_in, conv_w, w_out, ln1_g, ln1_b,
              peer_wq, peer_keys, peer_u, peer_v, ln2_g, ln2_b):
    sc = jax.nn.silu(c)
    scc = jax.nn.silu(c_ctx)
    x_lat, x_ctx = x, ctx
    for l in range(DEPTH):
        last = l == DEPTH - 1
        m_lat = [m[:, None, :] for m in jnp.split(sc @ w_mod[l] + b_mod[l], 6, axis=-1)]
        m_ctx = jnp.split(scc @ w_mod[l] + b_mod[l], 6, axis=-1)
        h_lat = _modulate(x_lat, m_lat[0], m_lat[1])
        h_ctx = _modulate(x_ctx, m_ctx[0], m_ctx[1])
        y_lat, y_ctx = _token_mixer(h_lat, h_ctx, w_in[l], conv_w[l], w_out[l], not last)
        x_lat = _layer_norm(ALPHA * x_lat + m_lat[2] * y_lat, ln1_g[l], ln1_b[l])
        h2 = _modulate(x_lat, m_lat[3], m_lat[4])
        f_lat = _peer_ffn(h2, peer_wq[l], peer_keys[l], peer_u[l], peer_v[l])
        x_lat = _layer_norm(ALPHA * x_lat + m_lat[5] * f_lat, ln2_g[l], ln2_b[l])
        if not last:
            x_ctx = _layer_norm(ALPHA * x_ctx + m_ctx[2] * y_ctx, ln1_g[l], ln1_b[l])
            h2c = _modulate(x_ctx, m_ctx[3], m_ctx[4])
            f_ctx = _peer_ffn(h2c, peer_wq[l], peer_keys[l], peer_u[l], peer_v[l])
            x_ctx = _layer_norm(ALPHA * x_ctx + m_ctx[5] * f_ctx, ln2_g[l], ln2_b[l])
    return x_lat


_drawn_inputs = setup_inputs


def setup_inputs(seed=0):
    import zlib

    import numpy as np

    out = dict(_drawn_inputs(seed))
    spreads = {}
    factors = {}
    for name, (base, spread) in spreads.items():
        noise = np.random.default_rng([zlib.crc32(name.encode()), seed]).standard_normal(out[name].shape)
        drawn = base * np.exp(spread * noise) if base else spread * noise
        out[name] = jnp.asarray(drawn.astype(out[name].dtype))
    for name, factor in factors.items():
        out[name] = (out[name] * factor).astype(out[name].dtype)
    return out
```

```python
from contextlib import ExitStack

import concourse.bass as bass
from concourse import mybir

F32 = mybir.dt.float32
F16 = mybir.dt.float16
U32 = mybir.dt.uint32
ALU = mybir.AluOpType
ACT = mybir.ActivationFunctionType
AX = mybir.AxisListType

P = 128
D = 1024
KC = D // P
SEQ, CTX = 512, 256
LAT_B, CTX_B = SEQ // P, CTX // P
NBLK = LAT_B + CTX_B
TOK = NBLK * P
DEPTH = 2
GRID = 64
CONV = D // 2
CCT = CONV // P
HEADS = 4
NCOL = 7 * CCT
ALPHA = float((2 * DEPTH) ** 0.25)
EPS = 1e-5
NKEY = 128
PH, TOPK = 8, 16
NMOD = 6 * KC
MODG = 4
NEG = -3.0e38
RECTS = [(0, 1, 16, 0), (1, 3, 8, 16), (4, 4, 4, 40), (8, 8, 1, 56)]
NCAND = 64
GRP = 4
NGRP = NKEY // GRP
QT = 8
S_H, S_U, S_W, S_V = 16.0, 1024.0, 256.0, 256.0
STRIP1, STRIP2 = SEQ + 384, SEQ + 128


def blocks_of(layer):
    return NBLK if layer < DEPTH - 1 else LAT_B


def nscore(layer):
    return NBLK + (CTX_B if blocks_of(layer) > LAT_B else 0)


def spans_of(layer):
    return [(0, 384), (384, 384)] if layer < DEPTH - 1 else [(0, 512)]


def build(nc, t):
    with ExitStack() as ctx:
        def sb(name, shape, dt=F32):
            return ctx.enter_context(nc.sbuf_tensor(name, shape, dt))

        def sem(name):
            return ctx.enter_context(nc.semaphore(name))

        layer_sems = []

        def persem(name):
            layer_sems.append(sem(name))
            return layer_sems[-1:] * DEPTH

        x = sb("x", [P, NBLK, D])
        ident = sb("ident", [P, P])
        iota = sb("iota", [P, P])
        ones = sb("ones", [P, P])
        perm = sb("perm", [P, P])
        cT = sb("cT", [P, KC, 2])
        sT = sb("sT", [P, KC, 2])
        bmod = sb("bmod", [P, NMOD])
        modc = sb("modc", [P, NMOD, 2])
        eps = sb("eps", [P, 1])
        gate = sb("gate", [P, 2, D])
        lng = sb("lng", [P, D])
        lnb = sb("lnb", [P, D])
        st = sb("st", [P, 2, 6])
        mv = sb("mv", [P, NBLK, 2])
        sd = sb("sd", [P, NBLK])
        rs = sb("rs", [P, NBLK])

        ARENA = 40500
        arena = sb("arena", [P, ARENA])
        at = [0]

        def take(*shape, dt=F32, where=None):
            n = 1
            for s in shape:
                n *= s
            words = n if dt != F16 else n // 2
            a = at[0] if where is None else where
            assert a + words <= ARENA, (a, words)
            if where is None:
                at[0] = a + words
            v = arena[:, a:a + words]
            if dt != F32:
                v = v.bitcast(dt)
            if len(shape) == 1:
                return v
            names = "abcd"[:len(shape)]
            return v.rearrange(f"p ({' '.join(names)}) -> p {' '.join(names)}",
                               **{n_: s for n_, s in zip(names, shape)})

        at[0] = 0
        wmod = [take(MODG, KC, P) for _ in range(2)]
        dia = take(KC, P)
        at[0] = 0
        hT = take(KC, TOK)
        catT = take(KC, TOK)
        v_nat = take(NBLK, CONV)
        g_nat = take(NBLK, CONV)
        big = at[0]
        wv = take(KC, CONV)
        wg = take(KC, CONV)
        w_out = take(KC, D, where=big)
        wring = [take(KC, P) for _ in range(3)]
        strip1 = take(STRIP1)
        strip2 = take(STRIP2)
        ropeC = take(SEQ)
        ropeS = take(SEQ)
        convw = take(CCT, 3)
        rest = at[0]
        cg_sb = take(TOK)
        z_sb = take(TOK)
        y_sb = take(TOK)
        at[0] = rest
        q_raw = take(SEQ)
        k_raw = take(SEQ)
        qT = take(TOK)
        kT = take(TOK)
        Psc = take(NBLK, SEQ)
        Pctx = q_raw.rearrange("p (a b) -> p a b", a=CTX_B)
        gst = take(NBLK, 6)
        onrm = Psc.rearrange("p a b -> p (a b)")[:, 0:NBLK * P].rearrange("p (a b) -> p a b", a=NBLK)
        retn = Psc.rearrange("p a b -> p (a b)")[:, NBLK * P:2 * NBLK * P].rearrange("p (a b) -> p a b", a=NBLK)
        tmp = take(D, where=rest)
        h2T = hT
        at[0] = KC * TOK
        hh = take(KC, TOK, dt=F16)
        hl = take(KC, TOK, dt=F16)
        after_h = at[0]
        sv = take(NBLK, PH, 2, TOPK)
        si = take(NBLK, PH, 2, TOPK)
        after_s = at[0]
        wq = [take(KC, P) for _ in range(2)]
        keys = take(2, NKEY)
        qs = [take(TOK) for _ in range(2)]
        svj2 = [take(NBLK, TOPK) for _ in range(2)]
        sij2 = [take(NBLK, TOPK, dt=U32) for _ in range(2)]
        left = take(NBLK, NKEY)
        NR = PH * TOPK
        at[0] = 0
        cand = take(PH, NCAND)
        cand2 = take(PH, NCAND)
        cv = take(PH, TOPK)
        ci = take(PH, TOPK, dt=U32)
        shifted = take(2, NR, dt=U32)
        pos = take(3, NR)
        inrect = take(3, NR)
        part = take(6, NR)
        rank = take(2, NR)
        route = take(3, NR)
        gsum = take(PH)
        hot = take(NR, TOPK)
        assert at[0] <= KC * TOK
        at[0] = after_s
        gbuf = take(NKEY, P)
        routeT = take(3, P)
        oh1 = take(QT, NKEY)
        oh2 = take(QT, NKEY)
        at[0] = 0
        facc = take(NBLK, D)
        at[0] = after_h
        uraw = [take(KC, P) for _ in range(2)]
        vraw = [take(D) for _ in range(2)]
        ush = [take(KC, P, dt=F16) for _ in range(2)]
        usl = [take(KC, P, dt=F16) for _ in range(2)]
        vsh = take(GRP, D, dt=F16)
        vsl = take(GRP, D, dt=F16)
        graw = take(GRP, NBLK, P)
        actb = [take(TOK) for _ in range(2)]
        wf = [take(TOK) for _ in range(2)]
        wth = take(GRP, TOK, dt=F16)
        wtl = take(GRP, TOK, dt=F16)
        ftmp = take(D, where=after_h)
        dia2 = take(KC, P, where=after_h + D)

        ps = [ctx.enter_context(nc.psum_tensor(f"ps{i}", [P, 512], F32)) for i in range(8)]

        consts_in = sem("consts_in")
        x_in = sem("x_in")
        silu_ok = sem("silu_ok")
        eps_ok = sem("eps_ok")
        stage_done = sem("stage_done")
        out_done = sem("out_done")
        dve_chain = sem("dve_chain")
        dve_held = sem("dve_held")
        wmod_in = [persem(f"wmod_in{s}_") for s in range(2)]
        rows_in = persem("rows_in")
        bmod_in = persem("bmod_in")
        mod_mm = persem("mod_mm")
        modc_ok = persem("modc_ok")
        dia_ok = persem("dia_ok")
        gate_mm = persem("gate_mm")
        gate_ok = persem("gate_ok")
        tr_mm = [persem(f"tr_mm{k}_") for k in range(2)]
        tr_dve = [persem(f"tr_dve{k}_") for k in range(2)]
        tr_act = [persem(f"tr_act{k}_") for k in range(2)]
        wv_in = persem("wv_in")
        wg_in = persem("wg_in")
        vg_mm = persem("vg_mm")
        vg_ev = persem("vg_ev")
        wout_in = persem("wout_in")
        cw_in = persem("cw_in")
        wr_in = [persem(f"wr_in{r}_") for r in range(3)]
        conv_mm = persem("conv_mm")
        cg_ev = persem("cg_ev")
        conv_ok = persem("conv_ok")
        strip_in = persem("strip_in")
        qk_mm = persem("qk_mm")
        qk_ev = persem("qk_ev")
        rot_mm = persem("rot_mm")
        rope_ok = persem("rope_ok")
        sc_mm = persem("sc_mm")
        p_ok = persem("p_ok")
        o_mm = persem("o_mm")
        var_ok = persem("var_ok")
        sd_ok = persem("sd_ok")
        ret_ok = persem("ret_ok")
        retT_mm = persem("retT_mm")
        head_ok = persem("head_ok")
        y_mm = persem("y_mm")
        y_used = persem("y_used")
        lnvar_ok = [persem(f"lnvar_ok{k}_") for k in range(2)]
        lnsd_ok = [persem(f"lnsd_ok{k}_") for k in range(2)]
        x_ok = persem("x_ok")
        wq_in = [persem(f"wq_in{s}_") for s in range(2)]
        keys_in = persem("keys_in")
        hh_ok = persem("hh_ok")
        q_mm = persem("q_mm")
        q_ev = persem("q_ev")
        s_mm = persem("s_mm")
        topk_ok = persem("topk_ok")
        expo_in = persem("expo_in")
        expo_ok = persem("expo_ok")
        route_ok = persem("route_ok")
        routeT_mm = persem("routeT_mm")
        routeT_ok = persem("routeT_ok")
        hot_ok = persem("hot_ok")
        g_mm = persem("g_mm")
        g_ev = persem("g_ev")
        g_out = persem("g_out")
        u_in = [persem(f"u_in{s}_") for s in range(2)]
        v_in = [persem(f"v_in{s}_") for s in range(2)]
        g_in = [persem(f"g_in{s}_") for s in range(GRP)]
        uh_ok = persem("uh_ok")
        ul_ok = persem("ul_ok")
        vh_ok = persem("vh_ok")
        vl_ok = persem("vl_ok")
        u_mm = persem("u_mm")
        gelu_ok = persem("gelu_ok")
        wf_ok = persem("wf_ok")
        wh_ok = persem("wh_ok")
        wl_ok = persem("wl_ok")
        v_mm = persem("v_mm")
        f_ok = persem("f_ok")
        rows2_in = persem("rows2_in")
        dia2_ok = persem("dia2_ok")
        gate2_mm = persem("gate2_mm")
        gate2_ok = persem("gate2_ok")
        x2_ok = persem("x2_ok")

        class Own:

            def __init__(self, eng, s):
                self.eng, self.s, self.n = eng, s, 0

            def link(self, ins):
                self.n += 1
                ins.then_inc(self.s, 1)
                self.eng.wait_ge(self.s, self.n)

            def clear(self):
                if self.n:
                    self.eng.sem_clear(self.s)
                    self.n = 0

        class Stages:

            def __init__(self, eng):
                self.eng, self.n = eng, 0

            def end(self):
                self.n += 1
                self.eng.drain().then_inc(stage_done, 1)
                self.eng.wait_ge(stage_done, 4 * self.n)

            def begin(self):
                self.end()
                self.eng.drain()

        def new_layer(sp):
            nums = sorted(s.num for s in layer_sems)
            runs = [i for i in range(len(nums)) if not i or nums[i] != nums[i - 1] + 1] + [len(nums)]
            for a, b in zip(runs, runs[1:]):
                sp.sem_clear(range(nums[a], nums[b - 1] + 1))

        def ds(i, n=1):
            return bass.ds(i, n)

        NMG = NMOD // MODG
        block = ctx.enter_context(nc.Block())

        @block.sync
        def _(sp):
            stages = Stages(sp)

            def modulation(l):
                if l == 0:
                    for dst, src in ((ident, "ident"), (iota, "iota"), (perm, "perm")):
                        sp.dma_start(dst[:, :], t[src]).then_inc(consts_in, 16)
                    sp.dma_start(cT[:, :, :], t["c2"]).then_inc(consts_in, 16)
                    sp.dma_start(x[:, :, :], t["x"].rearrange("(b p) d -> p b d", p=P)).then_inc(x_in, 16)
                sp.dma_start(bmod[:, :], t["b_mod"][l]).then_inc(bmod_in[l], 16)
                for s in range(2):
                    sp.dma_start(wmod[s], t["w_mod"][l, s]).then_inc(wmod_in[s][l], 16)
                with sp.Fori(1, NMG // 2) as i:
                    for s in range(2):
                        sp.wait_ge(mod_mm[l], i * 2 + (s - 1))
                        sp.dma_start(wmod[s], t["w_mod"][l, ds(i * 2 + s)].rearrange("g p a b c -> (g p) a b c")).then_inc(wmod_in[s][l], 16)
                sp.dma_start(lng[:, :], t["ln"][l, 0:1, :].to_broadcast([P, D])).then_inc(rows_in[l], 16)
                sp.dma_start(lnb[:, :], t["ln"][l, 1:2, :].to_broadcast([P, D])).then_inc(rows_in[l], 16)

            def w_tile(dst, l, tile, s):
                sp.dma_start(dst, t["w_in"][l, ds(tile)].rearrange("g p a b -> (g p) a b")).then_inc(s, 16)

            def mixer(l):
                sp.dma_start(wv, t["w_v"][l]).then_inc(wv_in[l], 16)
                sp.dma_start(wg, t["w_g"][l]).then_inc(wg_in[l], 16)
                sp.dma_start(convw, t["conv_w"][l]).then_inc(cw_in[l], 16)
                sp.dma_start(ropeC, t["ropeC"]).then_inc(cw_in[l], 16)
                sp.dma_start(ropeS, t["ropeS"]).then_inc(cw_in[l], 16)
                first = (CCT, 2 * CCT, 0)
                for r in range(3):
                    w_tile(wring[r], l, first[r], wr_in[r][l])
                sp.dma_start(strip1, t["strip1"][0]).then_inc(strip_in[l], 16)
                sp.dma_start(strip2, t["strip2"][0]).then_inc(strip_in[l], 16)
                sp.wait_ge(vg_mm[l], NBLK + blocks_of(l))
                sp.dma_start(w_out, t["w_out"][l]).then_inc(wout_in[l], 16)
                with sp.Fori(1, CCT) as i:
                    for r in range(3):
                        sp.wait_ge(conv_mm[l], i * 3 + (r - 2))
                        w_tile(wring[r], l, i + first[r], wr_in[r][l])
                for r in range(2):
                    sp.wait_ge(conv_mm[l], 3 * CCT + r - 2)
                    w_tile(wring[r], l, (3 + r) * CCT, wr_in[r][l])
                with sp.Fori(1, HEADS) as i:
                    for r in range(2):
                        sp.wait_ge(qk_mm[l], i * 2 + (r - 1))
                        w_tile(wring[r], l, i + (3 + r) * CCT, wr_in[r][l])
                    sp.wait_ge(p_ok[l], i * nscore(l))
                    sp.dma_start(strip1, t["strip1"][ds(i)].rearrange("g p a -> (g p) a")).then_inc(strip_in[l], 16)
                    sp.dma_start(strip2, t["strip2"][ds(i)].rearrange("g p a -> (g p) a")).then_inc(strip_in[l], 16)

            def queries(l):
                sp.dma_start(keys, t["keys"][l]).then_inc(keys_in[l], 16)
                for s in range(2):
                    sp.dma_start(wq[s], t["w_q"][l, s]).then_inc(wq_in[s][l], 16)
                with sp.Fori(1, PH) as i:
                    for s in range(2):
                        sp.wait_ge(q_mm[l], i * 2 + (s - 1))
                        sp.dma_start(wq[s], t["w_q"][l, ds(i * 2 + s)].rearrange("g p a b -> (g p) a b")).then_inc(wq_in[s][l], 16)

            def routing(l):
                sp.sem_inc(g_out[l], 16)
                with sp.Fori(0, blocks_of(l)) as b:
                    sp.wait_ge(g_ev[l], b * (P // 4) + (P // 4 + 2))
                    sp.dma_start(t["gates"][ds(b)].rearrange("b p i t -> (b p) i t"), gbuf).then_inc(g_out[l], 16)
                sp.wait_ge(g_out[l], 16 * (blocks_of(l) + 1))

            def experts(l):
                NB = blocks_of(l)
                with sp.Fori(0, NGRP) as g:
                    for e in range(GRP):
                        s = e % 2
                        n = g * GRP + e
                        sp.wait_ge(ul_ok[l], n + 1)
                        sp.dma_start(uraw[s], t["peer_u"][l, ds(n)].rearrange("g p a b -> (g p) a b")).then_inc(u_in[s][l], 16)
                        sp.wait_ge(wf_ok[l], n + 1)
                        sp.dma_start(graw[:, e, 0:NB, :],
                                     t["gates"][0:NB, :, ds(n), :].rearrange("b p i t -> p (b i) t")).then_inc(g_in[e][l], 16)
                        sp.wait_ge(vl_ok[l], n + 1)
                        sp.dma_start(vraw[s], t["peer_v"][l, ds(n)].rearrange("g p a -> (g p) a")).then_inc(v_in[s][l], 16)
                sp.dma_start(lng[:, :], t["ln"][l, 2:3, :].to_broadcast([P, D])).then_inc(rows2_in[l], 16)
                sp.dma_start(lnb[:, :], t["ln"][l, 3:4, :].to_broadcast([P, D])).then_inc(rows2_in[l], 16)

            def norm2(l):
                if l == DEPTH - 1:
                    for b in range(LAT_B):
                        sp.wait_ge(x2_ok[l], b + 1)
                        sp.dma_start(t["out"][b * P:(b + 1) * P, :], x[:, b, :]).then_inc(out_done, 16)
                    sp.wait_ge(out_done, 16 * LAT_B)

            def nothing(l):
                pass

            for l in range(DEPTH):
                for stage in (modulation, nothing, mixer, nothing, queries, routing, experts, norm2):
                    stage(l)
                    stages.end()
                if l < DEPTH - 1:
                    new_layer(sp)
                    stages.begin()

        @block.tensor
        def _(pe):
            stages = Stages(pe)

            def mm(out, lhsT, rhs, start, stop):
                return pe.matmul(out, lhsT, rhs, start=start, stop=stop)

            def modulation(l):
                if l == 0:
                    pe.wait_ge(consts_in, 64)
                    pe.wait_ge(silu_ok, 1)
                with pe.Fori(0, NMG // 2) as i:
                    for s in range(2):
                        pe.wait_ge(wmod_in[s][l], i * 16 + 16)
                        for c in range(MODG):
                            for k in range(KC):
                                last = mm(ps[0][:, ds(i * (4 * MODG) + (s * 2 * MODG + 2 * c), 2)], wmod[s][:, c, k, :], sT[:, k, :], k == 0, k == KC - 1)
                        last.then_inc(mod_mm[l], 1)
                spread(l, dia_ok[l], gate_mm[l], gate_ok[l])

            def spread(l, ready, done, free):
                for r in range(2 if l == 0 else 1):
                    pe.wait_ge(ready, r + 1)
                    dd = dia if ready is dia_ok[l] else dia2
                    if r:
                        pe.wait_ge(free, r)
                    for k in range(KC):
                        last = mm(ps[1 + k // 4][:, (k % 4) * P:(k % 4 + 1) * P], ones[:, :], dd[:, k, :], True, True)
                    last.then_inc(done, 1)

            def to_columns(l, k, b):
                for half in range(2):
                    n = 2 * b + half
                    if n >= 4:
                        pe.wait_ge((tr_act if n % 2 else tr_dve)[k][l], (n - 4) // 2 + 1)
                    for j in range(4):
                        c = half * 4 + j
                        last = pe.transpose(ps[4 + n % 4][:, j * P:(j + 1) * P], x[:, b, c * P:(c + 1) * P], ident[:, :])
                    last.then_inc(tr_mm[k][l], 1)

            def columns(l):
                if l == 0:
                    pe.wait_ge(x_in, 16)
                for b in range(NBLK):
                    to_columns(l, 0, b)

            def mixer(l):
                NB = blocks_of(l)
                TC = [(0, SEQ), (SEQ, CTX)]
                n = 0
                for b in range(NBLK):
                    for w, s, on_ in ((wv, wv_in, True), (wg, wg_in, b < NB)):
                        if not on_:
                            continue
                        if b == 0:
                            pe.wait_ge(s[l], 16)
                        if n >= 2:
                            pe.wait_ge(vg_ev[l], n - 1)
                        for k in range(KC):
                            last = mm(ps[6 + n % 2][:, :], hT[:, k, b * P:(b + 1) * P], w[:, k, :], k == 0, k == KC - 1)
                        last.then_inc(vg_mm[l], 1)
                        n += 1
                with pe.Fori(0, CCT) as i:
                    pe.wait_ge(conv_ok[l], i + 1)
                    for r in range(3):
                        pe.wait_ge(wr_in[r][l], i * 16 + 16)
                        for z, (c0, w) in enumerate(TC[:1 if NB == LAT_B else 2]):
                            for k in range(KC):
                                last = mm(ps[2 * r + z][:, 0:w], wring[r][:, k, :], hT[:, k, c0:c0 + w], k == 0, k == KC - 1)
                        last.then_inc(conv_mm[l], 1)
                pe.wait_ge(conv_ok[l], CCT + 1)
                with pe.Fori(0, HEADS) as i:
                    pe.wait_ge(head_ok[l], i + 1)
                    for r in range(2):
                        pe.wait_ge(wr_in[r][l], i * 16 + 16 * (CCT + 1))
                        for z, (c0, w) in enumerate(TC):
                            if z and r == 0 and NB == LAT_B:
                                continue
                            for k in range(KC):
                                last = mm(ps[2 * r + z][:, 0:w], wring[r][:, k, :], hT[:, k, c0:c0 + w], k == 0, k == KC - 1)
                        last.then_inc(qk_mm[l], 1)
                    for r, raw in enumerate((q_raw, k_raw)):
                        pe.wait_ge(qk_ev[l], i * 2 + (r + 1))
                        mm(ps[4 + r][:, :], perm[:, :], raw, True, True).then_inc(rot_mm[l], 1)
                    pe.wait_ge(rope_ok[l], i * 2 + 2)
                    NS = nscore(l)
                    for n in range(NS):
                        if n >= 2:
                            pe.wait_ge(p_ok[l], i * NS + (n - 1))
                        if n < NBLK:
                            mm(ps[6 + n % 2][:, :], kT[:, n * P:(n + 1) * P], qT[:, 0:SEQ], True, True).then_inc(sc_mm[l], 1)
                        else:
                            s = n - NBLK + LAT_B
                            mm(ps[6 + n % 2][:, 0:CTX], kT[:, s * P:(s + 1) * P], qT[:, SEQ:TOK], True, True).then_inc(sc_mm[l], 1)
                    pe.wait_ge(p_ok[l], i * NS + NS)
                    for b in range(LAT_B):
                        for s in range(NBLK):
                            last = mm(ps[4][:, b * P:(b + 1) * P], Psc[:, s, b * P:(b + 1) * P], v_nat[:, s, ds(i * P, P)], s == 0, s == NBLK - 1)
                    if NB > LAT_B:
                        for b in range(CTX_B):
                            for s in range(CTX_B):
                                last = mm(ps[5][:, b * P:(b + 1) * P], Pctx[:, s, b * P:(b + 1) * P], v_nat[:, LAT_B + s, ds(i * P, P)], s == 0, s == CTX_B - 1)
                    last.then_inc(o_mm[l], 1)
                    pe.wait_ge(ret_ok[l], i + 1)
                    for b in range(NB):
                        last = pe.transpose(ps[b // 4][:, (b % 4) * P:(b % 4 + 1) * P], retn[:, b, :], ident[:, :])
                    last.then_inc(retT_mm[l], 1)

            def project(l):
                NB = blocks_of(l)
                pe.wait_ge(wout_in[l], 16)
                for b in range(NB + 1):
                    if b < NB:
                        if b >= 2:
                            pe.wait_ge(y_used[l], b - 1)
                        for half in range(2):
                            for k in range(KC):
                                last = mm(ps[b % 2 * 2 + half][:, :], catT[:, k, b * P:(b + 1) * P],
                                          w_out[:, k, half * 512:(half + 1) * 512], k == 0, k == KC - 1)
                        last.then_inc(y_mm[l], 1)
                    if b:
                        pe.wait_ge(x_ok[l], b)
                        to_columns(l, 1, b - 1)

            def queries(l):
                NB = blocks_of(l)
                pe.wait_ge(keys_in[l], 16)
                with pe.Fori(0, PH) as i:
                    for s in range(2):
                        pe.wait_ge(wq_in[s][l], i * 16 + 16)
                        pe.wait_ge(q_ev[l], i * 2 + (s + 1))
                        for z, (c0, w) in enumerate(spans_of(l)):
                            for k in range(KC):
                                last = mm(ps[2 * s + z][:, 0:w], wq[s][:, k, :], h2T[:, k, c0:c0 + w], k == 0, k == KC - 1)
                        last.then_inc(q_mm[l], 1)
                    for s in range(2):
                        pe.wait_ge(q_ev[l], i * 2 + (s + 3))
                        pe.wait_ge(topk_ok[l], i * 2 + (s + 1))
                        for b in range(NB):
                            last = mm(ps[4 + 2 * s + b // 4][:, (b % 4) * P:(b % 4 + 1) * P], qs[s][:, b * P:(b + 1) * P], keys[:, s, :], True, True)
                        last.then_inc(s_mm[l], 1)

            def routing(l):
                with pe.Fori(0, blocks_of(l)) as b:
                    pe.wait_ge(route_ok[l], b + 1)
                    for j in range(3):
                        last = pe.transpose(ps[0][:, j * P:(j + 1) * P], route[:, j, :], ident[:, :])
                    last.then_inc(routeT_mm[l], 1)
                    with pe.Fori(0, P // QT) as i:
                        for h in range(2):
                            n = b * (P // 4) + i * 2
                            pe.wait_ge(hot_ok[l], n + (h + 1))
                            pe.wait_ge(g_ev[l], n + (h + 1))
                            for j in range(4):
                                last = mm(ps[1 + h][:, j * P:(j + 1) * P], oh2[:, 4 * h + j, :], oh1[:, 4 * h + j, :], True, True)
                            last.then_inc(g_mm[l], 1)

            def experts(l):
                NB = blocks_of(l)
                outs = [(b, half) for b in range(NB) for half in range(2)]
                with pe.Fori(0, NGRP) as g:
                    for e in range(GRP):
                        n = g * GRP + e
                        s = e % 2
                        pe.wait_ge(uh_ok[l], n + 1)
                        pe.wait_ge(ul_ok[l], n + 3)
                        pe.wait_ge(gelu_ok[l], n + 1)
                        for z, (c0, w) in enumerate(spans_of(l)):
                            out = ps[2 * s + z][:, 0:w]
                            for k in range(KC):
                                mm(out, ush[s][:, k, :], hh[:, k, c0:c0 + w], k == 0, False)
                                mm(out, ush[s][:, k, :], hl[:, k, c0:c0 + w], False, False)
                                last = mm(out, usl[s][:, k, :], hh[:, k, c0:c0 + w], False, k == KC - 1)
                        last.then_inc(u_mm[l], 1)
                    for r in range(0, len(outs), 4):
                        for es in (range(GRP - 1), (GRP - 1,)):
                            for j in range(4):
                                b, half = outs[r + j]
                                if r == 0 and j == 0:
                                    m = g * GRP + es[-1]
                                    pe.wait_ge(wh_ok[l], m + 1)
                                    pe.wait_ge(wl_ok[l], m + 1)
                                    pe.wait_ge(vh_ok[l], m + 1)
                                    pe.wait_ge(vl_ok[l], m + 3)
                                if es != (GRP - 1,):
                                    pe.wait_ge(f_ok[l], g * len(outs) + (r + j + 1))
                                for e in es:
                                    wh, wl = wth[:, e, b * P:(b + 1) * P], wtl[:, e, b * P:(b + 1) * P]
                                    vh, vl = (v[:, e, half * 512:(half + 1) * 512] for v in (vsh, vsl))
                                    mm(ps[4 + j][:, :], wh, vh, e == 0, False)
                                    mm(ps[4 + j][:, :], wh, vl, False, False)
                                    last = mm(ps[4 + j][:, :], wl, vh, False, e == GRP - 1)
                                if es == (GRP - 1,):
                                    last.then_inc(v_mm[l], 1)

            def norm2(l):
                spread(l, dia2_ok[l], gate2_mm[l], gate2_ok[l])

            for l in range(DEPTH):
                for stage in (modulation, columns, mixer, project, queries, routing, experts, norm2):
                    stage(l)
                    stages.end()
                if l < DEPTH - 1:
                    stages.begin()

        @block.scalar
        def _(act):
            stages = Stages(act)

            def copy(out, in_, scale=1.0):
                return act.activation(out, in_, ACT.Copy, scale=scale)

            def modulation(l):
                if l == 0:
                    act.wait_ge(consts_in, 64)
                    act.activation(sT[:, :, :], cT[:, :, :], ACT.Silu).then_inc(silu_ok, 1)
                    act.wait_ge(eps_ok, 1)
                spread(l, gate_mm[l], gate_ok[l])

            def spread(l, ready, done):
                for r in range(2 if l == 0 else 1):
                    act.wait_ge(ready, r + 1)
                    for half in range(2):
                        last = copy(gate[:, r, half * 512:(half + 1) * 512], ps[1 + half][:, :])
                    last.then_inc(done, 1)

            def to_columns(l, k, b):
                r = b // LAT_B
                n = 2 * b + 1
                act.wait_ge(tr_mm[k][l], n + 1)
                for j in range(4):
                    c = 4 + j
                    last = act.activation(hT[:, c, b * P:(b + 1) * P], ps[4 + n % 4][:, j * P:(j + 1) * P], ACT.Identity,
                                          bias=modc[:, 3 * k * KC + c, r:r + 1], scale=modc[:, (3 * k + 1) * KC + c, r:r + 1])
                last.then_inc(tr_act[k][l], 1)

            def columns(l):
                act.wait_ge(modc_ok[l], 1)
                for b in range(NBLK):
                    to_columns(l, 0, b)

            def mixer(l):
                NB = blocks_of(l)
                act.sem_inc(head_ok[l], 1)
                n = 0
                for b in range(NBLK):
                    act.wait_ge(vg_mm[l], n + 1)
                    copy(v_nat[:, b, :], ps[6 + n % 2][:, :]).then_inc(vg_ev[l], 1)
                    n += 1
                    if b < NB:
                        act.wait_ge(vg_mm[l], n + 1)
                        act.activation(g_nat[:, b, :], ps[6 + n % 2][:, :], ACT.Silu).then_inc(vg_ev[l], 1)
                        n += 1
                with act.Fori(0, CCT) as i:
                    act.wait_ge(conv_mm[l], i * 3 + 1)
                    act.wait_ge(conv_ok[l], i + 1)
                    last = copy(cg_sb[:, 0:SEQ], ps[0][:, :])
                    if NB > LAT_B:
                        last = copy(cg_sb[:, SEQ:TOK], ps[1][:, 0:CTX])
                    last.then_inc(cg_ev[l], 1)
                act.wait_ge(conv_ok[l], CCT + 1)
                with act.Fori(0, HEADS) as i:
                    for r, (raw, dst) in enumerate(((q_raw, qT), (k_raw, kT))):
                        act.wait_ge(qk_mm[l], i * 2 + (r + 1))
                        last = copy(raw, ps[2 * r][:, :])
                        if r or NB > LAT_B:
                            last = copy(dst[:, SEQ:TOK], ps[2 * r + 1][:, 0:CTX])
                        last.then_inc(qk_ev[l], 1)
                    act.wait_ge(var_ok[l], i + 1)
                    act.activation(sd[:, 0:NB], mv[:, 0:NB, 1], ACT.Sqrt, bias=eps[:, :]).then_inc(sd_ok[l], 1)
                    act.wait_ge(retT_mm[l], i + 1)
                    last = copy(catT[:, ds(i + CCT), 0:SEQ].rearrange("p a b -> p (a b)"), ps[0][:, :])
                    if NB > LAT_B:
                        last = copy(catT[:, ds(i + CCT), SEQ:TOK].rearrange("p a b -> p (a b)"), ps[1][:, 0:CTX])
                    last.then_inc(head_ok[l], 1)

            def deviation(l, k, b):
                act.wait_ge(lnvar_ok[k][l], b + 1)
                act.activation(sd[:, b:b + 1], mv[:, b, 1:2], ACT.Sqrt, bias=eps[:, :]).then_inc(lnsd_ok[k][l], 1)

            def project(l):
                NB = blocks_of(l)
                for b in range(NB + 1):
                    if b < NB:
                        deviation(l, 0, b)
                    if b:
                        to_columns(l, 1, b - 1)

            def queries(l):
                T = blocks_of(l) * P
                act.sem_inc(q_ev[l], 2)
                for k in range(KC):
                    copy(hh[:, k, 0:T], h2T[:, k, 0:T], S_H).then_inc(hh_ok[l], 1)
                with act.Fori(0, PH) as i:
                    for s in range(2):
                        act.wait_ge(q_mm[l], i * 2 + (s + 1))
                        for z, (c0, w) in enumerate(spans_of(l)):
                            last = copy(qs[s][:, c0:c0 + w], ps[2 * s + z][:, 0:w])
                        last.then_inc(q_ev[l], 1)

            def routing(l):
                act.sem_inc(g_ev[l], 2)
                with act.Fori(0, blocks_of(l)) as b:
                    act.wait_ge(expo_in[l], b + 1)
                    act.activation(route[:, 2, :], route[:, 2, :], ACT.Exp).then_inc(expo_ok[l], 1)
                    act.wait_ge(routeT_mm[l], b + 1)
                    copy(routeT.rearrange("p a b -> p (a b)"), ps[0][:, 0:3 * P]).then_inc(routeT_ok[l], 1)
                    act.wait_ge(g_out[l], b * 16 + 16)
                    with act.Fori(0, P // QT) as i:
                        for h in range(2):
                            act.wait_ge(g_mm[l], b * (P // 4) + i * 2 + (h + 3))
                            copy(gbuf[:, :, ds(i * QT + 4 * h, 4)], ps[1 + h][:, :].rearrange("p (j i) -> p i j", j=4)).then_inc(g_ev[l], 1)

            def experts(l):
                T = blocks_of(l) * P
                act.sem_inc(gelu_ok[l], 2)
                act.sem_inc(u_mm[l], 1)
                act.sem_inc(v_mm[l], 1)

                def group(g, more):
                    for e in range(GRP):
                        s = e % 2
                        n = g * GRP + e
                        if e < GRP - 1 or more:
                            u_split(n + 1, (e + 1) % 2, g * (8 * GRP) + 16 * ((e + 1) // 2 + 1))
                        if e == 0:
                            act.wait_ge(v_mm[l], g * (2 * blocks_of(l)) + 1)
                        act.wait_ge(v_in[s][l], g * (8 * GRP) + 16 * (e // 2 + 1))
                        copy(vsh[:, e, :], vraw[s], S_V).then_inc(vh_ok[l], 1)
                        act.wait_ge(u_mm[l], n + 2)
                        for z, (c0, w) in enumerate(spans_of(l)):
                            last = act.activation(actb[s][:, c0:c0 + w], ps[2 * s + z][:, 0:w], ACT.Gelu, scale=1.0 / (S_H * S_U))
                        last.then_inc(gelu_ok[l], 1)
                        act.wait_ge(wf_ok[l], n + (GRP + 1))
                        copy(wth[:, e, 0:T], wf[s][:, 0:T], S_W).then_inc(wh_ok[l], 1)

                def u_split(n, s, landed):
                    act.wait_ge(u_in[s][l], landed)
                    act.wait_ge(u_mm[l], n)
                    copy(ush[s], uraw[s], S_U).then_inc(uh_ok[l], 1)

                act.wait_ge(u_in[0][l], 16)
                copy(ush[0], uraw[0], S_U).then_inc(uh_ok[l], 1)
                with act.Fori(0, NGRP - 1) as g:
                    group(g, True)
                group(NGRP - 1, False)

            def norm2(l):
                spread(l, gate2_mm[l], gate2_ok[l])
                for b in range(blocks_of(l)):
                    deviation(l, 1, b)

            for l in range(DEPTH):
                for stage in (modulation, columns, mixer, project, queries, routing, experts, norm2):
                    stage(l)
                    stages.end()
                if l < DEPTH - 1:
                    stages.begin()


        @block.vector
        def _(dve):
            stages = Stages(dve)
            own = Own(dve, dve_chain)
            link = own.link

            def hold():
                dve.sem_inc(dve_held, 1)

            def tt(out, a, b, op):
                return dve.tensor_tensor(out, a, b, op)

            def modulation(l):
                if l == 0:
                    dve.memset(ones[:, :], 1.0)
                    dve.memset(eps[:, :], EPS).then_inc(eps_ok, 1)
                    dve.wait_ge(eps_ok, 1)
                    dve.wait_ge(consts_in, 64)
                dve.wait_ge(bmod_in[l], 16)
                dve.wait_ge(mod_mm[l], NMG)
                link(tt(modc[:, :, :], ps[0][:, 0:2 * NMOD].rearrange("p (a b) -> p a b", b=2),
                        bmod[:, :, None].to_broadcast([P, NMOD, 2]), ALU.add))
                dve.tensor_scalar(modc[:, KC:2 * KC, :], modc[:, KC:2 * KC, :], 1.0, None, ALU.add)
                dve.tensor_scalar(modc[:, 4 * KC:5 * KC, :], modc[:, 4 * KC:5 * KC, :], 1.0, None, ALU.add).then_inc(modc_ok[l], 1)
                dve.wait_ge(modc_ok[l], 1)
                diagonals(l, dia, 2 * KC, dia_ok[l], gate_mm[l])

            def diagonals(l, dd, col, ready, used):
                for r in range(2 if l == 0 else 1):
                    if r:
                        dve.wait_ge(used, r)
                    for k in range(KC):
                        last = dve.tensor_scalar(dd[:, k, :], ident[:, :], modc[:, col + k, r:r + 1], None, ALU.mult)
                    last.then_inc(ready, 1)

            def to_columns(l, k, b):
                r = b // LAT_B
                n = 2 * b
                dve.wait_ge(tr_mm[k][l], n + 1)
                for c in range(4):
                    last = dve.tensor_scalar(hT[:, c, b * P:(b + 1) * P], ps[4 + n % 4][:, c * P:(c + 1) * P],
                                             modc[:, (3 * k + 1) * KC + c, r:r + 1], modc[:, 3 * k * KC + c, r:r + 1], ALU.mult, ALU.add)
                last.then_inc(tr_dve[k][l], 1)

            def columns(l):
                for b in range(NBLK):
                    to_columns(l, 0, b)

            def taps(z, y, w0, w2):
                n = z.shape[-1]
                if len(z.shape) == 3:
                    link(dve.scalar_tensor_tensor(y[:, :, 1:n], z[:, :, 0:n - 1], w0, y[:, :, 1:n], ALU.mult, ALU.add))
                    link(dve.scalar_tensor_tensor(y[:, :, 0:n - 1], z[:, :, 1:n], w2, y[:, :, 0:n - 1], ALU.mult, ALU.add))
                else:
                    link(dve.scalar_tensor_tensor(y[:, 1:n], z[:, 0:n - 1], w0, y[:, 1:n], ALU.mult, ALU.add))
                    link(dve.scalar_tensor_tensor(y[:, 0:n - 1], z[:, 1:n], w2, y[:, 0:n - 1], ALU.mult, ALU.add))

            def mixer(l):
                NB = blocks_of(l)
                both = NB > LAT_B
                T = NB * P
                own.clear()
                dve.sem_inc(conv_ok[l], 1)
                dve.wait_ge(cw_in[l], 48)
                with dve.Fori(0, CCT) as i:
                    dve.wait_ge(cg_ev[l], i + 1)
                    dve.wait_ge(conv_mm[l], i * 3 + 2)
                    last = tt(z_sb[:, 0:SEQ], cg_sb[:, 0:SEQ], ps[2][:, :], ALU.mult)
                    if both:
                        last = tt(z_sb[:, SEQ:TOK], cg_sb[:, SEQ:TOK], ps[3][:, 0:CTX], ALU.mult)
                    link(last)
                    w = [convw[:, ds(i), j:j + 1].rearrange("p a b -> p (a b)") for j in range(3)]
                    link(dve.tensor_scalar(y_sb[:, 0:T], z_sb[:, 0:T], w[1], None, ALU.mult))
                    taps(z_sb[:, 0:SEQ].rearrange("p (r c) -> p r c", c=GRID), y_sb[:, 0:SEQ].rearrange("p (r c) -> p r c", c=GRID), w[0], w[2])
                    if both:
                        taps(z_sb[:, SEQ:TOK], y_sb[:, SEQ:TOK], w[0], w[2])
                    dve.wait_ge(conv_mm[l], i * 3 + 3)
                    last = tt(catT[:, ds(i), 0:SEQ].rearrange("p a b -> p (a b)"), y_sb[:, 0:SEQ], ps[4][:, :], ALU.mult)
                    if both:
                        last = tt(catT[:, ds(i), SEQ:TOK].rearrange("p a b -> p (a b)"), y_sb[:, SEQ:TOK], ps[5][:, 0:CTX], ALU.mult)
                    last.then_inc(conv_ok[l], 1)
                    own.clear()
                NS = nscore(l)
                with dve.Fori(0, HEADS) as i:
                    for r, (raw, dst) in enumerate(((q_raw, qT), (k_raw, kT))):
                        dve.wait_ge(rot_mm[l], i * 2 + (r + 1))
                        link(tt(dst[:, 0:SEQ], raw, ropeC, ALU.mult))
                        link(tt(raw, ps[4 + r][:, :], ropeS, ALU.mult))
                        tt(dst[:, 0:SEQ], dst[:, 0:SEQ], raw, ALU.add).then_inc(rope_ok[l], 1)
                    dve.wait_ge(rope_ok[l], i * 2 + 2)
                    dve.wait_ge(strip_in[l], i * 32 + 32)
                    for n in range(NS):
                        dve.wait_ge(sc_mm[l], i * NS + (n + 1))
                        if n < LAT_B:
                            a = 384 - P * n
                            tt(Psc[:, n, :], ps[6 + n % 2][:, :], strip1[:, a:a + SEQ], ALU.mult).then_inc(p_ok[l], 1)
                        elif n < NBLK:
                            a = P - P * (n - LAT_B)
                            tt(Psc[:, n, :], ps[6 + n % 2][:, :], strip2[:, a:a + SEQ], ALU.mult).then_inc(p_ok[l], 1)
                        else:
                            a = 384 - P * (n - NBLK)
                            tt(Pctx[:, n - NBLK, :], ps[6 + n % 2][:, 0:CTX], strip1[:, a:a + CTX], ALU.mult).then_inc(p_ok[l], 1)
                    dve.wait_ge(o_mm[l], i + 1)
                    for b in range(NB):
                        last = dve.bn_stats(gst[:, b, :], ps[4 + b // 4][:, (b % 4) * P:(b % 4 + 1) * P])
                    link(last)
                    for b in range(NB):
                        last = dve.bn_aggr(mv[:, b, :], gst[:, b, :])
                    last.then_inc(var_ok[l], 1)
                    dve.wait_ge(sd_ok[l], i + 1)
                    link(dve.reciprocal(rs[:, 0:NB], sd[:, 0:NB]))
                    for b in range(NB):
                        last = dve.tensor_scalar(onrm[:, b, :], ps[4 + b // 4][:, (b % 4) * P:(b % 4 + 1) * P], mv[:, b, 0:1], rs[:, b:b + 1], ALU.subtract, ALU.mult)
                    link(last)
                    tt(retn[:, 0:NB, :], onrm[:, 0:NB, :], g_nat[:, 0:NB, ds(i * P, P)], ALU.mult).then_inc(ret_ok[l], 1)
                    own.clear()

            def norm(l, k, b):
                xb = x[:, b, :]
                dve.bn_stats(st[:, 0, :], x[:, b, 0:512])
                link(dve.bn_stats(st[:, 1, :], x[:, b, 512:D]))
                dve.bn_aggr(mv[:, b, :], st[:, :, :]).then_inc(lnvar_ok[k][l], 1)
                dve.wait_ge(lnsd_ok[k][l], b + 1)
                link(dve.reciprocal(rs[:, b:b + 1], sd[:, b:b + 1]))
                link(dve.tensor_scalar(xb, xb, mv[:, b, 0:1], rs[:, b:b + 1], ALU.subtract, ALU.mult))
                link(tt(xb, xb, lng[:, :], ALU.mult))
                tt(xb, xb, lnb[:, :], ALU.add).then_inc((x_ok, x2_ok)[k][l], 1)
                dve.wait_ge((x_ok, x2_ok)[k][l], b + 1)

            def project(l):
                NB = blocks_of(l)
                dve.wait_ge(rows_in[l], 32)
                for b in range(NB + 1):
                    if b < NB:
                        dve.wait_ge(y_mm[l], b + 1)
                        for half in range(2):
                            c = slice(half * 512, (half + 1) * 512)
                            last = tt(tmp[:, c], ps[b % 2 * 2 + half][:, :], gate[:, b // LAT_B, c], ALU.mult)
                        last.then_inc(y_used[l], 1)
                        dve.wait_ge(y_used[l], b + 1)
                        link(dve.scalar_tensor_tensor(x[:, b, :], x[:, b, :], ALPHA, tmp, ALU.mult, ALU.add))
                        norm(l, 0, b)
                    if b:
                        to_columns(l, 1, b - 1)

            def queries(l):
                NB = blocks_of(l)
                T = NB * P
                dve.sem_inc(topk_ok[l], 2)
                for k in range(KC):
                    dve.wait_ge(hh_ok[l], k + 1)
                    dve.scalar_tensor_tensor(hl[:, k, 0:T], h2T[:, k, 0:T], S_H, hh[:, k, 0:T], ALU.mult, ALU.subtract)
                own.clear()
                with dve.Fori(0, PH) as i:
                    for s in range(2):
                        dve.wait_ge(s_mm[l], i * 2 + (s + 1))
                        svj, sij = svj2[s], sij2[s]
                        hold()
                        sc = [ps[4 + 2 * s + b // 4][:, (b % 4) * P:(b % 4 + 1) * P] for b in range(NB)]
                        for b in range(NB):
                            last = dve.max(svj[:, b, 0:8], sc[b])
                        link(last)
                        for b in range(NB):
                            dve.max_index(sij[:, b, 0:8], svj[:, b, 0:8], sc[b])
                        for b in range(NB):
                            last = dve.match_replace(left[:, b, :], svj[:, b, 0:8], sc[b], NEG)
                        link(last)
                        for b in range(NB):
                            last = dve.max(svj[:, b, 8:16], left[:, b, :])
                        link(last)
                        for b in range(NB):
                            last = dve.max_index(sij[:, b, 8:16], svj[:, b, 8:16], left[:, b, :])
                        link(last)
                        dve.tensor_copy(sv[:, 0:NB, ds(i), s, :].rearrange("p b a t -> p b (a t)"), svj[:, 0:NB, :])
                        dve.tensor_copy(si[:, 0:NB, ds(i), s, :].rearrange("p b a t -> p b (a t)"), sij[:, 0:NB, :]).then_inc(topk_ok[l], 1)
                    dve.wait_ge(topk_ok[l], i * 2 + 4)
                    hold()
                    own.clear()

            def routing(l):
                dve.sem_inc(g_mm[l], 2)
                own.clear()
                with dve.Fori(0, blocks_of(l)) as b:
                    svb = sv[:, ds(b), :, :, :].rearrange("p b h s t -> p (b h) s t")
                    sib = si[:, ds(b), :, :, :].rearrange("p b h s t -> p (b h) s t")
                    for a0, na, nb, c0 in RECTS:
                        last = tt(cand[:, :, c0:c0 + na * nb].rearrange("p h (a b) -> p h a b", a=na),
                                  svb[:, :, 0, a0:a0 + na][:, :, :, None].to_broadcast([P, PH, na, nb]),
                                  svb[:, :, 1, 0:nb][:, :, None, :].to_broadcast([P, PH, na, nb]), ALU.add)
                    link(last)
                    for h in range(PH):
                        last = dve.max(cv[:, h, 0:8], cand[:, h, :])
                    link(last)
                    for h in range(PH):
                        dve.max_index(ci[:, h, 0:8], cv[:, h, 0:8], cand[:, h, :])
                    for h in range(PH):
                        last = dve.match_replace(cand2[:, h, :], cv[:, h, 0:8], cand[:, h, :], NEG)
                    link(last)
                    for h in range(PH):
                        last = dve.max(cv[:, h, 8:16], cand2[:, h, :])
                    link(last)
                    for h in range(PH):
                        last = dve.max_index(ci[:, h, 8:16], cv[:, h, 8:16], cand2[:, h, :])
                    gat = route[:, 2, :].rearrange("p (h t) -> p h t", h=PH)
                    link(last)
                    tt(gat, cv, cv[:, :, 0:1].to_broadcast([P, PH, TOPK]), ALU.subtract).then_inc(expo_in[l], 1)
                    cif = ci.rearrange("p h t -> p (h t)")
                    dve.tensor_scalar(shifted[:, 0, :], cif, 3, None, ALU.logical_shift_right)
                    dve.tensor_scalar(shifted[:, 1, :], cif, 2, None, ALU.logical_shift_right)
                    link(dve.tensor_copy(pos[:, 0, :], cif))
                    link(dve.tensor_copy(pos[:, 1:3, :], shifted[:, :, :]))
                    p0, p3, p2 = pos[:, 0, :], pos[:, 1, :], pos[:, 2, :]
                    for r in range(3):
                        dve.tensor_scalar(inrect[:, r, :], p0, float(RECTS[r + 1][3]), None, ALU.is_ge)
                    tt(part[:, 0, :], p2, p3, ALU.subtract)
                    link(tt(part[:, 1, :], p0, p2, ALU.subtract))
                    m1, m2, m3 = inrect[:, 0, :], inrect[:, 1, :], inrect[:, 2, :]
                    stt = dve.scalar_tensor_tensor
                    stt(rank[:, 0, :], p3, -1.0, m1, ALU.add, ALU.mult)
                    stt(part[:, 0, :], part[:, 0, :], -5.0, m2, ALU.add, ALU.mult)
                    stt(part[:, 1, :], part[:, 1, :], -42.0, m3, ALU.add, ALU.mult)
                    stt(part[:, 2, :], p3, 8.0, m1, ALU.mult, ALU.mult)
                    stt(part[:, 3, :], p3, -2.0, p2, ALU.mult, ALU.add)
                    link(stt(part[:, 4, :], p2, -4.0, p0, ALU.mult, ALU.add))
                    tt(rank[:, 0, :], rank[:, 0, :], part[:, 0, :], ALU.add)
                    stt(part[:, 3, :], part[:, 3, :], 4.0, m2, ALU.mult, ALU.mult)
                    tt(part[:, 4, :], part[:, 4, :], m3, ALU.mult)
                    link(tt(rank[:, 1, :], p0, part[:, 2, :], ALU.subtract))
                    tt(rank[:, 0, :], rank[:, 0, :], part[:, 1, :], ALU.add)
                    link(tt(rank[:, 1, :], rank[:, 1, :], part[:, 3, :], ALU.subtract))
                    link(tt(rank[:, 1, :], rank[:, 1, :], part[:, 4, :], ALU.subtract))
                    for s in range(2):
                        link(tt(hot, rank[:, s, :, None].to_broadcast([P, NR, TOPK]), iota[:, None, 0:TOPK].to_broadcast([P, NR, TOPK]), ALU.is_equal))
                        hot4 = hot.rearrange("p (h t) a -> p h t a", h=PH)
                        link(tt(hot4, hot4, sib[:, :, s, :][:, :, None, :].to_broadcast([P, PH, TOPK, TOPK]), ALU.mult))
                        link(dve.reduce_sum(route[:, s, :], hot, axis=AX.X))
                    dve.wait_ge(expo_ok[l], b + 1)
                    link(dve.reduce_sum(gsum, gat, axis=AX.X))
                    link(dve.reciprocal(gsum, gsum))
                    tt(gat, gat, gsum[:, :, None].to_broadcast([P, PH, TOPK]), ALU.mult).then_inc(route_ok[l], 1)
                    dve.wait_ge(routeT_ok[l], b + 1)
                    hold()
                    with dve.Fori(0, P // QT) as i:
                        for h in range(2):
                            n = b * (P // 4) + i * 2
                            dve.wait_ge(g_mm[l], n + (h + 1))
                            for j in range(4):
                                c = i * QT + (4 * h + j)
                                dve.tensor_scalar(oh1[:, 4 * h + j, :], iota[:, :], routeT[:, 0, ds(c)], None, ALU.is_equal)
                                last = dve.tensor_scalar(oh2[:, 4 * h + j, :], iota[:, :], routeT[:, 1, ds(c)], routeT[:, 2, ds(c)], ALU.is_equal, ALU.mult)
                            last.then_inc(hot_ok[l], 1)
                    own.clear()

            def experts(l):
                NB = blocks_of(l)
                T = NB * P
                outs = [(b, half) for b in range(NB) for half in range(2)]
                own.clear()
                link(dve.memset(facc[:, 0:NB, :], 0.0))
                dve.sem_inc(ul_ok[l], 2)
                dve.sem_inc(vl_ok[l], 2)
                dve.sem_inc(wf_ok[l], GRP)
                dve.sem_inc(f_ok[l], 4)
                own.clear()

                def u_split(n, s):
                    dve.wait_ge(uh_ok[l], n + 1)
                    dve.scalar_tensor_tensor(usl[s], uraw[s], S_U, ush[s], ALU.mult, ALU.subtract).then_inc(ul_ok[l], 1)

                def group(g, more):
                    for e in range(GRP):
                        s = e % 2
                        n = g * GRP + e
                        if e < GRP - 1 or more:
                            u_split(n + 1, (e + 1) % 2)
                        dve.wait_ge(vh_ok[l], n + 1)
                        dve.scalar_tensor_tensor(vsl[:, e, :], vraw[s], S_V, vsh[:, e, :], ALU.mult, ALU.subtract).then_inc(vl_ok[l], 1)
                        dve.wait_ge(gelu_ok[l], n + 3)
                        dve.wait_ge(g_in[e][l], g * 16 + 16)
                        a3 = actb[s][:, 0:T].rearrange("p (b c) -> p b c", c=P)
                        w3 = wf[s][:, 0:T].rearrange("p (b c) -> p b c", c=P)
                        tt(w3, a3, graw[:, e, 0:NB, :], ALU.mult).then_inc(wf_ok[l], 1)
                        dve.wait_ge(wh_ok[l], n + 1)
                        dve.scalar_tensor_tensor(wtl[:, e, 0:T], wf[s][:, 0:T], S_W, wth[:, e, 0:T], ALU.mult, ALU.subtract).then_inc(wl_ok[l], 1)
                    for j, (b, half) in enumerate(outs):
                        dve.wait_ge(v_mm[l], g * len(outs) + (j + 2))
                        f = facc[:, b, half * 512:(half + 1) * 512]
                        tt(f, f, ps[4 + j % 4][:, :], ALU.add).then_inc(f_ok[l], 1)
                    dve.wait_ge(f_ok[l], g * len(outs) + (len(outs) + 4))

                u_split(0, 0)
                with dve.Fori(0, NGRP - 1) as g:
                    group(g, True)
                group(NGRP - 1, False)

            def norm2(l):
                NB = blocks_of(l)
                diagonals(l, dia2, 5 * KC, dia2_ok[l], gate2_mm[l])
                dve.wait_ge(rows2_in[l], 32)
                dve.wait_ge(gate2_ok[l], 2 if l == 0 else 1)
                for b in range(NB):
                    link(dve.scalar_tensor_tensor(ftmp, facc[:, b, :], 1.0 / (S_W * S_V), gate[:, b // LAT_B, :], ALU.mult, ALU.mult))
                    link(dve.scalar_tensor_tensor(x[:, b, :], x[:, b, :], ALPHA, ftmp, ALU.mult, ALU.add))
                    norm(l, 1, b)

            for l in range(DEPTH):
                for stage in (modulation, columns, mixer, project, queries, routing, experts, norm2):
                    stage(l)
                    stages.end()
                if l < DEPTH - 1:
                    stages.begin()


def layouts(inputs):
    import numpy as np

    a = {k: np.asarray(v) for k, v in inputs.items()}
    L = DEPTH
    out = {
        "x": np.concatenate([a["x"][0], a["ctx"][0]], 0),
        "c2": np.stack([a["c"][0], a["c_ctx"]], -1).reshape(KC, P, 2).transpose(1, 0, 2),
        "b_mod": a["b_mod"].reshape(L, NMOD, P).transpose(0, 2, 1),
        "w_mod": a["w_mod"].reshape(L, KC, P, NMOD // MODG, MODG, P).transpose(0, 3, 2, 4, 1, 5),
        "w_in": a["w_in"].reshape(L, KC, P, NCOL, P).transpose(0, 3, 2, 1, 4),
        "w_v": a["w_in"][:, :, 5 * CONV:6 * CONV].reshape(L, KC, P, CONV).transpose(0, 2, 1, 3),
        "w_g": a["w_in"][:, :, 6 * CONV:].reshape(L, KC, P, CONV).transpose(0, 2, 1, 3),
        "conv_w": a["conv_w"].reshape(L, CCT, P, 3).transpose(0, 2, 1, 3),
        "w_out": a["w_out"].reshape(L, KC, P, D).transpose(0, 2, 1, 3),
        "ln": np.stack([a["ln1_g"], a["ln1_b"], a["ln2_g"], a["ln2_b"]], 1),
        "w_q": a["peer_wq"].reshape(L, KC, P, 2 * PH, P).transpose(0, 3, 2, 1, 4),
        "keys": a["peer_keys"].transpose(0, 3, 1, 2),
        "peer_u": a["peer_u"].reshape(L, NKEY, P, KC, P).transpose(0, 1, 4, 3, 2),
        "peer_v": a["peer_v"].reshape(L, NKEY, P, D),
        "ident": np.eye(P),
        "iota": np.tile(np.arange(P), (P, 1)),
    }
    nf = P // 4
    d = np.arange(P)
    where = np.arange(SEQ)
    ang = np.where(d[:, None] < P // 2, where // GRID, where % GRID) * 10000.0 ** (-(d[:, None] % nf) / nf)
    out["ropeC"], out["ropeS"] = np.cos(ang), np.sin(ang)
    perm = np.zeros((P, P))
    for i in d:
        if i % (P // 2) < nf:
            perm[i + nf, i] = -1.0
        else:
            perm[i - nf, i] = 1.0
    out["perm"] = perm
    h = np.arange(HEADS)
    lf = np.log1p(-np.exp2(-(5.0 + h)))[:, None, None]
    lb = np.log1p(-np.exp2(-(5.5 + h)))[:, None, None]
    u = (np.arange(STRIP1)[None, :] - 384 - d[:, None])[None]
    out["strip1"] = np.where(u >= 0, np.exp(np.abs(u) * lf), np.exp(np.abs(u) * lb)) * P ** -0.5
    u = (np.arange(STRIP2)[None, :] - P - d[:, None])[None]
    out["strip2"] = (np.exp((u + CTX) * lf) + np.exp((SEQ - u) * lb)) * P ** -0.5
    return {k: np.ascontiguousarray(v, np.float32) for k, v in out.items()}


def kernel(**inputs):
    import concourse.bacc as bacc
    from concourse.bass_utils import run_bass_kernel_spmd

    arrays = layouts(inputs)
    nc = bacc.Bacc("TRN2", target_bir_lowering=False, num_devices=1)
    t = {k: nc.dram_tensor(f"in_{k}", v.shape, F32, kind="ExternalInput").ap() for k, v in arrays.items()}
    t["gates"] = nc.dram_tensor("gates", [NBLK, P, NKEY, P], F32, kind="Internal").ap()
    t["out"] = nc.dram_tensor("out", [SEQ, D], F32, kind="ExternalOutput").ap()
    build(nc, t)
    r = run_bass_kernel_spmd(nc, [{f"in_{k}": v for k, v in arrays.items()}], core_ids=[0])
    return r.results[0]["out"].reshape(1, SEQ, D)
```

```python
from contextlib import ExitStack

import concourse.bass as bass
from concourse import mybir

F32 = mybir.dt.float32
F16 = mybir.dt.float16
U32 = mybir.dt.uint32
ALU = mybir.AluOpType
ACT = mybir.ActivationFunctionType
AX = mybir.AxisListType

P = 128
D = 1024
KC = D // P
SEQ, CTX = 512, 256
LAT_B, CTX_B = SEQ // P, CTX // P
NBLK = LAT_B + CTX_B
TOK = NBLK * P
DEPTH = 2
GRID = 64
CONV = D // 2
CCT = CONV // P
HEADS = 4
NCOL = 7 * CCT
ALPHA = float((2 * DEPTH) ** 0.25)
EPS = 1e-5
NKEY = 128
PH, TOPK = 8, 16
NMOD = 6 * KC
MODW = 512
NMG = NMOD * P // MODW
NEG = -3.0e38
RECTS = [(0, 1, 16, 0), (1, 3, 8, 16), (4, 4, 4, 40), (8, 8, 1, 56)]
NCAND = 64
GRP = 4
NGRP = NKEY // GRP
QT = 8
S_H, S_U, S_W, S_V = 16.0, 1024.0, 256.0, 256.0
STRIP1, STRIP2 = SEQ + 384, SEQ + 128


def blocks_of(layer):
    return NBLK if layer < DEPTH - 1 else LAT_B


def group_runs(layer, end):
    n = NMG // 2 if layer < DEPTH - 1 else 0
    return [(0, n, True)] * (n > 0) + [(n, end, False)]


def nscore(layer):
    return NBLK + (CTX_B if blocks_of(layer) > LAT_B else 0)


def spans_of(layer):
    return [(0, 384), (384, 384)] if layer < DEPTH - 1 else [(0, 512)]


def build(nc, t):
    with ExitStack() as ctx:
        def sb(name, shape, dt=F32):
            return ctx.enter_context(nc.sbuf_tensor(name, shape, dt))

        def sem(name):
            return ctx.enter_context(nc.semaphore(name))

        layer_sems = []

        def persem(name):
            layer_sems.append(sem(name))
            return layer_sems[-1:] * DEPTH

        x = sb("x", [P, NBLK, D])
        ident = sb("ident", [P, P])
        iota = sb("iota", [P, P])
        perm = sb("perm", [P, P])
        cT = sb("cT", [P, KC, 2])
        sT = sb("sT", [P, KC, 2])
        modc = sb("modc", [P, NMOD, 2])
        eps = sb("eps", [P, 1])
        gate = sb("gate", [P, 2, D])
        lng = sb("lng", [P, D])
        lnb = sb("lnb", [P, D])
        st = sb("st", [P, 2, 6])
        mv = sb("mv", [P, NBLK, 2])
        sd = sb("sd", [P, NBLK])
        rs = sb("rs", [P, NBLK])

        ARENA = 42200
        arena = sb("arena", [P, ARENA])
        at = [0]

        def take(*shape, dt=F32, where=None):
            n = 1
            for s in shape:
                n *= s
            words = n if dt != F16 else n // 2
            a = at[0] if where is None else where
            assert a + words <= ARENA, (a, words)
            if where is None:
                at[0] = a + words
            v = arena[:, a:a + words]
            if dt != F32:
                v = v.bitcast(dt)
            if len(shape) == 1:
                return v
            names = "abcd"[:len(shape)]
            return v.rearrange(f"p ({' '.join(names)}) -> p {' '.join(names)}",
                               **{n_: s for n_, s in zip(names, shape)})

        MODAT = 31744
        at[0] = MODAT
        wmod = [take(KC, MODW) for _ in range(2)]
        bmodr = [take(MODW) for _ in range(2)]
        modr = [take(MODW) for _ in range(2)]
        modt = take(2, P, where=0)
        at[0] = 0
        hT = take(KC, TOK)
        catT = take(KC, TOK)
        v_nat = take(NBLK, CONV)
        g_nat = take(NBLK, CONV)
        big = at[0]
        wv = take(KC, CONV)
        wg = take(KC, CONV)
        w_out = take(KC, D, where=big)
        wring = [take(KC, P) for _ in range(3)]
        strip1 = take(STRIP1)
        strip2 = take(STRIP2)
        ropeC = take(SEQ)
        ropeS = take(SEQ)
        convw = take(CCT, 3)
        rest = at[0]
        cg_sb = take(TOK)
        z_sb = take(TOK)
        y_sb = take(TOK)
        at[0] = rest
        q_raw = take(SEQ)
        k_raw = take(SEQ)
        qT = take(TOK)
        kT = take(TOK)
        Psc = take(NBLK, SEQ)
        Pctx = q_raw.rearrange("p (a b) -> p a b", a=CTX_B)
        gst = take(NBLK, 6)
        onrm = Psc.rearrange("p a b -> p (a b)")[:, 0:NBLK * P].rearrange("p (a b) -> p a b", a=NBLK)
        retn = Psc.rearrange("p a b -> p (a b)")[:, NBLK * P:2 * NBLK * P].rearrange("p (a b) -> p a b", a=NBLK)
        tmp = take(D, where=rest)
        h2T = hT
        at[0] = KC * TOK
        hh = take(KC, TOK, dt=F16)
        hl = take(KC, TOK, dt=F16)
        after_h = at[0]
        sv = take(NBLK, PH, 2, TOPK)
        si = take(NBLK, PH, 2, TOPK)
        after_s = at[0]
        wq = [take(KC, P) for _ in range(2)]
        keys = take(2, NKEY)
        qs = [take(TOK) for _ in range(2)]
        svj2 = [take(NBLK, TOPK) for _ in range(2)]
        sij2 = [take(NBLK, TOPK, dt=U32) for _ in range(2)]
        left = take(NBLK, NKEY)
        NR = PH * TOPK
        at[0] = 0
        cand = take(PH, NCAND)
        cand2 = take(PH, NCAND)
        cv = take(PH, TOPK)
        ci = take(PH, TOPK, dt=U32)
        shifted = take(2, NR, dt=U32)
        pos = take(3, NR)
        inrect = take(3, NR)
        part = take(6, NR)
        rank = take(2, NR)
        route = take(3, NR)
        gsum = take(PH)
        assert at[0] <= KC * TOK
        at[0] = after_s
        gbuf = take(NKEY, P)
        routeT = take(3, P)
        oh1 = [take(QT, NKEY) for _ in range(2)]
        oh2 = [take(QT, NKEY) for _ in range(2)]
        hot = [take(NR, TOPK) for _ in range(2)]
        at[0] = 0
        facc = take(NBLK, D)
        at[0] = after_h
        uraw = [take(KC, P) for _ in range(2)]
        vraw = [take(D) for _ in range(2)]
        ush = [take(KC, P, dt=F16) for _ in range(2)]
        usl = [take(KC, P, dt=F16) for _ in range(2)]
        vsh = take(GRP, D, dt=F16)
        vsl = take(GRP, D, dt=F16)
        graw = take(GRP, NBLK, P)
        actb = [take(TOK) for _ in range(2)]
        wf = [take(TOK) for _ in range(2)]
        wth = take(GRP, TOK, dt=F16)
        wtl = take(GRP, TOK, dt=F16)
        assert at[0] <= MODAT
        ftmp = take(D, where=after_h)

        ps = [ctx.enter_context(nc.psum_tensor(f"ps{i}", [P, 512], F32)) for i in range(8)]

        consts_in = sem("consts_in")
        x_in = sem("x_in")
        silu_ok = sem("silu_ok")
        eps_ok = sem("eps_ok")
        stage_done = sem("stage_done")
        out_done = sem("out_done")
        dve_chain = sem("dve_chain")
        dve_held = sem("dve_held")
        pool_held = sem("pool_held")
        wmod_in = [persem(f"wmod_in{s}_") for s in range(2)]
        rows_in = persem("rows_in")
        mod_mm = persem("mod_mm")
        mod_ok = persem("mod_ok")
        modr_out = [persem(f"modr_out{s}_") for s in range(2)]
        modt_in = persem("modt_in")
        modt_mm = persem("modt_mm")
        modc_ok = persem("modc_ok")
        tr_mm = [persem(f"tr_mm{k}_") for k in range(2)]
        tr_dve = [persem(f"tr_dve{k}_") for k in range(2)]
        tr_act = [persem(f"tr_act{k}_") for k in range(2)]
        wv_in = persem("wv_in")
        wg_in = persem("wg_in")
        vg_mm = persem("vg_mm")
        vg_ev = persem("vg_ev")
        wout_in = persem("wout_in")
        cw_in = persem("cw_in")
        wr_in = [persem(f"wr_in{r}_") for r in range(3)]
        conv_mm = persem("conv_mm")
        cg_ev = persem("cg_ev")
        conv_ok = persem("conv_ok")
        strip_in = persem("strip_in")
        qk_mm = persem("qk_mm")
        qk_ev = persem("qk_ev")
        rot_mm = persem("rot_mm")
        rope_ok = persem("rope_ok")
        sc_mm = persem("sc_mm")
        p_ok = persem("p_ok")
        o_mm = persem("o_mm")
        var_ok = persem("var_ok")
        sd_ok = persem("sd_ok")
        ret_ok = persem("ret_ok")
        retT_mm = persem("retT_mm")
        head_ok = persem("head_ok")
        y_mm = persem("y_mm")
        y_used = persem("y_used")
        lnvar_ok = [persem(f"lnvar_ok{k}_") for k in range(2)]
        lnsd_ok = [persem(f"lnsd_ok{k}_") for k in range(2)]
        x_ok = persem("x_ok")
        wq_in = [persem(f"wq_in{s}_") for s in range(2)]
        keys_in = persem("keys_in")
        hh_ok = persem("hh_ok")
        q_mm = persem("q_mm")
        q_ev = persem("q_ev")
        s_mm = persem("s_mm")
        topk_ok = persem("topk_ok")
        expo_in = persem("expo_in")
        expo_ok = persem("expo_ok")
        route_ok = persem("route_ok")
        routeT_mm = persem("routeT_mm")
        routeT_ok = persem("routeT_ok")
        rank_ok = persem("rank_ok")
        rank_idx = persem("rank_idx")
        hot_ok = persem("hot_ok")
        hot2_ok = persem("hot2_ok")
        hotg_ok = persem("hotg_ok")
        g_mm = persem("g_mm")
        g_ev = persem("g_ev")
        g_out = persem("g_out")
        u_in = [persem(f"u_in{s}_") for s in range(2)]
        v_in = [persem(f"v_in{s}_") for s in range(2)]
        g_in = [persem(f"g_in{s}_") for s in range(GRP)]
        uh_ok = persem("uh_ok")
        ul_ok = persem("ul_ok")
        vh_ok = persem("vh_ok")
        vl_ok = persem("vl_ok")
        u_mm = persem("u_mm")
        gelu_ok = persem("gelu_ok")
        wf_ok = persem("wf_ok")
        wh_ok = persem("wh_ok")
        wl_ok = persem("wl_ok")
        v_mm = persem("v_mm")
        f_ok = persem("f_ok")
        rows2_in = persem("rows2_in")
        x2_ok = persem("x2_ok")

        class Own:

            def __init__(self, eng, s):
                self.eng, self.s, self.n = eng, s, 0

            def link(self, ins):
                self.n += 1
                ins.then_inc(self.s, 1)
                self.eng.wait_ge(self.s, self.n)

            def clear(self):
                if self.n:
                    self.eng.sem_clear(self.s)
                    self.n = 0

        class Stages:

            def __init__(self, eng):
                self.eng, self.n = eng, 0

            def end(self):
                self.n += 1
                self.eng.drain().then_inc(stage_done, 1)
                self.eng.wait_ge(stage_done, 5 * self.n)

            def begin(self):
                self.end()
                self.eng.drain()

        def new_layer(sp):
            nums = sorted(s.num for s in layer_sems)
            runs = [i for i in range(len(nums)) if not i or nums[i] != nums[i - 1] + 1] + [len(nums)]
            for a, b in zip(runs, runs[1:]):
                sp.sem_clear(range(nums[a], nums[b - 1] + 1))

        def ds(i, n=1):
            return bass.ds(i, n)

        block = ctx.enter_context(nc.Block())

        @block.sync
        def _(sp):
            stages = Stages(sp)

            def mod_load(run, n, s):
                sp.wait_ge(mod_ok[0], n + (NMG * run + 1))
                sp.dma_start(wmod[s], t["w_mod"][run, ds(n)].rearrange("g p a b -> (g p) a b")).then_inc(wmod_in[s][0], 16)
                sp.dma_start(bmodr[s][0:2, :], t["b_mod"][run, ds(n)].to_broadcast([2, MODW])).then_inc(wmod_in[s][0], 16)

            def mod_stored(run):
                for s in range(2):
                    sp.wait_ge(modr_out[s][0], 16 * (NMG // 2 * (run + 1) + 1))

            def gate_row(l, r, which, s):
                sp.dma_start(gate[:, r, :], t["mod"][l, r:r + 1, which * D:(which + 1) * D].to_broadcast([P, D])).then_inc(s[l], 16)

            def modulation(l):
                if l == 0:
                    for dst, src in ((ident, "ident"), (iota, "iota"), (perm, "perm")):
                        sp.dma_start(dst[:, :], t[src]).then_inc(consts_in, 16)
                    sp.dma_start(cT[:, :, :], t["c2"]).then_inc(consts_in, 16)
                    with sp.Fori(0, NMG // 2) as i:
                        for s in range(2):
                            mod_load(0, i * 2 + s, s)
                    sp.dma_start(x[:, :, :], t["x"].rearrange("(b p) d -> p b d", p=P)).then_inc(x_in, 16)
                    mod_stored(0)
                for r in range(2):
                    sp.dma_start(modt[0:NMOD, r, :], t["mod"][l, r].rearrange("(a b) -> a b", b=P)).then_inc(modt_in[l], 16)
                for r in range(2 if l == 0 else 1):
                    gate_row(l, r, 2, rows_in)
                sp.dma_start(lng[:, :], t["ln"][l, 0:1, :].to_broadcast([P, D])).then_inc(rows_in[l], 16)
                sp.dma_start(lnb[:, :], t["ln"][l, 1:2, :].to_broadcast([P, D])).then_inc(rows_in[l], 16)

            def w_tile(dst, l, tile, s):
                sp.dma_start(dst, t["w_in"][l, ds(tile)].rearrange("g p a b -> (g p) a b")).then_inc(s, 16)

            def mixer(l):
                sp.dma_start(wv, t["w_v"][l]).then_inc(wv_in[l], 16)
                sp.dma_start(wg, t["w_g"][l]).then_inc(wg_in[l], 16)
                sp.dma_start(convw, t["conv_w"][l]).then_inc(cw_in[l], 16)
                sp.dma_start(ropeC, t["ropeC"]).then_inc(cw_in[l], 16)
                sp.dma_start(ropeS, t["ropeS"]).then_inc(cw_in[l], 16)
                first = (CCT, 2 * CCT, 0)
                for r in range(3):
                    w_tile(wring[r], l, first[r], wr_in[r][l])
                sp.dma_start(strip1, t["strip1"][0]).then_inc(strip_in[l], 16)
                sp.dma_start(strip2, t["strip2"][0]).then_inc(strip_in[l], 16)
                sp.wait_ge(vg_mm[l], NBLK + blocks_of(l))
                sp.dma_start(w_out, t["w_out"][l]).then_inc(wout_in[l], 16)
                with sp.Fori(1, CCT) as i:
                    for r in range(3):
                        sp.wait_ge(conv_mm[l], i * 3 + (r - 2))
                        w_tile(wring[r], l, i + first[r], wr_in[r][l])
                for r in range(2):
                    sp.wait_ge(conv_mm[l], 3 * CCT + r - 2)
                    w_tile(wring[r], l, (3 + r) * CCT, wr_in[r][l])
                with sp.Fori(1, HEADS) as i:
                    for r in range(2):
                        sp.wait_ge(qk_mm[l], i * 2 + (r - 1))
                        w_tile(wring[r], l, i + (3 + r) * CCT, wr_in[r][l])
                    sp.wait_ge(p_ok[l], i * nscore(l))
                    sp.dma_start(strip1, t["strip1"][ds(i)].rearrange("g p a -> (g p) a")).then_inc(strip_in[l], 16)
                    sp.dma_start(strip2, t["strip2"][ds(i)].rearrange("g p a -> (g p) a")).then_inc(strip_in[l], 16)

            def queries(l):
                sp.dma_start(keys, t["keys"][l]).then_inc(keys_in[l], 16)
                for s in range(2):
                    sp.dma_start(wq[s], t["w_q"][l, s]).then_inc(wq_in[s][l], 16)
                with sp.Fori(1, PH) as i:
                    for s in range(2):
                        sp.wait_ge(q_mm[l], i * 2 + (s - 1))
                        sp.dma_start(wq[s], t["w_q"][l, ds(i * 2 + s)].rearrange("g p a b -> (g p) a b")).then_inc(wq_in[s][l], 16)

            def routing(l):
                sp.sem_inc(g_out[l], 16)
                with sp.Fori(0, blocks_of(l)) as b:
                    sp.wait_ge(g_ev[l], b * (P // QT) + (P // QT + 2))
                    sp.dma_start(t["gates"][ds(b)].rearrange("b p i t -> (b p) i t"), gbuf).then_inc(g_out[l], 16)
                sp.wait_ge(g_out[l], 16 * (blocks_of(l) + 1))

            def experts(l):
                NB = blocks_of(l)
                def group(g, mod):
                    for e in range(GRP):
                        s = e % 2
                        n = g * GRP + e
                        sp.wait_ge(ul_ok[l], n + 1)
                        sp.dma_start(uraw[s], t["peer_u"][l, ds(n)].rearrange("g p a b -> (g p) a b")).then_inc(u_in[s][l], 16)
                        if mod and e < 2:
                            mod_load(l + 1, g * 2 + e, e)
                        sp.wait_ge(wf_ok[l], n + 1)
                        sp.dma_start(graw[:, e, 0:NB, :],
                                     t["gates"][0:NB, :, ds(n), :].rearrange("b p i t -> p (b i) t")).then_inc(g_in[e][l], 16)
                        sp.wait_ge(vl_ok[l], n + 1)
                        sp.dma_start(vraw[s], t["peer_v"][l, ds(n)].rearrange("g p a -> (g p) a")).then_inc(v_in[s][l], 16)

                for lo, hi, mod in group_runs(l, NGRP):
                    with sp.Fori(lo, hi) as g:
                        group(g, mod)
                if l < DEPTH - 1:
                    mod_stored(l + 1)
                for r in range(NB // LAT_B + (1 if NB > LAT_B else 0)):
                    gate_row(l, r, 5, rows2_in)
                sp.dma_start(lng[:, :], t["ln"][l, 2:3, :].to_broadcast([P, D])).then_inc(rows2_in[l], 16)
                sp.dma_start(lnb[:, :], t["ln"][l, 3:4, :].to_broadcast([P, D])).then_inc(rows2_in[l], 16)

            def norm2(l):
                if l == DEPTH - 1:
                    for b in range(LAT_B):
                        sp.wait_ge(x2_ok[l], b + 1)
                        sp.dma_start(t["out"][b * P:(b + 1) * P, :], x[:, b, :]).then_inc(out_done, 16)
                    sp.wait_ge(out_done, 16 * LAT_B)

            def nothing(l):
                pass

            for l in range(DEPTH):
                for stage in (modulation, nothing, mixer, nothing, queries, routing, experts, norm2):
                    stage(l)
                    stages.end()
                if l < DEPTH - 1:
                    new_layer(sp)
                    stages.begin()

        @block.tensor
        def _(pe):
            stages = Stages(pe)

            def mm(out, lhsT, rhs, start, stop):
                return pe.matmul(out, lhsT, rhs, start=start, stop=stop)

            def mod_rows(run, n, s):
                pe.wait_ge(wmod_in[s][0], n * 16 + (32 - 16 * s + 16 * NMG * run))
                for k in range(KC):
                    last = mm(ps[4 + s][0:2, :], sT[:, k, :], wmod[s][:, k, :], k == 0, k == KC - 1)
                last.then_inc(mod_mm[0], 1)

            def modulation(l):
                if l == 0:
                    pe.wait_ge(consts_in, 64)
                    pe.wait_ge(silu_ok, 1)
                    with pe.Fori(0, NMG // 2) as i:
                        for s in range(2):
                            pe.wait_ge(mod_ok[0], i * 2 + (s + 1))
                            mod_rows(0, i * 2 + s, s)
                pe.wait_ge(modt_in[l], 32)
                for r in range(2):
                    last = pe.transpose(ps[0][:, r * NMOD:(r + 1) * NMOD], modt[0:NMOD, r, :], ident[0:NMOD, 0:NMOD])
                last.then_inc(modt_mm[l], 1)

            def to_columns(l, k, b):
                for half in range(2):
                    n = 2 * b + half
                    if n >= 4:
                        pe.wait_ge((tr_act if n % 2 else tr_dve)[k][l], (n - 4) // 2 + 1)
                    for j in range(4):
                        c = half * 4 + j
                        last = pe.transpose(ps[4 + n % 4][:, j * P:(j + 1) * P], x[:, b, c * P:(c + 1) * P], ident[:, :])
                    last.then_inc(tr_mm[k][l], 1)

            def columns(l):
                if l == 0:
                    pe.wait_ge(x_in, 16)
                for b in range(NBLK):
                    to_columns(l, 0, b)

            def mixer(l):
                NB = blocks_of(l)
                TC = [(0, SEQ), (SEQ, CTX)]
                n = 0
                for b in range(NBLK):
                    for w, s, on_ in ((wv, wv_in, True), (wg, wg_in, b < NB)):
                        if not on_:
                            continue
                        if b == 0:
                            pe.wait_ge(s[l], 16)
                        if n >= 2:
                            pe.wait_ge(vg_ev[l], n - 1)
                        for k in range(KC):
                            last = mm(ps[6 + n % 2][:, :], hT[:, k, b * P:(b + 1) * P], w[:, k, :], k == 0, k == KC - 1)
                        last.then_inc(vg_mm[l], 1)
                        n += 1
                with pe.Fori(0, CCT) as i:
                    pe.wait_ge(conv_ok[l], i + 1)
                    for r in range(3):
                        pe.wait_ge(wr_in[r][l], i * 16 + 16)
                        for z, (c0, w) in enumerate(TC[:1 if NB == LAT_B else 2]):
                            for k in range(KC):
                                last = mm(ps[2 * r + z][:, 0:w], wring[r][:, k, :], hT[:, k, c0:c0 + w], k == 0, k == KC - 1)
                        last.then_inc(conv_mm[l], 1)
                pe.wait_ge(conv_ok[l], CCT + 1)
                with pe.Fori(0, HEADS) as i:
                    pe.wait_ge(head_ok[l], i + 1)
                    for r in range(2):
                        pe.wait_ge(wr_in[r][l], i * 16 + 16 * (CCT + 1))
                        for z, (c0, w) in enumerate(TC):
                            if z and r == 0 and NB == LAT_B:
                                continue
                            for k in range(KC):
                                last = mm(ps[2 * r + z][:, 0:w], wring[r][:, k, :], hT[:, k, c0:c0 + w], k == 0, k == KC - 1)
                        last.then_inc(qk_mm[l], 1)
                    for r, raw in enumerate((q_raw, k_raw)):
                        pe.wait_ge(qk_ev[l], i * 2 + (r + 1))
                        mm(ps[4 + r][:, :], perm[:, :], raw, True, True).then_inc(rot_mm[l], 1)
                    pe.wait_ge(rope_ok[l], i * 2 + 2)
                    NS = nscore(l)
                    for n in range(NS):
                        if n >= 2:
                            pe.wait_ge(p_ok[l], i * NS + (n - 1))
                        if n < NBLK:
                            mm(ps[6 + n % 2][:, :], kT[:, n * P:(n + 1) * P], qT[:, 0:SEQ], True, True).then_inc(sc_mm[l], 1)
                        else:
                            s = n - NBLK + LAT_B
                            mm(ps[6 + n % 2][:, 0:CTX], kT[:, s * P:(s + 1) * P], qT[:, SEQ:TOK], True, True).then_inc(sc_mm[l], 1)
                    pe.wait_ge(p_ok[l], i * NS + NS)
                    for b in range(LAT_B):
                        for s in range(NBLK):
                            last = mm(ps[4][:, b * P:(b + 1) * P], Psc[:, s, b * P:(b + 1) * P], v_nat[:, s, ds(i * P, P)], s == 0, s == NBLK - 1)
                    if NB > LAT_B:
                        for b in range(CTX_B):
                            for s in range(CTX_B):
                                last = mm(ps[5][:, b * P:(b + 1) * P], Pctx[:, s, b * P:(b + 1) * P], v_nat[:, LAT_B + s, ds(i * P, P)], s == 0, s == CTX_B - 1)
                    last.then_inc(o_mm[l], 1)
                    pe.wait_ge(ret_ok[l], i + 1)
                    for b in range(NB):
                        last = pe.transpose(ps[b // 4][:, (b % 4) * P:(b % 4 + 1) * P], retn[:, b, :], ident[:, :])
                    last.then_inc(retT_mm[l], 1)

            def project(l):
                NB = blocks_of(l)
                pe.wait_ge(wout_in[l], 16)
                for b in range(NB + 1):
                    if b < NB:
                        if b >= 2:
                            pe.wait_ge(y_used[l], b - 1)
                        for half in range(2):
                            for k in range(KC):
                                last = mm(ps[b % 2 * 2 + half][:, :], catT[:, k, b * P:(b + 1) * P],
                                          w_out[:, k, half * 512:(half + 1) * 512], k == 0, k == KC - 1)
                        last.then_inc(y_mm[l], 1)
                    if b:
                        pe.wait_ge(x_ok[l], b)
                        to_columns(l, 1, b - 1)

            def queries(l):
                NB = blocks_of(l)
                pe.wait_ge(keys_in[l], 16)
                with pe.Fori(0, PH) as i:
                    for s in range(2):
                        pe.wait_ge(wq_in[s][l], i * 16 + 16)
                        pe.wait_ge(q_ev[l], i * 2 + (s + 1))
                        for z, (c0, w) in enumerate(spans_of(l)):
                            for k in range(KC):
                                last = mm(ps[2 * s + z][:, 0:w], wq[s][:, k, :], h2T[:, k, c0:c0 + w], k == 0, k == KC - 1)
                        last.then_inc(q_mm[l], 1)
                    for s in range(2):
                        pe.wait_ge(q_ev[l], i * 2 + (s + 3))
                        pe.wait_ge(topk_ok[l], i * 2 + (s + 1))
                        for b in range(NB):
                            last = mm(ps[4 + 2 * s + b // 4][:, (b % 4) * P:(b % 4 + 1) * P], qs[s][:, b * P:(b + 1) * P], keys[:, s, :], True, True)
                        last.then_inc(s_mm[l], 1)

            def routing(l):
                with pe.Fori(0, blocks_of(l)) as b:
                    pe.wait_ge(route_ok[l], b + 1)
                    for j in range(3):
                        last = pe.transpose(ps[0][:, j * P:(j + 1) * P], route[:, j, :], ident[:, :])
                    last.then_inc(routeT_mm[l], 1)
                    with pe.Fori(0, P // (2 * QT)) as i:
                        for h in range(2):
                            n = b * (P // QT) + i * 2
                            pe.wait_ge(hot2_ok[l], n + (h + 1))
                            pe.wait_ge(hotg_ok[l], n + (h + 1))
                            pe.wait_ge(g_ev[l], n + (h + 1))
                            for j in range(QT):
                                last = mm(ps[1 + 2 * h + j // 4][:, (j % 4) * P:(j % 4 + 1) * P], oh2[h][:, j, :], oh1[h][:, j, :], True, True)
                            last.then_inc(g_mm[l], 1)

            def experts(l):
                NB = blocks_of(l)
                outs = [(b, half) for b in range(NB) for half in range(2)]

                def group(g, mod):
                    if mod:
                        for s in range(2):
                            pe.wait_ge(f_ok[l], g * len(outs) + (s + 1))
                            mod_rows(l + 1, g * 2 + s, s)
                    for e in range(GRP):
                        n = g * GRP + e
                        s = e % 2
                        pe.wait_ge(uh_ok[l], n + 1)
                        pe.wait_ge(ul_ok[l], n + 3)
                        pe.wait_ge(gelu_ok[l], n + 1)
                        for z, (c0, w) in enumerate(spans_of(l)):
                            out = ps[2 * s + z][:, 0:w]
                            for k in range(KC):
                                mm(out, ush[s][:, k, :], hh[:, k, c0:c0 + w], k == 0, False)
                                mm(out, ush[s][:, k, :], hl[:, k, c0:c0 + w], False, False)
                                last = mm(out, usl[s][:, k, :], hh[:, k, c0:c0 + w], False, k == KC - 1)
                        last.then_inc(u_mm[l], 1)
                    for r in range(0, len(outs), 4):
                        for es in (range(GRP - 1), (GRP - 1,)):
                            for j in range(4):
                                b, half = outs[r + j]
                                if r == 0 and j == 0:
                                    m = g * GRP + es[-1]
                                    pe.wait_ge(wh_ok[l], m + 1)
                                    pe.wait_ge(wl_ok[l], m + 1)
                                    pe.wait_ge(vh_ok[l], m + 1)
                                    pe.wait_ge(vl_ok[l], m + 3)
                                if mod and r == 0 and j == 0 and es != (GRP - 1,):
                                    pe.wait_ge(mod_ok[0], g * 2 + (2 + NMG * (l + 1) + 2))
                                if es != (GRP - 1,):
                                    pe.wait_ge(f_ok[l], g * len(outs) + (r + j + 1))
                                for e in es:
                                    wh, wl = wth[:, e, b * P:(b + 1) * P], wtl[:, e, b * P:(b + 1) * P]
                                    vh, vl = (v[:, e, half * 512:(half + 1) * 512] for v in (vsh, vsl))
                                    mm(ps[4 + j][:, :], wh, vh, e == 0, False)
                                    mm(ps[4 + j][:, :], wh, vl, False, False)
                                    last = mm(ps[4 + j][:, :], wl, vh, False, e == GRP - 1)
                                if es == (GRP - 1,):
                                    last.then_inc(v_mm[l], 1)

                for lo, hi, mod in group_runs(l, NGRP):
                    with pe.Fori(lo, hi) as g:
                        group(g, mod)

            def norm2(l):
                pass

            for l in range(DEPTH):
                for stage in (modulation, columns, mixer, project, queries, routing, experts, norm2):
                    stage(l)
                    stages.end()
                if l < DEPTH - 1:
                    stages.begin()

        @block.scalar
        def _(act):
            stages = Stages(act)

            def copy(out, in_, scale=1.0):
                return act.activation(out, in_, ACT.Copy, scale=scale)

            def mod_store(run, n, s):
                act.wait_ge(mod_ok[0], n + (NMG * run + 3))
                act.dma_start(t["mod"][run, :, ds(n * MODW, MODW)], modr[s][0:2, :]).then_inc(modr_out[s][0], 16)

            def modulation(l):
                if l == 0:
                    act.sem_inc(modr_out[0][0], 16)
                    act.sem_inc(modr_out[1][0], 16)
                    act.wait_ge(consts_in, 64)
                    act.activation(sT[:, :, :], cT[:, :, :], ACT.Silu).then_inc(silu_ok, 1)
                    act.wait_ge(eps_ok, 1)
                    with act.Fori(0, NMG // 2) as i:
                        for s in range(2):
                            mod_store(0, i * 2 + s, s)

            def to_columns(l, k, b):
                r = b // LAT_B
                n = 2 * b + 1
                act.wait_ge(tr_mm[k][l], n + 1)
                for j in range(4):
                    c = 4 + j
                    last = act.activation(hT[:, c, b * P:(b + 1) * P], ps[4 + n % 4][:, j * P:(j + 1) * P], ACT.Identity,
                                          bias=modc[:, 3 * k * KC + c, r:r + 1], scale=modc[:, (3 * k + 1) * KC + c, r:r + 1])
                last.then_inc(tr_act[k][l], 1)

            def columns(l):
                act.wait_ge(modc_ok[l], 1)
                for b in range(NBLK):
                    to_columns(l, 0, b)

            def mixer(l):
                NB = blocks_of(l)
                act.sem_inc(head_ok[l], 1)
                n = 0
                for b in range(NBLK):
                    act.wait_ge(vg_mm[l], n + 1)
                    copy(v_nat[:, b, :], ps[6 + n % 2][:, :]).then_inc(vg_ev[l], 1)
                    n += 1
                    if b < NB:
                        act.wait_ge(vg_mm[l], n + 1)
                        act.activation(g_nat[:, b, :], ps[6 + n % 2][:, :], ACT.Silu).then_inc(vg_ev[l], 1)
                        n += 1
                with act.Fori(0, CCT) as i:
                    act.wait_ge(conv_mm[l], i * 3 + 1)
                    act.wait_ge(conv_ok[l], i + 1)
                    last = copy(cg_sb[:, 0:SEQ], ps[0][:, :])
                    if NB > LAT_B:
                        last = copy(cg_sb[:, SEQ:TOK], ps[1][:, 0:CTX])
                    last.then_inc(cg_ev[l], 1)
                act.wait_ge(conv_ok[l], CCT + 1)
                with act.Fori(0, HEADS) as i:
                    for r, (raw, dst) in enumerate(((q_raw, qT), (k_raw, kT))):
                        act.wait_ge(qk_mm[l], i * 2 + (r + 1))
                        last = copy(raw, ps[2 * r][:, :])
                        if r or NB > LAT_B:
                            last = copy(dst[:, SEQ:TOK], ps[2 * r + 1][:, 0:CTX])
                        last.then_inc(qk_ev[l], 1)
                    act.wait_ge(var_ok[l], i + 1)
                    act.activation(sd[:, 0:NB], mv[:, 0:NB, 1], ACT.Sqrt, bias=eps[:, :]).then_inc(sd_ok[l], 1)
                    act.wait_ge(retT_mm[l], i + 1)
                    last = copy(catT[:, ds(i + CCT), 0:SEQ].rearrange("p a b -> p (a b)"), ps[0][:, :])
                    if NB > LAT_B:
                        last = copy(catT[:, ds(i + CCT), SEQ:TOK].rearrange("p a b -> p (a b)"), ps[1][:, 0:CTX])
                    last.then_inc(head_ok[l], 1)

            def deviation(l, k, b):
                act.wait_ge(lnvar_ok[k][l], b + 1)
                act.activation(sd[:, b:b + 1], mv[:, b, 1:2], ACT.Sqrt, bias=eps[:, :]).then_inc(lnsd_ok[k][l], 1)

            def project(l):
                NB = blocks_of(l)
                for b in range(NB + 1):
                    if b < NB:
                        deviation(l, 0, b)
                    if b:
                        to_columns(l, 1, b - 1)

            def queries(l):
                T = blocks_of(l) * P
                act.sem_inc(q_ev[l], 2)
                for k in range(KC):
                    copy(hh[:, k, 0:T], h2T[:, k, 0:T], S_H).then_inc(hh_ok[l], 1)
                with act.Fori(0, PH) as i:
                    for s in range(2):
                        act.wait_ge(q_mm[l], i * 2 + (s + 1))
                        for z, (c0, w) in enumerate(spans_of(l)):
                            last = copy(qs[s][:, c0:c0 + w], ps[2 * s + z][:, 0:w])
                        last.then_inc(q_ev[l], 1)

            def routing(l):
                act.sem_inc(g_ev[l], 2)
                with act.Fori(0, blocks_of(l)) as b:
                    act.wait_ge(expo_in[l], b + 1)
                    act.activation(route[:, 2, :], route[:, 2, :], ACT.Exp).then_inc(expo_ok[l], 1)
                    act.wait_ge(routeT_mm[l], b + 1)
                    copy(routeT.rearrange("p a b -> p (a b)"), ps[0][:, 0:3 * P]).then_inc(routeT_ok[l], 1)
                    act.wait_ge(g_out[l], b * 16 + 16)
                    with act.Fori(0, P // (2 * QT)) as i:
                        for h in range(2):
                            act.wait_ge(g_mm[l], b * (P // QT) + i * 2 + (h + 3))
                            for j in range(QT // 4):
                                last = copy(gbuf[:, :, ds(i * (2 * QT) + (h * QT + 4 * j), 4)],
                                            ps[1 + 2 * h + j][:, :].rearrange("p (j i) -> p i j", j=4))
                            last.then_inc(g_ev[l], 1)

            def experts(l):
                T = blocks_of(l) * P
                act.sem_inc(gelu_ok[l], 2)
                act.sem_inc(u_mm[l], 1)
                act.sem_inc(v_mm[l], 1)

                def group(g, more, mod):
                    for e in range(GRP):
                        s = e % 2
                        n = g * GRP + e
                        if e < GRP - 1 or more:
                            u_split(n + 1, (e + 1) % 2, g * (8 * GRP) + 16 * ((e + 1) // 2 + 1))
                        if e == 0:
                            act.wait_ge(v_mm[l], g * (2 * blocks_of(l)) + 1)
                        act.wait_ge(v_in[s][l], g * (8 * GRP) + 16 * (e // 2 + 1))
                        copy(vsh[:, e, :], vraw[s], S_V).then_inc(vh_ok[l], 1)
                        if mod and e == 0:
                            for k in range(2):
                                mod_store(l + 1, g * 2 + k, k)
                        act.wait_ge(u_mm[l], n + 2)
                        for z, (c0, w) in enumerate(spans_of(l)):
                            last = act.activation(actb[s][:, c0:c0 + w], ps[2 * s + z][:, 0:w], ACT.Gelu, scale=1.0 / (S_H * S_U))
                        last.then_inc(gelu_ok[l], 1)
                        act.wait_ge(wf_ok[l], n + (GRP + 1))
                        copy(wth[:, e, 0:T], wf[s][:, 0:T], S_W).then_inc(wh_ok[l], 1)

                def u_split(n, s, landed):
                    act.wait_ge(u_in[s][l], landed)
                    act.wait_ge(u_mm[l], n)
                    copy(ush[s], uraw[s], S_U).then_inc(uh_ok[l], 1)

                act.wait_ge(u_in[0][l], 16)
                copy(ush[0], uraw[0], S_U).then_inc(uh_ok[l], 1)
                for lo, hi, mod in group_runs(l, NGRP - 1):
                    with act.Fori(lo, hi) as g:
                        group(g, True, mod)
                group(NGRP - 1, False, False)

            def norm2(l):
                for b in range(blocks_of(l)):
                    deviation(l, 1, b)

            for l in range(DEPTH):
                for stage in (modulation, columns, mixer, project, queries, routing, experts, norm2):
                    stage(l)
                    stages.end()
                if l < DEPTH - 1:
                    stages.begin()


        @block.gpsimd
        def _(pool):
            stages = Stages(pool)

            def nothing(l):
                pass

            def routing(l):
                with pool.Fori(0, blocks_of(l)) as b:
                    sib = si[:, ds(b), :, :, :].rearrange("p b h s t -> p (b h) s t")
                    for s in range(2):
                        hot4 = hot[s].rearrange("p (h t) a -> p h t a", h=PH)
                        pool.wait_ge(rank_ok[l], b * 2 + (s + 1))
                        pool.tensor_tensor(hot4, hot4, sib[:, :, s, :][:, :, None, :].to_broadcast([P, PH, TOPK, TOPK]), ALU.mult).then_inc(rank_idx[l], 1)
                    pool.wait_ge(routeT_ok[l], b + 1)
                    pool.sem_inc(pool_held, 1)
                    with pool.Fori(0, P // (2 * QT)) as i:
                        for h in range(2):
                            pool.wait_ge(hot_ok[l], b * (P // QT) + i * 2 + (h + 1))
                            pool.tensor_tensor(oh1[h], oh1[h], routeT[:, 2, ds(i * (2 * QT) + h * QT, QT)][:, :, None].to_broadcast([P, QT, NKEY]), ALU.mult).then_inc(hotg_ok[l], 1)

            for l in range(DEPTH):
                for stage in (nothing, nothing, nothing, nothing, nothing, routing, nothing, nothing):
                    stage(l)
                    stages.end()
                if l < DEPTH - 1:
                    stages.begin()

        @block.vector
        def _(dve):
            stages = Stages(dve)
            own = Own(dve, dve_chain)
            link = own.link

            def hold():
                dve.sem_inc(dve_held, 1)

            def tt(out, a, b, op):
                return dve.tensor_tensor(out, a, b, op)

            def mod_rows(run, n, s):
                dve.wait_ge(mod_mm[0], n + (NMG * run + 1))
                dve.wait_ge(modr_out[s][0], n * 8 + (16 - 8 * s + 8 * NMG * run))
                tt(modr[s][0:2, :], ps[4 + s][0:2, :], bmodr[s][0:2, :], ALU.add).then_inc(mod_ok[0], 1)

            def modulation(l):
                if l == 0:
                    dve.memset(eps[:, :], EPS).then_inc(eps_ok, 1)
                    dve.sem_inc(mod_ok[0], 2)
                    dve.wait_ge(consts_in, 64)
                    with dve.Fori(0, NMG // 2) as i:
                        for s in range(2):
                            mod_rows(0, i * 2 + s, s)
                dve.wait_ge(modt_mm[l], 1)
                for r in range(2):
                    last = dve.tensor_copy(modc[:, :, r], ps[0][:, r * NMOD:(r + 1) * NMOD])
                link(last)
                dve.tensor_scalar(modc[:, KC:2 * KC, :], modc[:, KC:2 * KC, :], 1.0, None, ALU.add)
                dve.tensor_scalar(modc[:, 4 * KC:5 * KC, :], modc[:, 4 * KC:5 * KC, :], 1.0, None, ALU.add).then_inc(modc_ok[l], 1)
                dve.wait_ge(modc_ok[l], 1)

            def to_columns(l, k, b):
                r = b // LAT_B
                n = 2 * b
                dve.wait_ge(tr_mm[k][l], n + 1)
                for c in range(4):
                    last = dve.tensor_scalar(hT[:, c, b * P:(b + 1) * P], ps[4 + n % 4][:, c * P:(c + 1) * P],
                                             modc[:, (3 * k + 1) * KC + c, r:r + 1], modc[:, 3 * k * KC + c, r:r + 1], ALU.mult, ALU.add)
                last.then_inc(tr_dve[k][l], 1)

            def columns(l):
                for b in range(NBLK):
                    to_columns(l, 0, b)

            def taps(z, y, w0, w2):
                n = z.shape[-1]
                if len(z.shape) == 3:
                    link(dve.scalar_tensor_tensor(y[:, :, 1:n], z[:, :, 0:n - 1], w0, y[:, :, 1:n], ALU.mult, ALU.add))
                    link(dve.scalar_tensor_tensor(y[:, :, 0:n - 1], z[:, :, 1:n], w2, y[:, :, 0:n - 1], ALU.mult, ALU.add))
                else:
                    link(dve.scalar_tensor_tensor(y[:, 1:n], z[:, 0:n - 1], w0, y[:, 1:n], ALU.mult, ALU.add))
                    link(dve.scalar_tensor_tensor(y[:, 0:n - 1], z[:, 1:n], w2, y[:, 0:n - 1], ALU.mult, ALU.add))

            def mixer(l):
                NB = blocks_of(l)
                both = NB > LAT_B
                T = NB * P
                own.clear()
                dve.sem_inc(conv_ok[l], 1)
                dve.wait_ge(cw_in[l], 48)
                with dve.Fori(0, CCT) as i:
                    dve.wait_ge(cg_ev[l], i + 1)
                    dve.wait_ge(conv_mm[l], i * 3 + 2)
                    last = tt(z_sb[:, 0:SEQ], cg_sb[:, 0:SEQ], ps[2][:, :], ALU.mult)
                    if both:
                        last = tt(z_sb[:, SEQ:TOK], cg_sb[:, SEQ:TOK], ps[3][:, 0:CTX], ALU.mult)
                    link(last)
                    w = [convw[:, ds(i), j:j + 1].rearrange("p a b -> p (a b)") for j in range(3)]
                    link(dve.tensor_scalar(y_sb[:, 0:T], z_sb[:, 0:T], w[1], None, ALU.mult))
                    taps(z_sb[:, 0:SEQ].rearrange("p (r c) -> p r c", c=GRID), y_sb[:, 0:SEQ].rearrange("p (r c) -> p r c", c=GRID), w[0], w[2])
                    if both:
                        taps(z_sb[:, SEQ:TOK], y_sb[:, SEQ:TOK], w[0], w[2])
                    dve.wait_ge(conv_mm[l], i * 3 + 3)
                    last = tt(catT[:, ds(i), 0:SEQ].rearrange("p a b -> p (a b)"), y_sb[:, 0:SEQ], ps[4][:, :], ALU.mult)
                    if both:
                        last = tt(catT[:, ds(i), SEQ:TOK].rearrange("p a b -> p (a b)"), y_sb[:, SEQ:TOK], ps[5][:, 0:CTX], ALU.mult)
                    last.then_inc(conv_ok[l], 1)
                    own.clear()
                NS = nscore(l)
                with dve.Fori(0, HEADS) as i:
                    for r, (raw, dst) in enumerate(((q_raw, qT), (k_raw, kT))):
                        dve.wait_ge(rot_mm[l], i * 2 + (r + 1))
                        link(tt(dst[:, 0:SEQ], raw, ropeC, ALU.mult))
                        link(tt(raw, ps[4 + r][:, :], ropeS, ALU.mult))
                        tt(dst[:, 0:SEQ], dst[:, 0:SEQ], raw, ALU.add).then_inc(rope_ok[l], 1)
                    dve.wait_ge(rope_ok[l], i * 2 + 2)
                    dve.wait_ge(strip_in[l], i * 32 + 32)
                    for n in range(NS):
                        dve.wait_ge(sc_mm[l], i * NS + (n + 1))
                        if n < LAT_B:
                            a = 384 - P * n
                            tt(Psc[:, n, :], ps[6 + n % 2][:, :], strip1[:, a:a + SEQ], ALU.mult).then_inc(p_ok[l], 1)
                        elif n < NBLK:
                            a = P - P * (n - LAT_B)
                            tt(Psc[:, n, :], ps[6 + n % 2][:, :], strip2[:, a:a + SEQ], ALU.mult).then_inc(p_ok[l], 1)
                        else:
                            a = 384 - P * (n - NBLK)
                            tt(Pctx[:, n - NBLK, :], ps[6 + n % 2][:, 0:CTX], strip1[:, a:a + CTX], ALU.mult).then_inc(p_ok[l], 1)
                    dve.wait_ge(o_mm[l], i + 1)
                    for b in range(NB):
                        last = dve.bn_stats(gst[:, b, :], ps[4 + b // 4][:, (b % 4) * P:(b % 4 + 1) * P])
                    link(last)
                    for b in range(NB):
                        last = dve.bn_aggr(mv[:, b, :], gst[:, b, :])
                    last.then_inc(var_ok[l], 1)
                    dve.wait_ge(sd_ok[l], i + 1)
                    link(dve.reciprocal(rs[:, 0:NB], sd[:, 0:NB]))
                    for b in range(NB):
                        last = dve.tensor_scalar(onrm[:, b, :], ps[4 + b // 4][:, (b % 4) * P:(b % 4 + 1) * P], mv[:, b, 0:1], rs[:, b:b + 1], ALU.subtract, ALU.mult)
                    link(last)
                    tt(retn[:, 0:NB, :], onrm[:, 0:NB, :], g_nat[:, 0:NB, ds(i * P, P)], ALU.mult).then_inc(ret_ok[l], 1)
                    own.clear()

            def norm(l, k, b):
                xb = x[:, b, :]
                dve.bn_stats(st[:, 0, :], x[:, b, 0:512])
                link(dve.bn_stats(st[:, 1, :], x[:, b, 512:D]))
                dve.bn_aggr(mv[:, b, :], st[:, :, :]).then_inc(lnvar_ok[k][l], 1)
                dve.wait_ge(lnsd_ok[k][l], b + 1)
                link(dve.reciprocal(rs[:, b:b + 1], sd[:, b:b + 1]))
                link(dve.tensor_scalar(xb, xb, mv[:, b, 0:1], rs[:, b:b + 1], ALU.subtract, ALU.mult))
                link(tt(xb, xb, lng[:, :], ALU.mult))
                tt(xb, xb, lnb[:, :], ALU.add).then_inc((x_ok, x2_ok)[k][l], 1)
                dve.wait_ge((x_ok, x2_ok)[k][l], b + 1)

            def project(l):
                NB = blocks_of(l)
                dve.wait_ge(rows_in[l], 64 if NB > LAT_B else 48)
                for b in range(NB + 1):
                    if b < NB:
                        dve.wait_ge(y_mm[l], b + 1)
                        for half in range(2):
                            c = slice(half * 512, (half + 1) * 512)
                            last = tt(tmp[:, c], ps[b % 2 * 2 + half][:, :], gate[:, b // LAT_B, c], ALU.mult)
                        last.then_inc(y_used[l], 1)
                        dve.wait_ge(y_used[l], b + 1)
                        link(dve.scalar_tensor_tensor(x[:, b, :], x[:, b, :], ALPHA, tmp, ALU.mult, ALU.add))
                        norm(l, 0, b)
                    if b:
                        to_columns(l, 1, b - 1)

            def queries(l):
                NB = blocks_of(l)
                T = NB * P
                dve.sem_inc(topk_ok[l], 2)
                for k in range(KC):
                    dve.wait_ge(hh_ok[l], k + 1)
                    dve.scalar_tensor_tensor(hl[:, k, 0:T], h2T[:, k, 0:T], S_H, hh[:, k, 0:T], ALU.mult, ALU.subtract)
                own.clear()
                with dve.Fori(0, PH) as i:
                    for s in range(2):
                        dve.wait_ge(s_mm[l], i * 2 + (s + 1))
                        svj, sij = svj2[s], sij2[s]
                        hold()
                        sc = [ps[4 + 2 * s + b // 4][:, (b % 4) * P:(b % 4 + 1) * P] for b in range(NB)]
                        for b in range(NB):
                            last = dve.max(svj[:, b, 0:8], sc[b])
                        link(last)
                        for b in range(NB):
                            dve.max_index(sij[:, b, 0:8], svj[:, b, 0:8], sc[b])
                        for b in range(NB):
                            last = dve.match_replace(left[:, b, :], svj[:, b, 0:8], sc[b], NEG)
                        link(last)
                        for b in range(NB):
                            last = dve.max(svj[:, b, 8:16], left[:, b, :])
                        link(last)
                        for b in range(NB):
                            last = dve.max_index(sij[:, b, 8:16], svj[:, b, 8:16], left[:, b, :])
                        link(last)
                        dve.tensor_copy(sv[:, 0:NB, ds(i), s, :].rearrange("p b a t -> p b (a t)"), svj[:, 0:NB, :])
                        dve.tensor_copy(si[:, 0:NB, ds(i), s, :].rearrange("p b a t -> p b (a t)"), sij[:, 0:NB, :]).then_inc(topk_ok[l], 1)
                    dve.wait_ge(topk_ok[l], i * 2 + 4)
                    hold()
                    own.clear()

            def routing(l):
                dve.sem_inc(g_mm[l], 2)
                own.clear()
                with dve.Fori(0, blocks_of(l)) as b:
                    svb = sv[:, ds(b), :, :, :].rearrange("p b h s t -> p (b h) s t")
                    sib = si[:, ds(b), :, :, :].rearrange("p b h s t -> p (b h) s t")
                    for a0, na, nb, c0 in RECTS:
                        last = tt(cand[:, :, c0:c0 + na * nb].rearrange("p h (a b) -> p h a b", a=na),
                                  svb[:, :, 0, a0:a0 + na][:, :, :, None].to_broadcast([P, PH, na, nb]),
                                  svb[:, :, 1, 0:nb][:, :, None, :].to_broadcast([P, PH, na, nb]), ALU.add)
                    link(last)
                    for h in range(PH):
                        last = dve.max(cv[:, h, 0:8], cand[:, h, :])
                    link(last)
                    for h in range(PH):
                        dve.max_index(ci[:, h, 0:8], cv[:, h, 0:8], cand[:, h, :])
                    for h in range(PH):
                        last = dve.match_replace(cand2[:, h, :], cv[:, h, 0:8], cand[:, h, :], NEG)
                    link(last)
                    for h in range(PH):
                        last = dve.max(cv[:, h, 8:16], cand2[:, h, :])
                    link(last)
                    for h in range(PH):
                        last = dve.max_index(ci[:, h, 8:16], cv[:, h, 8:16], cand2[:, h, :])
                    gat = route[:, 2, :].rearrange("p (h t) -> p h t", h=PH)
                    link(last)
                    tt(gat, cv, cv[:, :, 0:1].to_broadcast([P, PH, TOPK]), ALU.subtract).then_inc(expo_in[l], 1)
                    cif = ci.rearrange("p h t -> p (h t)")
                    dve.tensor_scalar(shifted[:, 0, :], cif, 3, None, ALU.logical_shift_right)
                    dve.tensor_scalar(shifted[:, 1, :], cif, 2, None, ALU.logical_shift_right)
                    link(dve.tensor_copy(pos[:, 0, :], cif))
                    link(dve.tensor_copy(pos[:, 1:3, :], shifted[:, :, :]))
                    p0, p3, p2 = pos[:, 0, :], pos[:, 1, :], pos[:, 2, :]
                    for r in range(3):
                        dve.tensor_scalar(inrect[:, r, :], p0, float(RECTS[r + 1][3]), None, ALU.is_ge)
                    tt(part[:, 0, :], p2, p3, ALU.subtract)
                    link(tt(part[:, 1, :], p0, p2, ALU.subtract))
                    m1, m2, m3 = inrect[:, 0, :], inrect[:, 1, :], inrect[:, 2, :]
                    stt = dve.scalar_tensor_tensor
                    stt(rank[:, 0, :], p3, -1.0, m1, ALU.add, ALU.mult)
                    stt(part[:, 0, :], part[:, 0, :], -5.0, m2, ALU.add, ALU.mult)
                    stt(part[:, 1, :], part[:, 1, :], -42.0, m3, ALU.add, ALU.mult)
                    stt(part[:, 2, :], p3, 8.0, m1, ALU.mult, ALU.mult)
                    stt(part[:, 3, :], p3, -2.0, p2, ALU.mult, ALU.add)
                    link(stt(part[:, 4, :], p2, -4.0, p0, ALU.mult, ALU.add))
                    tt(rank[:, 0, :], rank[:, 0, :], part[:, 0, :], ALU.add)
                    stt(part[:, 3, :], part[:, 3, :], 4.0, m2, ALU.mult, ALU.mult)
                    tt(part[:, 4, :], part[:, 4, :], m3, ALU.mult)
                    link(tt(rank[:, 1, :], p0, part[:, 2, :], ALU.subtract))
                    tt(rank[:, 0, :], rank[:, 0, :], part[:, 1, :], ALU.add)
                    link(tt(rank[:, 1, :], rank[:, 1, :], part[:, 3, :], ALU.subtract))
                    link(tt(rank[:, 1, :], rank[:, 1, :], part[:, 4, :], ALU.subtract))
                    for s in range(2):
                        tt(hot[s], rank[:, s, :, None].to_broadcast([P, NR, TOPK]), iota[:, None, 0:TOPK].to_broadcast([P, NR, TOPK]), ALU.is_equal).then_inc(rank_ok[l], 1)
                    dve.wait_ge(expo_ok[l], b + 1)
                    link(dve.reduce_sum(gsum, gat, axis=AX.X))
                    link(dve.reciprocal(gsum, gsum))
                    link(tt(gat, gat, gsum[:, :, None].to_broadcast([P, PH, TOPK]), ALU.mult))
                    for s in range(2):
                        dve.wait_ge(rank_idx[l], b * 2 + (s + 1))
                        last = dve.reduce_sum(route[:, s, :], hot[s], axis=AX.X)
                    last.then_inc(route_ok[l], 1)
                    dve.wait_ge(routeT_ok[l], b + 1)
                    hold()
                    with dve.Fori(0, P // (2 * QT)) as i:
                        for h in range(2):
                            dve.wait_ge(g_mm[l], b * (P // QT) + i * 2 + (h + 1))
                            for oh, j in ((oh1, 0), (oh2, 1)):
                                last = tt(oh[h], iota[:, None, :].to_broadcast([P, QT, NKEY]),
                                          routeT[:, j, ds(i * (2 * QT) + h * QT, QT)][:, :, None].to_broadcast([P, QT, NKEY]), ALU.is_equal)
                                if not j:
                                    last.then_inc(hot_ok[l], 1)
                            last.then_inc(hot2_ok[l], 1)
                    own.clear()

            def experts(l):
                NB = blocks_of(l)
                T = NB * P
                outs = [(b, half) for b in range(NB) for half in range(2)]
                own.clear()
                link(dve.memset(facc[:, 0:NB, :], 0.0))
                dve.sem_inc(ul_ok[l], 2)
                dve.sem_inc(vl_ok[l], 2)
                dve.sem_inc(wf_ok[l], GRP)
                dve.sem_inc(f_ok[l], 4)
                own.clear()

                def u_split(n, s):
                    dve.wait_ge(uh_ok[l], n + 1)
                    dve.scalar_tensor_tensor(usl[s], uraw[s], S_U, ush[s], ALU.mult, ALU.subtract).then_inc(ul_ok[l], 1)

                def group(g, more, mod):
                    if mod:
                        for s in range(2):
                            mod_rows(l + 1, g * 2 + s, s)
                    for e in range(GRP):
                        s = e % 2
                        n = g * GRP + e
                        if e < GRP - 1 or more:
                            u_split(n + 1, (e + 1) % 2)
                        dve.wait_ge(vh_ok[l], n + 1)
                        dve.scalar_tensor_tensor(vsl[:, e, :], vraw[s], S_V, vsh[:, e, :], ALU.mult, ALU.subtract).then_inc(vl_ok[l], 1)
                        dve.wait_ge(gelu_ok[l], n + 3)
                        dve.wait_ge(g_in[e][l], g * 16 + 16)
                        a3 = actb[s][:, 0:T].rearrange("p (b c) -> p b c", c=P)
                        w3 = wf[s][:, 0:T].rearrange("p (b c) -> p b c", c=P)
                        tt(w3, a3, graw[:, e, 0:NB, :], ALU.mult).then_inc(wf_ok[l], 1)
                        dve.wait_ge(wh_ok[l], n + 1)
                        dve.scalar_tensor_tensor(wtl[:, e, 0:T], wf[s][:, 0:T], S_W, wth[:, e, 0:T], ALU.mult, ALU.subtract).then_inc(wl_ok[l], 1)
                    for j, (b, half) in enumerate(outs):
                        dve.wait_ge(v_mm[l], g * len(outs) + (j + 2))
                        f = facc[:, b, half * 512:(half + 1) * 512]
                        tt(f, f, ps[4 + j % 4][:, :], ALU.add).then_inc(f_ok[l], 1)
                    dve.wait_ge(f_ok[l], g * len(outs) + (len(outs) + 4))

                u_split(0, 0)
                for lo, hi, mod in group_runs(l, NGRP - 1):
                    with dve.Fori(lo, hi) as g:
                        group(g, True, mod)
                group(NGRP - 1, False, False)

            def norm2(l):
                NB = blocks_of(l)
                dve.wait_ge(rows2_in[l], 64 if NB > LAT_B else 48)
                for b in range(NB):
                    link(dve.scalar_tensor_tensor(ftmp, facc[:, b, :], 1.0 / (S_W * S_V), gate[:, b // LAT_B, :], ALU.mult, ALU.mult))
                    link(dve.scalar_tensor_tensor(x[:, b, :], x[:, b, :], ALPHA, ftmp, ALU.mult, ALU.add))
                    norm(l, 1, b)

            for l in range(DEPTH):
                for stage in (modulation, columns, mixer, project, queries, routing, experts, norm2):
                    stage(l)
                    stages.end()
                if l < DEPTH - 1:
                    stages.begin()


def layouts(inputs):
    import numpy as np

    a = {k: np.asarray(v) for k, v in inputs.items()}
    L = DEPTH
    out = {
        "x": np.concatenate([a["x"][0], a["ctx"][0]], 0),
        "c2": np.stack([a["c"][0], a["c_ctx"]], -1).reshape(KC, P, 2).transpose(1, 0, 2),
        "b_mod": a["b_mod"].reshape(L, NMG, MODW),
        "w_mod": a["w_mod"].reshape(L, KC, P, NMG, MODW).transpose(0, 3, 2, 1, 4),
        "w_in": a["w_in"].reshape(L, KC, P, NCOL, P).transpose(0, 3, 2, 1, 4),
        "w_v": a["w_in"][:, :, 5 * CONV:6 * CONV].reshape(L, KC, P, CONV).transpose(0, 2, 1, 3),
        "w_g": a["w_in"][:, :, 6 * CONV:].reshape(L, KC, P, CONV).transpose(0, 2, 1, 3),
        "conv_w": a["conv_w"].reshape(L, CCT, P, 3).transpose(0, 2, 1, 3),
        "w_out": a["w_out"].reshape(L, KC, P, D).transpose(0, 2, 1, 3),
        "ln": np.stack([a["ln1_g"], a["ln1_b"], a["ln2_g"], a["ln2_b"]], 1),
        "w_q": a["peer_wq"].reshape(L, KC, P, 2 * PH, P).transpose(0, 3, 2, 1, 4),
        "keys": a["peer_keys"].transpose(0, 3, 1, 2),
        "peer_u": a["peer_u"].reshape(L, NKEY, P, KC, P).transpose(0, 1, 4, 3, 2),
        "peer_v": a["peer_v"].reshape(L, NKEY, P, D),
        "ident": np.eye(P),
        "iota": np.tile(np.arange(P), (P, 1)),
    }
    nf = P // 4
    d = np.arange(P)
    where = np.arange(SEQ)
    ang = np.where(d[:, None] < P // 2, where // GRID, where % GRID) * 10000.0 ** (-(d[:, None] % nf) / nf)
    out["ropeC"], out["ropeS"] = np.cos(ang), np.sin(ang)
    perm = np.zeros((P, P))
    for i in d:
        if i % (P // 2) < nf:
            perm[i + nf, i] = -1.0
        else:
            perm[i - nf, i] = 1.0
    out["perm"] = perm
    h = np.arange(HEADS)
    lf = np.log1p(-np.exp2(-(5.0 + h)))[:, None, None]
    lb = np.log1p(-np.exp2(-(5.5 + h)))[:, None, None]
    u = (np.arange(STRIP1)[None, :] - 384 - d[:, None])[None]
    out["strip1"] = np.where(u >= 0, np.exp(np.abs(u) * lf), np.exp(np.abs(u) * lb)) * P ** -0.5
    u = (np.arange(STRIP2)[None, :] - P - d[:, None])[None]
    out["strip2"] = (np.exp((u + CTX) * lf) + np.exp((SEQ - u) * lb)) * P ** -0.5
    return {k: np.ascontiguousarray(v, np.float32) for k, v in out.items()}


def kernel(**inputs):
    import concourse.bacc as bacc
    from concourse.bass_utils import run_bass_kernel_spmd

    arrays = layouts(inputs)
    nc = bacc.Bacc("TRN2", target_bir_lowering=False, num_devices=1)
    t = {k: nc.dram_tensor(f"in_{k}", v.shape, F32, kind="ExternalInput").ap() for k, v in arrays.items()}
    t["gates"] = nc.dram_tensor("gates", [NBLK, P, NKEY, P], F32, kind="Internal").ap()
    t["mod"] = nc.dram_tensor("mod", [DEPTH, 2, 6 * D], F32, kind="Internal").ap()
    t["out"] = nc.dram_tensor("out", [SEQ, D], F32, kind="ExternalOutput").ap()
    build(nc, t)
    r = run_bass_kernel_spmd(nc, [{f"in_{k}": v for k, v in arrays.items()}], core_ids=[0])
    return r.results[0]["out"].reshape(1, SEQ, D)
```

```python
from contextlib import ExitStack

import concourse.bass as bass
from concourse import mybir

F32 = mybir.dt.float32
F16 = mybir.dt.float16
U32 = mybir.dt.uint32
ALU = mybir.AluOpType
ACT = mybir.ActivationFunctionType
AX = mybir.AxisListType

P = 128
D = 1024
KC = D // P
SEQ, CTX = 512, 256
LAT_B, CTX_B = SEQ // P, CTX // P
NBLK = LAT_B + CTX_B
TOK = NBLK * P
DEPTH = 2
GRID = 64
CONV = D // 2
CCT = CONV // P
HEADS = 4
NCOL = 7 * CCT
ALPHA = float((2 * DEPTH) ** 0.25)
EPS = 1e-5
NKEY = 128
PH, TOPK = 8, 16
NMOD = 6 * KC
MODW = 256
NMG = NMOD * P // MODW
MS = 4
NEG = -3.0e38
RECTS = [(0, 1, 16, 0), (1, 3, 8, 16), (4, 4, 4, 40), (8, 8, 1, 56)]
NCAND = 64
GRP = 4
NGRP = NKEY // GRP
HT = P // 2
QT = 8
QP = 5
S_H, S_U, S_W, S_V = 16.0, 1024.0, 256.0, 256.0
FIRST = (CCT, 2 * CCT, 0)
S_G = 1024.0
INV = 1.0 / (S_H * S_U)
STRIP1, STRIP2 = SEQ + 384, SEQ + 128


def blocks_of(layer):
    return NBLK if layer < DEPTH - 1 else LAT_B


def group_runs(layer, end):
    n = NMG // MS if layer < DEPTH - 1 else 0
    return [(0, n, True)] * (n > 0) + [(n, end, False)]


def nscore(layer):
    return NBLK + (CTX_B if blocks_of(layer) > LAT_B else 0)


def spans_of(layer):
    return [(0, 384), (384, 384)] if layer < DEPTH - 1 else [(0, 512)]


def build(nc, t):
    with ExitStack() as ctx:
        def sb(name, shape, dt=F32):
            return ctx.enter_context(nc.sbuf_tensor(name, shape, dt))

        def sem(name):
            return ctx.enter_context(nc.semaphore(name))

        layer_sems = []

        def persem(name):
            layer_sems.append(sem(name))
            return layer_sems[-1:] * DEPTH

        x = sb("x", [P, NBLK, D])
        ident = sb("ident", [P, P])
        iota = sb("iota", [P, P])
        perm = sb("perm", [P, P])
        cT = sb("cT", [P, KC, 2])
        sT = sb("sT", [P, KC, 2])
        modc = sb("modc", [P, NMOD, 2])
        eps = sb("eps", [P, 1])
        gate = sb("gate", [P, 2, D])
        lng = sb("lng", [P, D])
        lnb = sb("lnb", [P, D])
        st = sb("st", [P, 2, 6])
        mv = sb("mv", [P, NBLK, 2])
        sd = sb("sd", [P, NBLK])
        rs = sb("rs", [P, NBLK])
        nm = sb("nm", [P, NBLK])

        ARENA = 42200
        MODB = 15104
        arena = sb("arena", [P, ARENA])
        at = [0]

        def take(*shape, dt=F32, where=None):
            n = 1
            for s in shape:
                n *= s
            words = n if dt != F16 else n // 2
            a = at[0] if where is None else where
            assert a + words <= ARENA, (a, words)
            if where is None:
                at[0] = a + words
            v = arena[:, a:a + words]
            if dt != F32:
                v = v.bitcast(dt)
            if len(shape) == 1:
                return v
            names = "abcd"[:len(shape)]
            return v.rearrange(f"p ({' '.join(names)}) -> p {' '.join(names)}",
                               **{n_: s for n_, s in zip(names, shape)})

        MODAT = 32384
        at[0] = MODAT
        wmod = [take(KC, MODW) for _ in range(MS)]
        bmodr = [take(MODW) if s >= 2 else take(MODW, where=MODB + s * MODW) for s in range(MS)]
        modr = [take(MODW) for _ in range(MS)]
        modt = take(2, P, where=0)
        at[0] = 0
        hT = take(KC, TOK)
        cath = take(KC, TOK, dt=F16, where=0)
        catl = take(KC, TOK, dt=F16, where=KC * TOK // 2)
        hh = take(KC, TOK, dt=F16)
        hl = take(KC, TOK, dt=F16)
        v_nat = take(NBLK, CONV)
        g_nat = take(NBLK, CONV)
        big = at[0]
        wv = take(KC, CONV)
        wg = take(KC, CONV)
        woh = take(KC, D, dt=F16, where=big)
        wol = take(KC, D, dt=F16, where=big + KC * D // 2)
        wring = [take(KC, P) for _ in range(3)]
        slot3_at = at[0] - KC * P
        strip1 = take(STRIP1)
        strip2 = take(STRIP2)
        ropeC = take(SEQ)
        ropeS = take(SEQ)
        convw = take(CCT, 3)
        split_at = at[0]
        wvh, wvl, wgh, wgl = (take(KC, CONV, dt=F16) for _ in range(4))
        at[0] = split_at
        wrh = [take(KC, P, dt=F16) for _ in range(3)]
        wrl = [take(KC, P, dt=F16) for _ in range(3)]
        rest = at[0]
        cg_sb = take(TOK)
        z_sb = take(TOK)
        y_sb = take(TOK)
        at[0] = rest
        q_raw = take(SEQ)
        k_raw = take(SEQ)
        qT = take(TOK)
        kT = take(TOK)
        Psc = take(NBLK, SEQ)
        gst = take(NBLK, 6)
        wo_raw = take(D)
        Pctx = take(CTX_B, CTX, where=split_at + KC * P)
        onrm = take(NBLK, P, where=slot3_at)
        tmp = take(D, where=rest)
        h2T = take(KC, TOK, where=big + KC * D + 2 * KC * P)
        assert big + KC * D + 2 * KC * P + KC * TOK <= rest
        at[0] = after_h = 2 * KC * TOK
        sv = take(NBLK, PH, 2, TOPK)
        si = take(NBLK, PH, 2, TOPK)
        after_s = at[0]
        wq = [take(KC, P) for _ in range(2)]
        keys = take(2, NKEY)
        assert at[0] <= big
        wqh = [take(KC, P, dt=F16, where=big + KC * D + s * KC * P) for s in range(2)]
        wql = [take(KC, P, dt=F16, where=big + KC * D + s * KC * P + KC * P // 2) for s in range(2)]
        qs = [take(TOK) for _ in range(2)]
        svj2 = [take(NBLK, TOPK) for _ in range(2)]
        sij2 = [take(NBLK, TOPK, dt=U32) for _ in range(2)]
        left = take(NBLK, NKEY)
        NR = PH * TOPK
        at[0] = 0
        cand = take(PH, NCAND)
        cand2 = take(PH, NCAND)
        cv = take(PH, TOPK)
        ci = take(PH, TOPK, dt=U32)
        shifted = take(2, NR, dt=U32)
        pos = take(3, NR)
        inrect = take(3, NR)
        part = take(6, NR)
        rank = take(2, NR)
        rankh = take(2, NR, dt=F16)
        route = take(3, NR)
        gsum = take(PH)
        expo = take(NR)
        gaten = take(NR)
        assert at[0] <= KC * TOK
        at[0] = after_s
        routeT = take(4, P, dt=F16)
        glowT = take(P)
        hot_at = at[0]
        hot = take(2, TOPK, NR, dt=F16)
        iotar = take(TOPK, NR, dt=F16)
        after_hot = at[0] = hot_at + 2 * KC * P + 2 * D
        oh2, oh1, oh1h, oh1l = ([take(NKEY, QT, dt=F16) for _ in range(2)] for _ in range(4))
        iotaq = take(NKEY, QT, dt=F16)
        after_oh = at[0]
        at[0] = 0
        facc = take(NBLK, D)
        at[0] = after_h
        ush = [take(KC, P, dt=F16) for _ in range(2)]
        usl = [take(KC, P, dt=F16) for _ in range(2)]
        actb0 = take(TOK)
        assert at[0] == MODB and MODB + 2 * MODW <= hot_at
        at[0] = hot_at
        uraw = [take(KC, P) for _ in range(2)]
        vraw = [take(D) for _ in range(2)]
        assert at[0] == after_hot
        vsh = take(GRP, D, dt=F16)
        vsl = take(GRP, D, dt=F16)
        actb = [actb0, take(TOK)]
        assert at[0] >= after_oh
        gbuf_at = at[0]
        graw = take(GRP // 2, 2 * NBLK, 2, HT)
        wf = [take(TOK) for _ in range(2)]
        wth = take(GRP, TOK, dt=F16)
        wtl = take(GRP, TOK, dt=F16)
        assert at[0] <= MODAT
        gbuf = [take(NKEY, HT, where=gbuf_at + h * NKEY * HT) for h in range(2)]
        ftmp = take(D, where=after_h)

        ps = [ctx.enter_context(nc.psum_tensor(f"ps{i}", [P, 512], F32)) for i in range(8)]

        consts_in = sem("consts_in")
        x_in = sem("x_in")
        silu_ok = sem("silu_ok")
        eps_ok = sem("eps_ok")
        stage_done = sem("stage_done")
        out_done = sem("out_done")
        dve_chain = sem("dve_chain")
        pool_chain = sem("pool_chain")
        dve_held = sem("dve_held")
        pool_held = sem("pool_held")
        wmod_in = [persem(f"wmod_in{s}_") for s in range(MS)]
        rows_in = persem("rows_in")
        mod_mm = persem("mod_mm")
        mod_ok = persem("mod_ok")
        modr_out = [persem(f"modr_out{s}_") for s in range(MS)]
        modt_in = persem("modt_in")
        modt_mm = persem("modt_mm")
        modc_ok = persem("modc_ok")
        tr_mm = [persem(f"tr_mm{k}_") for k in range(2)]
        tr_dve = [persem(f"tr_dve{k}_") for k in range(2)]
        tr_act = [persem(f"tr_act{k}_") for k in range(2)]
        mh_ok = persem("mh_ok")
        ml_ok = persem("ml_ok")
        vgh_ok = persem("vgh_ok")
        vgl_ok = persem("vgl_ok")
        wrh_ok = persem("wrh_ok")
        wrl_ok = persem("wrl_ok")
        wv_in = persem("wv_in")
        wg_in = persem("wg_in")
        vg_mm = persem("vg_mm")
        vg_ev = persem("vg_ev")
        wo_in = persem("wo_in")
        woh_ok = persem("woh_ok")
        wol_ok = persem("wol_ok")
        cath_ok = persem("cath_ok")
        cw_in = persem("cw_in")
        wr_in = [persem(f"wr_in{r}_") for r in range(3)]
        conv_mm = persem("conv_mm")
        cg_ev = persem("cg_ev")
        conv_ok = persem("conv_ok")
        strip_in = persem("strip_in")
        qk_mm = persem("qk_mm")
        qk_ev = persem("qk_ev")
        rot_mm = persem("rot_mm")
        rope_ok = persem("rope_ok")
        sc_mm = persem("sc_mm")
        p_ok = persem("p_ok")
        o_mm = persem("o_mm")
        var_ok = persem("var_ok")
        sd_ok = persem("sd_ok")
        ret_ok = persem("ret_ok")
        retT_mm = persem("retT_mm")
        head_ok = persem("head_ok")
        y_mm = persem("y_mm")
        y_used = persem("y_used")
        lnrs_ok = [persem(f"lnrs_ok{k}_") for k in range(2)]
        lnx_ok = [persem(f"lnx_ok{k}_") for k in range(2)]
        lnvar_ok = [persem(f"lnvar_ok{k}_") for k in range(2)]
        lnsd_ok = [persem(f"lnsd_ok{k}_") for k in range(2)]
        x_ok = persem("x_ok")
        wq_in = [persem(f"wq_in{s}_") for s in range(2)]
        keys_in = persem("keys_in")
        hh_ok = persem("hh_ok")
        hl_ok = persem("hl_ok")
        wqh_ok = persem("wqh_ok")
        wql_ok = persem("wql_ok")
        q_mm = persem("q_mm")
        q_ev = persem("q_ev")
        s_mm = persem("s_mm")
        topk_ok = persem("topk_ok")
        expo_in = persem("expo_in")
        expo_ok = persem("expo_ok")
        route_ok = persem("route_ok")
        routeT_mm = persem("routeT_mm")
        routeT_ok = persem("routeT_ok")
        glo_ok = persem("glo_ok")
        rank_ok = persem("rank_ok")
        rank_idx = persem("rank_idx")
        hot_ok = persem("hot_ok")
        hot2_ok = persem("hot2_ok")
        hotg_ok = persem("hotg_ok")
        hota_ok = persem("hota_ok")
        g_mm = persem("g_mm")
        g_ev = persem("g_ev")
        g_out = [persem(f"g_out{h}_") for h in range(2)]
        u_in = [persem(f"u_in{s}_") for s in range(2)]
        v_in = [persem(f"v_in{s}_") for s in range(2)]
        g_in = [persem(f"g_in{s}_") for s in range(GRP // 2)]
        uh_ok = persem("uh_ok")
        ul_ok = persem("ul_ok")
        vh_ok = persem("vh_ok")
        vl_ok = persem("vl_ok")
        u_mm = persem("u_mm")
        gelu_ok = persem("gelu_ok")
        wf_ok = persem("wf_ok")
        wh_ok = persem("wh_ok")
        wl_ok = persem("wl_ok")
        v_mm = persem("v_mm")
        f_ok = persem("f_ok")
        rows2_in = persem("rows2_in")
        x2_ok = persem("x2_ok")
        x2last_ok = persem("x2last_ok")

        class Own:

            def __init__(self, eng, s):
                self.eng, self.s, self.n = eng, s, 0

            def link(self, ins):
                self.n += 1
                ins.then_inc(self.s, 1)
                self.eng.wait_ge(self.s, self.n)

            def clear(self):
                if self.n:
                    self.eng.sem_clear(self.s)
                    self.n = 0

        class Stages:

            def __init__(self, eng):
                self.eng, self.n = eng, 0

            def end(self):
                self.n += 1
                self.eng.drain().then_inc(stage_done, 1)
                self.eng.wait_ge(stage_done, 5 * self.n)

            def begin(self):
                self.end()
                self.eng.drain()

        def new_layer(sp):
            nums = sorted(s.num for s in layer_sems)
            runs = [i for i in range(len(nums)) if not i or nums[i] != nums[i - 1] + 1] + [len(nums)]
            for a, b in zip(runs, runs[1:]):
                sp.sem_clear(range(nums[a], nums[b - 1] + 1))

        def ds(i, n=1):
            return bass.ds(i, n)

        block = ctx.enter_context(nc.Block())

        @block.sync
        def _(sp):
            stages = Stages(sp)

            def mod_load(run, n, s):
                sp.wait_ge(mod_ok[0], n + (NMG * run + 1))
                sp.dma_start(wmod[s], t["w_mod"][run, ds(n)].rearrange("g p a b -> (g p) a b")).then_inc(wmod_in[s][0], 16)
                sp.dma_start(bmodr[s][0:2, :], t["b_mod"][run, ds(n)].to_broadcast([2, MODW])).then_inc(wmod_in[s][0], 16)

            def mod_stored(run):
                for s in range(MS):
                    sp.wait_ge(modr_out[s][0], 16 * (NMG // MS * (run + 1) + 1))

            def gate_row(l, r, which, s):
                sp.dma_start(gate[:, r, :], t["mod"][l, r:r + 1, which * D:(which + 1) * D].to_broadcast([P, D])).then_inc(s[l], 16)

            def modulation(l):
                if l == 0:
                    for dst, src in ((ident, "ident"), (iota, "iota"), (perm, "perm")):
                        sp.dma_start(dst[:, :], t[src]).then_inc(consts_in, 16)
                    sp.dma_start(cT[:, :, :], t["c2"]).then_inc(consts_in, 16)
                    with sp.Fori(0, NMG // MS) as i:
                        for s in range(MS):
                            mod_load(0, i * MS + s, s)
                    sp.dma_start(x[:, :, :], t["x"].rearrange("(b p) d -> p b d", p=P)).then_inc(x_in, 16)
                    mod_stored(0)
                for r in range(2):
                    sp.dma_start(modt[0:NMOD, r, :], t["mod"][l, r].rearrange("(a b) -> a b", b=P)).then_inc(modt_in[l], 16)
                for r in range(2 if l == 0 else 1):
                    gate_row(l, r, 2, rows_in)
                sp.dma_start(lng[:, :], t["ln"][l, 0:1, :].to_broadcast([P, D])).then_inc(rows_in[l], 16)
                sp.dma_start(lnb[:, :], t["ln"][l, 1:2, :].to_broadcast([P, D])).then_inc(rows_in[l], 16)
                sp.dma_start(wv, t["w_v"][l]).then_inc(wv_in[l], 16)
                sp.dma_start(wg, t["w_g"][l]).then_inc(wg_in[l], 16)

            def w_tile(dst, l, tile, s):
                sp.dma_start(dst, t["w_in"][l, ds(tile)].rearrange("g p a b -> (g p) a b")).then_inc(s, 16)

            def columns(l):
                for r in range(3):
                    w_tile(wring[r], l, FIRST[r], wr_in[r][l])
                sp.dma_start(wo_raw, t["w_out"][l, 0]).then_inc(wo_in[l], 16)
                sp.dma_start(convw, t["conv_w"][l]).then_inc(cw_in[l], 16)
                sp.dma_start(ropeC, t["ropeC"]).then_inc(cw_in[l], 16)
                sp.dma_start(ropeS, t["ropeS"]).then_inc(cw_in[l], 16)
                sp.dma_start(strip1, t["strip1"][0]).then_inc(strip_in[l], 16)
                sp.dma_start(strip2, t["strip2"][0]).then_inc(strip_in[l], 16)

            def mixer(l):
                def wo_chunk(k):
                    sp.wait_ge(wol_ok[l], k)
                    sp.dma_start(wo_raw, t["w_out"][l, ds(k)].rearrange("g p d -> (g p) d")).then_inc(wo_in[l], 16)

                with sp.Fori(1, CCT) as i:
                    for r in range(3):
                        sp.wait_ge(wrl_ok[l], i * 3 + (r - 2))
                        w_tile(wring[r], l, i + FIRST[r], wr_in[r][l])
                    for c in range(2):
                        wo_chunk(i * 2 + (c - 1))
                for r in range(2):
                    sp.wait_ge(wrl_ok[l], 3 * CCT + r - 2)
                    w_tile(wring[r], l, (3 + r) * CCT, wr_in[r][l])
                wo_chunk(2 * CCT - 1)
                with sp.Fori(1, HEADS) as i:
                    for r in range(2):
                        sp.wait_ge(wrl_ok[l], i * 2 + (3 * CCT + r - 1))
                        w_tile(wring[r], l, i + (3 + r) * CCT, wr_in[r][l])
                    sp.wait_ge(p_ok[l], i * nscore(l))
                    sp.dma_start(strip1, t["strip1"][ds(i)].rearrange("g p a -> (g p) a")).then_inc(strip_in[l], 16)
                    sp.dma_start(strip2, t["strip2"][ds(i)].rearrange("g p a -> (g p) a")).then_inc(strip_in[l], 16)

            def project(l):
                sp.dma_start(keys, t["keys"][l]).then_inc(keys_in[l], 16)
                for s in range(2):
                    sp.dma_start(wq[s], t["w_q"][l, s]).then_inc(wq_in[s][l], 16)

            def queries(l):
                with sp.Fori(1, PH) as i:
                    for s in range(2):
                        sp.wait_ge(wql_ok[l], i * 2 + (s - 1))
                        sp.dma_start(wq[s], t["w_q"][l, ds(i * 2 + s)].rearrange("g p a b -> (g p) a b")).then_inc(wq_in[s][l], 16)

            def store_gates(l, b):
                for h in range(2):
                    sp.wait_ge(g_ev[l], b * (P // QT) + (HT // QT * (h + 1) + 2))
                    sp.dma_start(t["gates"][ds(b * 2 + h)].rearrange("b p i t -> (b p) i t"), gbuf[h]).then_inc(g_out[h][l], 16)

            def routing(l):
                NB = blocks_of(l)
                for h in range(2):
                    sp.sem_inc(g_out[h][l], 16)
                with sp.Fori(0, NB - 1) as b:
                    store_gates(l, b)
                sp.wait_ge(route_ok[l], NB)
                sp.dma_start(uraw[0], t["peer_u"][l, 0]).then_inc(u_in[0][l], 16)
                sp.dma_start(vraw[0], t["peer_v"][l, 0]).then_inc(v_in[0][l], 16)
                sp.dma_start(uraw[1], t["peer_u"][l, 1]).then_inc(u_in[1][l], 16)
                store_gates(l, NB - 1)

            def experts(l):
                NB = blocks_of(l)

                def load_u(n, s):
                    sp.wait_ge(ul_ok[l], n + 1)
                    sp.dma_start(uraw[s], t["peer_u"][l, ds(n)].rearrange("g p a b -> (g p) a b")).then_inc(u_in[s][l], 16)

                def load_v(n, s):
                    sp.wait_ge(vl_ok[l], n + 1)
                    sp.dma_start(vraw[s], t["peer_v"][l, ds(n)].rearrange("g p a -> (g p) a")).then_inc(v_in[s][l], 16)

                def group(g, more, mod):
                    for e in range(GRP):
                        n = g * GRP + e
                        if mod and e == 0:
                            for s in range(MS):
                                mod_load(l + 1, g * MS + s, s)
                        if e % 2 == 0:
                            sp.wait_ge(wf_ok[l], n + 2)
                            sp.dma_start(graw[:, e // 2, 0:2 * NB, :, :].rearrange("p c i t -> p c (i t)"),
                                         t["gates"][0:2 * NB, :, ds(n, 2), :].rearrange("c p i t -> p c (i t)")).then_inc(g_in[e // 2][l], 16)
                        if more or e < GRP - 1:
                            load_v(n + 1, (e + 1) % 2)
                        if more or e < GRP - 2:
                            load_u(n + 2, e % 2)

                for h in range(2):
                    sp.wait_ge(g_out[h][l], 16 * (NB + 1))
                for lo, hi, mod in group_runs(l, NGRP - 1):
                    with sp.Fori(lo, hi) as g:
                        group(g, True, mod)
                group(NGRP - 1, False, False)
                if l < DEPTH - 1:
                    mod_stored(l + 1)
                for r in range(NB // LAT_B + (1 if NB > LAT_B else 0)):
                    gate_row(l, r, 5, rows2_in)
                sp.dma_start(lng[:, :], t["ln"][l, 2:3, :].to_broadcast([P, D])).then_inc(rows2_in[l], 16)
                sp.dma_start(lnb[:, :], t["ln"][l, 3:4, :].to_broadcast([P, D])).then_inc(rows2_in[l], 16)
                if l == DEPTH - 1:
                    for b in range(LAT_B):
                        sp.wait_ge(*((x2_ok[l], b + 1) if b < LAT_B - 1 else (x2last_ok[l], 1)))
                        sp.dma_start(t["out"][b * P:(b + 1) * P, :], x[:, b, :]).then_inc(out_done, 16)
                    sp.wait_ge(out_done, 16 * LAT_B)

            def nothing(l):
                pass

            for l in range(DEPTH):
                for stage in (modulation, columns, mixer, project, queries, routing, experts):
                    stage(l)
                    stages.end()
                if l < DEPTH - 1:
                    new_layer(sp)
                    stages.begin()

        @block.tensor
        def _(pe):
            stages = Stages(pe)

            def mm(out, lhsT, rhs, start, stop):
                return pe.matmul(out, lhsT, rhs, start=start, stop=stop)

            def mm3(out, a, b, start, stop):
                mm(out, a[0], b[0], start, False)
                mm(out, a[0], b[1], False, False)
                return mm(out, a[1], b[0], False, stop)

            def mod_rows(run, n, s):
                pe.wait_ge(wmod_in[s][0], n * (32 // MS) + (32 - 32 // MS * (s - NMG * run)))
                for k in range(KC):
                    last = mm(ps[4 + s][0:2, 0:MODW], sT[:, k, :], wmod[s][:, k, :], k == 0, k == KC - 1)
                last.then_inc(mod_mm[0], 1)

            def modulation(l):
                if l == 0:
                    pe.wait_ge(consts_in, 64)
                    pe.wait_ge(silu_ok, 1)
                    with pe.Fori(0, NMG // MS) as i:
                        for s in range(MS):
                            pe.wait_ge(mod_ok[0], i * MS + (s + 1))
                            mod_rows(0, i * MS + s, s)
                pe.wait_ge(modt_in[l], 32)
                for r in range(2):
                    last = pe.transpose(ps[0][:, r * NMOD:(r + 1) * NMOD], modt[0:NMOD, r, :], ident[0:NMOD, 0:NMOD])
                last.then_inc(modt_mm[l], 1)

            def to_columns(l, k, b):
                for half in range(2):
                    n = 2 * b + half
                    if n >= 4:
                        pe.wait_ge((tr_act if n % 2 else tr_dve)[k][l], (n - 4) // 2 + 1)
                    for j in range(4):
                        c = half * 4 + j
                        last = pe.transpose(ps[4 + n % 4][:, j * P:(j + 1) * P], x[:, b, c * P:(c + 1) * P], ident[:, :])
                    last.then_inc(tr_mm[k][l], 1)

            def columns(l):
                if l == 0:
                    pe.wait_ge(x_in, 16)
                for b in range(NBLK):
                    to_columns(l, 0, b)

            def mixer(l):
                NB = blocks_of(l)
                TC = [(0, SEQ), (SEQ, CTX)]
                n = 0
                pe.wait_ge(ml_ok[l], NBLK)
                for m, (wh, wl) in enumerate(((wvh, wvl), (wgh, wgl))):
                    pe.wait_ge(vgl_ok[l], m + 1)
                    for b in range((NBLK, NB)[m]):
                        if n >= 2:
                            pe.wait_ge(vg_ev[l], n - 1)
                        c = slice(b * P, (b + 1) * P)
                        for k in range(KC):
                            last = mm3(ps[6 + n % 2][:, :], (hh[:, k, c], hl[:, k, c]), (wh[:, k, :], wl[:, k, :]), k == 0, k == KC - 1)
                        last.then_inc(vg_mm[l], 1)
                        n += 1
                with pe.Fori(0, CCT) as i:
                    pe.wait_ge(conv_ok[l], i + 1)
                    for r in range(3):
                        pe.wait_ge(wrl_ok[l], i * 3 + (r + 1))
                        for z, (c0, w) in enumerate(TC[:1 if NB == LAT_B else 2]):
                            for k in range(KC):
                                last = mm3(ps[2 * r + z][:, 0:w], (wrh[r][:, k, :], wrl[r][:, k, :]),
                                           (hh[:, k, c0:c0 + w], hl[:, k, c0:c0 + w]), k == 0, k == KC - 1)
                        last.then_inc(conv_mm[l], 1)
                pe.wait_ge(conv_ok[l], CCT + 1)

                def qk(i, k):
                    for r in range(2):
                        pe.wait_ge(wrl_ok[l], i * 2 + (3 * CCT + 2 * k + r + 1))
                        for z, (c0, w) in enumerate(TC):
                            if z and r == 0 and NB == LAT_B:
                                continue
                            for c in range(KC):
                                last = mm3(ps[2 * r + z][:, 0:w], (wrh[r][:, c, :], wrl[r][:, c, :]),
                                           (hh[:, c, c0:c0 + w], hl[:, c, c0:c0 + w]), c == 0, c == KC - 1)
                        last.then_inc(qk_mm[l], 1)

                def rotate(i, k):
                    for r, raw in enumerate((q_raw, k_raw)):
                        if not r and k:
                            pe.wait_ge(p_ok[l], i * NS + k * NS)
                        pe.wait_ge(qk_ev[l], i * 2 + (2 * k + r + 1))
                        mm(ps[6 + r][:, :], perm[:, :], raw, True, True).then_inc(rot_mm[l], 1)

                def scores(i, k):
                    pe.wait_ge(rope_ok[l], i * 2 + (2 * k + 2))
                    for n in range(NS):
                        if n >= 2:
                            pe.wait_ge(p_ok[l], i * NS + (k * NS + n - 1))
                        if n < NBLK:
                            mm(ps[6 + n % 2][:, :], kT[:, n * P:(n + 1) * P], qT[:, 0:SEQ], True, True).then_inc(sc_mm[l], 1)
                        else:
                            s = n - NBLK + LAT_B
                            mm(ps[6 + n % 2][:, 0:CTX], kT[:, s * P:(s + 1) * P], qT[:, SEQ:TOK], True, True).then_inc(sc_mm[l], 1)

                def values(i):
                    pe.wait_ge(p_ok[l], i * NS + NS)
                    pe.wait_ge(head_ok[l], i + 1)
                    for b in range(LAT_B):
                        for s in range(NBLK):
                            last = mm(ps[4][:, b * P:(b + 1) * P], Psc[:, s, b * P:(b + 1) * P], v_nat[:, s, ds(i * P, P)], s == 0, s == NBLK - 1)
                    if NB > LAT_B:
                        for b in range(CTX_B):
                            for s in range(CTX_B):
                                last = mm(ps[5][:, b * P:(b + 1) * P], Pctx[:, s, b * P:(b + 1) * P], v_nat[:, LAT_B + s, ds(i * P, P)], s == 0, s == CTX_B - 1)
                    last.then_inc(o_mm[l], 1)

                def turn(i):
                    pe.wait_ge(ret_ok[l], i + 1)
                    for b in range(NB):
                        last = pe.transpose(ps[4 + b // 4][:, (b % 4) * P:(b % 4 + 1) * P], onrm[:, b, :], ident[:, :])
                    last.then_inc(retT_mm[l], 1)

                NS = nscore(l)
                qk(0, 0)
                rotate(0, 0)
                scores(0, 0)
                qk(0, 1)
                rotate(0, 1)
                with pe.Fori(0, HEADS - 2) as i:
                    values(i)
                    scores(i, 1)
                    qk(i, 2)
                    turn(i)
                    rotate(i, 2)
                values(HEADS - 2)
                scores(HEADS - 2, 1)
                turn(HEADS - 2)
                values(HEADS - 1)
                turn(HEADS - 1)

            def project(l):
                NB = blocks_of(l)
                for b in range(NB + 1):
                    if b < NB:
                        if b >= 2:
                            pe.wait_ge(y_used[l], b - 1)
                        for half in range(2):
                            for k in range(KC):
                                c, d = slice(b * P, (b + 1) * P), slice(half * 512, (half + 1) * 512)
                                last = mm3(ps[b % 2 * 2 + half][:, :], (cath[:, k, c], catl[:, k, c]),
                                           (woh[:, k, d], wol[:, k, d]), k == 0, k == KC - 1)
                        last.then_inc(y_mm[l], 1)
                    if b:
                        pe.wait_ge(x_ok[l], b)
                        to_columns(l, 1, b - 1)

            def queries(l):
                NB = blocks_of(l)
                pe.wait_ge(keys_in[l], 16)
                pe.wait_ge(hl_ok[l], NB)
                with pe.Fori(0, PH) as i:
                    for s in range(2):
                        pe.wait_ge(wql_ok[l], i * 2 + (s + 1))
                        pe.wait_ge(q_ev[l], i * 2 + (s + 1))
                        for z, (c0, w) in enumerate(spans_of(l)):
                            for k in range(KC):
                                last = mm3(ps[2 * s + z][:, 0:w], (wqh[s][:, k, :], wql[s][:, k, :]),
                                           (hh[:, k, c0:c0 + w], hl[:, k, c0:c0 + w]), k == 0, k == KC - 1)
                        last.then_inc(q_mm[l], 1)
                    for s in range(2):
                        pe.wait_ge(q_ev[l], i * 2 + (s + 3))
                        pe.wait_ge(topk_ok[l], i * 2 + (s + 1))
                        for b in range(NB):
                            last = mm(ps[4 + 2 * s + b // 4][:, (b % 4) * P:(b % 4 + 1) * P], qs[s][:, b * P:(b + 1) * P], keys[:, s, :], True, True)
                        last.then_inc(s_mm[l], 1)

            def routing(l):
                NB = blocks_of(l)

                def turn(b, k):
                    pe.wait_ge(route_ok[l], b + (k + 1))
                    for j in range(3):
                        last = pe.transpose(ps[0][:, j * P:(j + 1) * P], route[:, j, :], ident[:, :])
                    last.then_inc(routeT_mm[l], 1)

                def matrices(b):
                    with pe.Fori(0, P // (2 * QT)) as i:
                        for h in range(2):
                            n = b * (P // QT) + i * 2
                            pe.wait_ge(hot2_ok[l], n + (h + 1))
                            pe.wait_ge(hotg_ok[l], n + (h + 1))
                            pe.wait_ge(hota_ok[l], n + (h + 1))
                            pe.wait_ge(g_ev[l], n + (h + 1))
                            for j in range(QT):
                                out = ps[1 + 2 * h + j // 4][:, (j % 4) * P:(j % 4 + 1) * P]
                                mm(out, oh2[h][:, :, j], oh1h[h][:, :, j], True, False)
                                last = mm(out, oh2[h][:, :, j], oh1l[h][:, :, j], False, True)
                            last.then_inc(g_mm[l], 1)

                turn(0, 0)
                with pe.Fori(0, NB - 1) as b:
                    matrices(b)
                    turn(b, 1)
                matrices(NB - 1)

            def experts(l):
                NB = blocks_of(l)
                outs = [(b, half) for b in range(NB) for half in range(2)]

                def group(g, mod):
                    for e in range(GRP):
                        if mod and e == 2:
                            for s in range(MS):
                                pe.wait_ge(f_ok[l], g * len(outs) + (s + 1))
                                mod_rows(l + 1, g * MS + s, s)
                        n = g * GRP + e
                        s = e % 2
                        pe.wait_ge(uh_ok[l], n + 1)
                        pe.wait_ge(ul_ok[l], n + 3)
                        pe.wait_ge(gelu_ok[l], n + 1)
                        for z, (c0, w) in enumerate(spans_of(l)):
                            out = ps[2 * s + z][:, 0:w]
                            for k in range(KC):
                                mm(out, ush[s][:, k, :], hh[:, k, c0:c0 + w], k == 0, False)
                                mm(out, ush[s][:, k, :], hl[:, k, c0:c0 + w], False, False)
                                last = mm(out, usl[s][:, k, :], hh[:, k, c0:c0 + w], False, k == KC - 1)
                        last.then_inc(u_mm[l], 1)
                    for r in range(0, len(outs), 4):
                        for es in (range(GRP - 1), (GRP - 1,)):
                            for j in range(4):
                                b, half = outs[r + j]
                                if r == 0 and j == 0:
                                    m = g * GRP + es[-1]
                                    pe.wait_ge(wh_ok[l], m + 1)
                                    pe.wait_ge(wl_ok[l], m + 1)
                                    pe.wait_ge(vh_ok[l], m + 1)
                                    pe.wait_ge(vl_ok[l], m + 3)
                                if mod and r == 0 and j == 0 and es != (GRP - 1,):
                                    pe.wait_ge(mod_ok[0], g * MS + (NMG * (l + 1) + 2 * MS))
                                if es != (GRP - 1,):
                                    pe.wait_ge(f_ok[l], g * len(outs) + (r + j + 1))
                                for e in es:
                                    wh, wl = wth[:, e, b * P:(b + 1) * P], wtl[:, e, b * P:(b + 1) * P]
                                    vh, vl = (v[:, e, half * 512:(half + 1) * 512] for v in (vsh, vsl))
                                    mm(ps[4 + j][:, :], wh, vh, e == 0, False)
                                    mm(ps[4 + j][:, :], wh, vl, False, False)
                                    last = mm(ps[4 + j][:, :], wl, vh, False, e == GRP - 1)
                                if es == (GRP - 1,):
                                    last.then_inc(v_mm[l], 1)

                for lo, hi, mod in group_runs(l, NGRP):
                    with pe.Fori(lo, hi) as g:
                        group(g, mod)

            for l in range(DEPTH):
                for stage in (modulation, columns, mixer, project, queries, routing, experts):
                    stage(l)
                    stages.end()
                if l < DEPTH - 1:
                    stages.begin()

        @block.scalar
        def _(act):
            stages = Stages(act)

            def copy(out, in_, scale=1.0):
                return act.activation(out, in_, ACT.Copy, scale=scale)

            def mod_store(run, n, s):
                act.wait_ge(mod_ok[0], n + (NMG * run + MS + 1))
                act.dma_start(t["mod"][run, :, ds(n * MODW, MODW)], modr[s][0:2, :]).then_inc(modr_out[s][0], 16)

            def modulation(l):
                if l == 0:
                    for s in range(MS):
                        act.sem_inc(modr_out[s][0], 16)
                    act.wait_ge(consts_in, 64)
                    act.activation(sT[:, :, :], cT[:, :, :], ACT.Silu).then_inc(silu_ok, 1)
                    act.wait_ge(eps_ok, 1)
                    with act.Fori(0, NMG // MS) as i:
                        for s in range(MS):
                            mod_store(0, i * MS + s, s)

            def to_columns(l, k, b):
                r = b // LAT_B
                n = 2 * b + 1
                act.wait_ge(tr_mm[k][l], n + 1)
                for j in range(4):
                    c = 4 + j
                    last = act.activation((hT, h2T)[k][:, c, b * P:(b + 1) * P], ps[4 + n % 4][:, j * P:(j + 1) * P], ACT.Identity,
                                          bias=modc[:, 3 * k * KC + c, r:r + 1], scale=modc[:, (3 * k + 1) * KC + c, r:r + 1])
                last.then_inc(tr_act[k][l], 1)

            def high(l, k, b, done):
                act.wait_ge(tr_dve[k][l], b + 1)
                act.wait_ge(tr_act[k][l], b + 1)
                c = slice(b * P, (b + 1) * P)
                copy(hh[:, :, c], (hT, h2T)[k][:, :, c], S_H).then_inc(done[l], 1)

            def columns(l):
                act.wait_ge(modc_ok[l], 1)
                for b in range(NBLK):
                    to_columns(l, 0, b)
                    high(l, 0, b, mh_ok)
                    if b == 2:
                        act.wait_ge(wv_in[l], 16)
                        copy(wvh, wv, S_U).then_inc(vgh_ok[l], 1)

            def w_split(l, r, landed):
                act.wait_ge(wr_in[r][l], landed)
                copy(wrh[r], wring[r], S_U).then_inc(wrh_ok[l], 1)

            def mixer(l):
                NB = blocks_of(l)
                act.sem_inc(head_ok[l], 1)
                act.wait_ge(wg_in[l], 16)
                copy(wgh, wg, S_U).then_inc(vgh_ok[l], 1)
                for n in range(NBLK + NB):
                    act.wait_ge(vg_mm[l], n + 1)
                    out, f = (v_nat[:, n, :], ACT.Copy) if n < NBLK else (g_nat[:, n - NBLK, :], ACT.Silu)
                    act.activation(out, ps[6 + n % 2][:, :], f, scale=INV).then_inc(vg_ev[l], 1)
                for r in range(3):
                    w_split(l, r, 16)

                act.wait_ge(vgl_ok[l], 2)

                def out_split(i, k):
                    act.wait_ge(wo_in[l], i * 32 + (16 * k + 16))
                    copy(woh[:, ds(i * 2 + k), :].rearrange("p a b -> p (a b)"), wo_raw, S_U).then_inc(woh_ok[l], 1)

                def channels(i, slots):
                    act.wait_ge(conv_mm[l], i * 3 + 1)
                    act.wait_ge(conv_ok[l], i + 1)
                    last = copy(cg_sb[:, 0:SEQ], ps[0][:, :], INV ** 3)
                    if NB > LAT_B:
                        last = copy(cg_sb[:, SEQ:TOK], ps[1][:, 0:CTX], INV ** 3)
                    last.then_inc(cg_ev[l], 1)
                    for r in range(slots):
                        act.wait_ge(conv_mm[l], i * 3 + (r + 1))
                        w_split(l, r, i * 16 + 32)
                        if r == 0:
                            out_split(i, 0)
                        if r == 1:
                            act.wait_ge(conv_ok[l], i + 2)
                            copy(cath[:, ds(i), 0:NB * P].rearrange("p a b -> p (a b)"), y_sb[:, 0:NB * P], S_H).then_inc(cath_ok[l], 1)
                            out_split(i, 1)

                with act.Fori(0, CCT - 1) as i:
                    channels(i, 3)
                channels(CCT - 1, 2)
                act.wait_ge(wol_ok[l], 2 * CCT)

                def qk(i, k):
                    for r, (raw, dst) in enumerate(((q_raw, qT), (k_raw, kT))):
                        act.wait_ge(qk_mm[l], i * 2 + (2 * k + r + 1))
                        last = copy(raw, ps[2 * r][:, :], INV)
                        if r or NB > LAT_B:
                            last = copy(dst[:, SEQ:TOK], ps[2 * r + 1][:, 0:CTX], INV)
                        last.then_inc(qk_ev[l], 1)

                def splits(i, k):
                    for r in range(2):
                        w_split(l, r, i * 16 + 16 * (CCT + k + 1))

                def spread(i):
                    act.wait_ge(var_ok[l], i + 1)
                    act.activation(sd[:, 0:NB], mv[:, 0:NB, 1], ACT.Sqrt, bias=eps[:, :]).then_inc(sd_ok[l], 1)

                def turned(i):
                    act.wait_ge(retT_mm[l], i + 2)
                    last = copy(cath[:, ds(i + CCT), 0:SEQ].rearrange("p a b -> p (a b)"), ps[4][:, :], S_H)
                    if NB > LAT_B:
                        last = copy(cath[:, ds(i + CCT), SEQ:TOK].rearrange("p a b -> p (a b)"), ps[5][:, 0:CTX], S_H)
                    last.then_inc(cath_ok[l], 1)

                qk(0, 0)
                splits(0, 1)
                qk(0, 1)
                with act.Fori(0, HEADS - 2) as i:
                    splits(i, 2)
                    spread(i)
                    qk(i, 2)
                    turned(i)
                for i in range(HEADS - 2, HEADS):
                    spread(i)
                    turned(i)

            def deviation(l, k, b):
                act.wait_ge(lnvar_ok[k][l], b + 1)
                act.activation(sd[:, b:b + 1], mv[:, b, 1:2], ACT.Sqrt, bias=eps[:, :]).then_inc(lnsd_ok[k][l], 1)

            def normalize(l, k, b):
                act.wait_ge(lnrs_ok[k][l], b + 1)
                act.activation(x[:, b, :], x[:, b, :], ACT.Identity, bias=nm[:, b:b + 1], scale=rs[:, b:b + 1]).then_inc(lnx_ok[k][l], 1)

            def project(l):
                NB = blocks_of(l)
                for s in range(2):
                    act.wait_ge(wq_in[s][l], 16)
                    copy(wqh[s], wq[s], S_U).then_inc(wqh_ok[l], 1)
                for b in range(NB + 1):
                    if b < NB:
                        deviation(l, 0, b)
                        normalize(l, 0, b)
                    if b:
                        to_columns(l, 1, b - 1)
                        high(l, 1, b - 1, hh_ok)

            def queries(l):
                act.sem_inc(q_ev[l], 2)
                def head(i, more):
                    for s in range(2):
                        act.wait_ge(q_mm[l], i * 2 + (s + 1))
                        for z, (c0, w) in enumerate(spans_of(l)):
                            last = copy(qs[s][:, c0:c0 + w], ps[2 * s + z][:, 0:w], INV)
                        last.then_inc(q_ev[l], 1)
                        if more:
                            act.wait_ge(wq_in[s][l], i * 16 + 32)
                            copy(wqh[s], wq[s], S_U).then_inc(wqh_ok[l], 1)

                with act.Fori(0, PH - 1) as i:
                    head(i, True)
                head(PH - 1, False)

            def routing(l):
                NB = blocks_of(l)
                act.sem_inc(g_ev[l], 2)

                def exponents(b, k):
                    act.wait_ge(expo_in[l], b + (k + 1))
                    act.activation(expo, expo, ACT.Exp).then_inc(expo_ok[l], 1)

                def turned(b, k):
                    act.wait_ge(routeT_mm[l], b + (k + 1))
                    copy(routeT[:, 0:2, :].rearrange("p a b -> p (a b)"), ps[0][:, 0:2 * P])
                    copy(routeT[:, 2, :], ps[0][:, 2 * P:3 * P], S_G).then_inc(routeT_ok[l], 1)

                def gated(b, i, h):
                    act.wait_ge(hot_ok[l], b * (P // QT) + i * 2 + (h + 1))
                    for j in range(QP, QT):
                        last = copy(oh1l[h % 2][:, :, j], oh1[h % 2][:, :, j], glowT[:, ds(i * (2 * QT) + (h * QT + j))])
                    last.then_inc(hota_ok[l], 1)

                def stored(b, half, i, h):
                    act.wait_ge(g_mm[l], b * (P // QT) + i * 2 + (h + 3))
                    for j in range(QT // 4):
                        last = copy(gbuf[half][:, :, ds(i * (2 * QT) + (h * QT + 4 * j - half * HT), 4)],
                                    ps[1 + 2 * h + j][:, :].rearrange("p (j i) -> p i j", j=4), 1.0 / S_G)
                    last.then_inc(g_ev[l], 1)

                def matrices(b):
                    act.wait_ge(glo_ok[l], b + 1)
                    gated(b, 0, 0)
                    steps = HT // (2 * QT)
                    for half in range(2):
                        act.wait_ge(g_out[half][l], b * 16 + 16)
                        with act.Fori(half * steps, (half + 1) * steps - half) as i:
                            for h in range(2):
                                gated(b, i, h + 1)
                                stored(b, half, i, h)
                    gated(b, 2 * steps - 1, 1)
                    stored(b, 1, 2 * steps - 1, 0)
                    stored(b, 1, 2 * steps - 1, 1)

                exponents(0, 0)
                exponents(1, 0)
                turned(0, 0)
                with act.Fori(0, NB - 2) as b:
                    matrices(b)
                    exponents(b, 2)
                    turned(b, 1)
                matrices(NB - 2)
                turned(NB - 2, 1)
                matrices(NB - 1)

            def experts(l):
                T = blocks_of(l) * P
                act.sem_inc(gelu_ok[l], 2)
                act.sem_inc(u_mm[l], 1)
                act.sem_inc(v_mm[l], 1)

                def group(g, more, mod):
                    for e in range(GRP):
                        s = e % 2
                        n = g * GRP + e
                        if e < GRP - 1 or more:
                            u_split(n + 1, (e + 1) % 2, g * (8 * GRP) + 16 * ((e + 1) // 2 + 1))
                        if e == 0:
                            act.wait_ge(v_mm[l], g * (2 * blocks_of(l)) + 1)
                        act.wait_ge(v_in[s][l], g * (8 * GRP) + 16 * (e // 2 + 1))
                        copy(vsh[:, e, :], vraw[s], S_V).then_inc(vh_ok[l], 1)
                        if mod and e == 3:
                            for k in range(MS):
                                mod_store(l + 1, g * MS + k, k)
                        act.wait_ge(u_mm[l], n + 2)
                        for z, (c0, w) in enumerate(spans_of(l)):
                            last = act.activation(actb[s][:, c0:c0 + w], ps[2 * s + z][:, 0:w], ACT.Gelu, scale=1.0 / (S_H * S_U))
                        last.then_inc(gelu_ok[l], 1)
                        act.wait_ge(wf_ok[l], n + (GRP + 1))
                        copy(wth[:, e, 0:T], wf[s][:, 0:T], S_W).then_inc(wh_ok[l], 1)

                def u_split(n, s, landed):
                    act.wait_ge(u_in[s][l], landed)
                    act.wait_ge(u_mm[l], n)
                    copy(ush[s], uraw[s], S_U).then_inc(uh_ok[l], 1)

                act.wait_ge(u_in[0][l], 16)
                copy(ush[0], uraw[0], S_U).then_inc(uh_ok[l], 1)
                for lo, hi, mod in group_runs(l, NGRP - 1):
                    with act.Fori(lo, hi) as g:
                        group(g, True, mod)
                group(NGRP - 1, False, False)
                for b in range(blocks_of(l)):
                    deviation(l, 1, b)
                    normalize(l, 1, b)

            for l in range(DEPTH):
                for stage in (modulation, columns, mixer, project, queries, routing, experts):
                    stage(l)
                    stages.end()
                if l < DEPTH - 1:
                    stages.begin()


        @block.gpsimd
        def _(pool):
            stages = Stages(pool)

            own = Own(pool, pool_chain)

            def nothing(l):
                pass

            def affine(l, k, rows):
                NB = blocks_of(l)
                pool.wait_ge(rows[l], 64 if NB > LAT_B else 48)
                for b in range(NB - k):
                    xb = x[:, b, :]
                    pool.wait_ge(lnx_ok[k][l], b + 1)
                    own.link(pool.tensor_tensor(xb, xb, lng[:, :], ALU.mult))
                    pool.tensor_tensor(xb, xb, lnb[:, :], ALU.add).then_inc((x_ok, x2_ok)[k][l], 1)

            def project(l):
                affine(l, 0, rows_in)

            def experts(l):
                affine(l, 1, rows2_in)

            def routing(l):
                NB = blocks_of(l)

                def indices(b, k):
                    sib = si[:, ds(b + k), :, :, :].rearrange("p b h s t -> p (b h) s t")
                    for s in range(2):
                        hot4 = hot[:, s, :, :].rearrange("p a (h t) -> p a h t", h=PH)
                        pool.wait_ge(rank_ok[l], b * 2 + (2 * k + s + 1))
                        pool.tensor_tensor(hot4, hot4, sib[:, :, s, :].rearrange("p h a -> p a h")[:, :, :, None].to_broadcast([P, TOPK, PH, TOPK]), ALU.mult).then_inc(rank_idx[l], 1)

                def gated(b):
                    pool.wait_ge(glo_ok[l], b + 1)
                    pool.sem_inc(pool_held, 1)
                    with pool.Fori(0, P // (2 * QT)) as i:
                        for h in range(2):
                            pool.wait_ge(hot_ok[l], b * (P // QT) + i * 2 + (h + 1))
                            pool.tensor_tensor(oh1l[h][:, :, 0:QP], oh1[h][:, :, 0:QP],
                                               routeT[:, 3, ds(i * (2 * QT) + h * QT, QP)][:, None, :].to_broadcast([P, NKEY, QP]), ALU.mult).then_inc(hotg_ok[l], 1)

                indices(0, 0)
                with pool.Fori(0, NB - 1) as b:
                    gated(b)
                    indices(b, 1)
                gated(NB - 1)

            for l in range(DEPTH):
                for stage in (nothing, nothing, nothing, project, nothing, routing, experts):
                    stage(l)
                    stages.end()
                if l < DEPTH - 1:
                    stages.begin()

        @block.vector
        def _(dve):
            stages = Stages(dve)
            own = Own(dve, dve_chain)
            link = own.link

            def hold():
                dve.sem_inc(dve_held, 1)

            def tt(out, a, b, op):
                return dve.tensor_tensor(out, a, b, op)

            def mod_rows(run, n, s):
                dve.wait_ge(mod_mm[0], n + (NMG * run + 1))
                dve.wait_ge(modr_out[s][0], n * (16 // MS) + (16 - 16 // MS * (s - NMG * run)))
                tt(modr[s][0:2, :], ps[4 + s][0:2, 0:MODW], bmodr[s][0:2, :], ALU.add).then_inc(mod_ok[0], 1)

            def modulation(l):
                if l == 0:
                    dve.memset(eps[:, :], EPS).then_inc(eps_ok, 1)
                    dve.sem_inc(mod_ok[0], MS)
                    dve.wait_ge(consts_in, 64)
                    with dve.Fori(0, NMG // MS) as i:
                        for s in range(MS):
                            mod_rows(0, i * MS + s, s)
                dve.wait_ge(modt_mm[l], 1)
                for r in range(2):
                    last = dve.tensor_copy(modc[:, :, r], ps[0][:, r * NMOD:(r + 1) * NMOD])
                link(last)
                dve.tensor_scalar(modc[:, KC:2 * KC, :], modc[:, KC:2 * KC, :], 1.0, None, ALU.add)
                dve.tensor_scalar(modc[:, 4 * KC:5 * KC, :], modc[:, 4 * KC:5 * KC, :], 1.0, None, ALU.add).then_inc(modc_ok[l], 1)
                dve.wait_ge(modc_ok[l], 1)

            def to_columns(l, k, b):
                r = b // LAT_B
                n = 2 * b
                dve.wait_ge(tr_mm[k][l], n + 1)
                for c in range(4):
                    last = dve.tensor_scalar((hT, h2T)[k][:, c, b * P:(b + 1) * P], ps[4 + n % 4][:, c * P:(c + 1) * P],
                                             modc[:, (3 * k + 1) * KC + c, r:r + 1], modc[:, 3 * k * KC + c, r:r + 1], ALU.mult, ALU.add)
                last.then_inc(tr_dve[k][l], 1)

            def low(out, raw, high, scale):
                return dve.scalar_tensor_tensor(out, raw, scale, high, ALU.mult, ALU.subtract)

            def columns(l):
                for b in range(NBLK):
                    to_columns(l, 0, b)
                    split_block(0, b, mh_ok[l], b + 1, ml_ok[l])
                    if b == 3:
                        dve.wait_ge(vgh_ok[l], 1)
                        low(wvl, wv, wvh, S_U).then_inc(vgl_ok[l], 1)

            def w_split(l, r, n):
                dve.wait_ge(wrh_ok[l], n)
                low(wrl[r], wring[r], wrh[r], S_U).then_inc(wrl_ok[l], 1)

            def taps(z, y, w0, w2):
                n = z.shape[-1]
                if len(z.shape) == 3:
                    link(dve.scalar_tensor_tensor(y[:, :, 1:n], z[:, :, 0:n - 1], w0, y[:, :, 1:n], ALU.mult, ALU.add))
                    link(dve.scalar_tensor_tensor(y[:, :, 0:n - 1], z[:, :, 1:n], w2, y[:, :, 0:n - 1], ALU.mult, ALU.add))
                else:
                    link(dve.scalar_tensor_tensor(y[:, 1:n], z[:, 0:n - 1], w0, y[:, 1:n], ALU.mult, ALU.add))
                    link(dve.scalar_tensor_tensor(y[:, 0:n - 1], z[:, 1:n], w2, y[:, 0:n - 1], ALU.mult, ALU.add))

            def mixer(l):
                NB = blocks_of(l)
                both = NB > LAT_B
                T = NB * P
                own.clear()
                dve.sem_inc(conv_ok[l], 1)
                dve.wait_ge(vgh_ok[l], 2)
                low(wgl, wg, wgh, S_U).then_inc(vgl_ok[l], 1)
                dve.wait_ge(cw_in[l], 48)
                for r in range(3):
                    w_split(l, r, r + 1)

                dve.wait_ge(vgl_ok[l], 2)

                def out_split(i, k):
                    dve.wait_ge(woh_ok[l], i * 2 + (k + 1))
                    low(wol[:, ds(i * 2 + k), :].rearrange("p a b -> p (a b)"), wo_raw,
                        woh[:, ds(i * 2 + k), :].rearrange("p a b -> p (a b)"), S_U).then_inc(wol_ok[l], 1)

                def cat_low(i, k, c0, w, source):
                    c = slice(c0, c0 + w)
                    return low(catl[:, ds(i + k), c].rearrange("p a b -> p (a b)"), source,
                               cath[:, ds(i + k), c].rearrange("p a b -> p (a b)"), S_H)

                def channels(i, slots):
                    w_split(l, 0, i * 3 + 4)
                    out_split(i, 0)
                    dve.wait_ge(cg_ev[l], i + 1)
                    dve.wait_ge(conv_mm[l], i * 3 + 2)
                    last = tt(z_sb[:, 0:SEQ], cg_sb[:, 0:SEQ], ps[2][:, :], ALU.mult)
                    if both:
                        last = tt(z_sb[:, SEQ:TOK], cg_sb[:, SEQ:TOK], ps[3][:, 0:CTX], ALU.mult)
                    link(last)
                    w_split(l, 1, i * 3 + 5)
                    w = [convw[:, ds(i), j:j + 1].rearrange("p a b -> p (a b)") for j in range(3)]
                    link(dve.tensor_scalar(y_sb[:, 0:T], z_sb[:, 0:T], w[1], None, ALU.mult))
                    taps(z_sb[:, 0:SEQ].rearrange("p (r c) -> p r c", c=GRID), y_sb[:, 0:SEQ].rearrange("p (r c) -> p r c", c=GRID), w[0], w[2])
                    if both:
                        taps(z_sb[:, SEQ:TOK], y_sb[:, SEQ:TOK], w[0], w[2])
                    dve.wait_ge(conv_mm[l], i * 3 + 3)
                    last = tt(y_sb[:, 0:SEQ], y_sb[:, 0:SEQ], ps[4][:, :], ALU.mult)
                    if both:
                        last = tt(y_sb[:, SEQ:TOK], y_sb[:, SEQ:TOK], ps[5][:, 0:CTX], ALU.mult)
                    last.then_inc(conv_ok[l], 1)
                    dve.wait_ge(cath_ok[l], i + 1)
                    link(cat_low(i, 0, 0, T, y_sb[:, 0:T]))
                    out_split(i, 1)
                    if slots == 3:
                        w_split(l, 2, i * 3 + 6)
                        dve.wait_ge(wrl_ok[l], i * 3 + 6)
                    else:
                        dve.wait_ge(conv_ok[l], i + 2)
                    hold()
                    own.clear()

                with dve.Fori(0, CCT - 1) as i:
                    channels(i, 3)
                channels(CCT - 1, 2)
                NS = nscore(l)

                def rope(i, k):
                    for r, (raw, dst) in enumerate(((q_raw, qT), (k_raw, kT))):
                        dve.wait_ge(rot_mm[l], i * 2 + (2 * k + r + 1))
                        link(tt(dst[:, 0:SEQ], raw, ropeC, ALU.mult))
                        link(tt(raw, ps[6 + r][:, :], ropeS, ALU.mult))
                        tt(dst[:, 0:SEQ], dst[:, 0:SEQ], raw, ALU.add).then_inc(rope_ok[l], 1)
                    dve.wait_ge(rope_ok[l], i * 2 + (2 * k + 2))

                def splits(i, k):
                    for r in range(2):
                        w_split(l, r, i * 2 + (3 * CCT + 2 * k + r + 1))

                def decays(i, k):
                    dve.wait_ge(strip_in[l], i * 32 + (32 * k + 32))
                    for n in range(NS):
                        dve.wait_ge(sc_mm[l], i * NS + (NS * k + n + 1))
                        if n < LAT_B:
                            a = 384 - P * n
                            tt(Psc[:, n, :], ps[6 + n % 2][:, :], strip1[:, a:a + SEQ], ALU.mult).then_inc(p_ok[l], 1)
                        elif n < NBLK:
                            a = P - P * (n - LAT_B)
                            tt(Psc[:, n, :], ps[6 + n % 2][:, :], strip2[:, a:a + SEQ], ALU.mult).then_inc(p_ok[l], 1)
                        else:
                            a = 384 - P * (n - NBLK)
                            tt(Pctx[:, n - NBLK, :], ps[6 + n % 2][:, 0:CTX], strip1[:, a:a + CTX], ALU.mult).then_inc(p_ok[l], 1)

                def turned(i):
                    dve.wait_ge(cath_ok[l], i + (CCT + 1))
                    last = cat_low(i, CCT, 0, SEQ, ps[4][:, :])
                    if both:
                        last = cat_low(i, CCT, SEQ, CTX, ps[5][:, 0:CTX])
                    last.then_inc(head_ok[l], 1)

                def normal(i):
                    dve.wait_ge(o_mm[l], i + 1)
                    for b in range(NB):
                        last = dve.bn_stats(gst[:, b, :], ps[4 + b // 4][:, (b % 4) * P:(b % 4 + 1) * P])
                    link(last)
                    for b in range(NB):
                        last = dve.bn_aggr(mv[:, b, :], gst[:, b, :])
                    last.then_inc(var_ok[l], 1)
                    dve.wait_ge(sd_ok[l], i + 1)
                    link(dve.reciprocal(rs[:, 0:NB], sd[:, 0:NB]))
                    dve.wait_ge(retT_mm[l], i + 1)
                    for b in range(NB):
                        last = dve.tensor_scalar(onrm[:, b, :], ps[4 + b // 4][:, (b % 4) * P:(b % 4 + 1) * P], mv[:, b, 0:1], rs[:, b:b + 1], ALU.subtract, ALU.mult)
                    link(last)
                    tt(onrm[:, 0:NB, :], onrm[:, 0:NB, :], g_nat[:, 0:NB, ds(i * P, P)], ALU.mult).then_inc(ret_ok[l], 1)
                    dve.wait_ge(ret_ok[l], i + 1)

                dve.sem_inc(retT_mm[l], 1)
                rope(0, 0)
                splits(0, 1)
                decays(0, 0)
                rope(0, 1)
                hold()
                own.clear()
                with dve.Fori(0, HEADS - 2) as i:
                    splits(i, 2)
                    decays(i, 1)
                    normal(i)
                    turned(i)
                    rope(i, 2)
                    hold()
                    own.clear()
                decays(HEADS - 2, 1)
                normal(HEADS - 2)
                turned(HEADS - 2)
                normal(HEADS - 1)
                turned(HEADS - 1)
                own.clear()

            def stats(l, k, b):
                dve.bn_stats(st[:, 0, :], x[:, b, 0:512])
                link(dve.bn_stats(st[:, 1, :], x[:, b, 512:D]))
                dve.bn_aggr(mv[:, b, :], st[:, :, :]).then_inc(lnvar_ok[k][l], 1)
                dve.wait_ge(lnvar_ok[k][l], b + 1)

            def factors(l, k, b):
                dve.wait_ge(lnsd_ok[k][l], b + 1)
                link(dve.reciprocal(rs[:, b:b + 1], sd[:, b:b + 1]))
                dve.scalar_tensor_tensor(nm[:, b:b + 1], mv[:, b, 0:1], -1.0, rs[:, b:b + 1], ALU.mult, ALU.mult).then_inc(lnrs_ok[k][l], 1)

            def split_block(k, b, high_done, n, low_done):
                dve.wait_ge(high_done, n)
                c = slice(b * P, (b + 1) * P)
                low(hl[:, :, c], (hT, h2T)[k][:, :, c], hh[:, :, c], S_H).then_inc(low_done, 1)

            def q_split(l, s, n):
                dve.wait_ge(wqh_ok[l], n)
                low(wql[s], wq[s], wqh[s], S_U).then_inc(wql_ok[l], 1)

            def project(l):
                NB = blocks_of(l)
                for s in range(2):
                    q_split(l, s, s + 1)
                dve.wait_ge(rows_in[l], 64 if NB > LAT_B else 48)
                for b in range(NB + 1):
                    if b < NB:
                        dve.wait_ge(y_mm[l], b + 1)
                        for half in range(2):
                            c = slice(half * 512, (half + 1) * 512)
                            last = dve.scalar_tensor_tensor(tmp[:, c], ps[b % 2 * 2 + half][:, :], INV, gate[:, b // LAT_B, c], ALU.mult, ALU.mult)
                        last.then_inc(y_used[l], 1)
                        dve.wait_ge(y_used[l], b + 1)
                        link(dve.scalar_tensor_tensor(x[:, b, :], x[:, b, :], ALPHA, tmp, ALU.mult, ALU.add))
                        stats(l, 0, b)
                        factors(l, 0, b)
                    if b:
                        to_columns(l, 1, b - 1)
                        split_block(1, b - 1, hh_ok[l], b, hl_ok[l])

            def queries(l):
                NB = blocks_of(l)
                dve.sem_inc(topk_ok[l], 2)
                own.clear()

                def head(i, more):
                    if more:
                        for s in range(2):
                            q_split(l, s, i * 2 + (s + 3))
                    for s in range(2):
                        dve.wait_ge(s_mm[l], i * 2 + (s + 1))
                        svj, sij = svj2[s], sij2[s]
                        hold()
                        sc = [ps[4 + 2 * s + b // 4][:, (b % 4) * P:(b % 4 + 1) * P] for b in range(NB)]
                        for b in range(NB):
                            last = dve.max(svj[:, b, 0:8], sc[b])
                        link(last)
                        for b in range(NB):
                            dve.max_index(sij[:, b, 0:8], svj[:, b, 0:8], sc[b])
                        for b in range(NB):
                            last = dve.match_replace(left[:, b, :], svj[:, b, 0:8], sc[b], NEG)
                        link(last)
                        for b in range(NB):
                            last = dve.max(svj[:, b, 8:16], left[:, b, :])
                        link(last)
                        for b in range(NB):
                            last = dve.max_index(sij[:, b, 8:16], svj[:, b, 8:16], left[:, b, :])
                        link(last)
                        dve.tensor_copy(sv[:, 0:NB, ds(i), s, :].rearrange("p b a t -> p b (a t)"), svj[:, 0:NB, :])
                        dve.tensor_copy(si[:, 0:NB, ds(i), s, :].rearrange("p b a t -> p b (a t)"), sij[:, 0:NB, :]).then_inc(topk_ok[l], 1)
                    dve.wait_ge(topk_ok[l], i * 2 + 4)
                    hold()
                    own.clear()

                with dve.Fori(0, PH - 1) as i:
                    head(i, True)
                head(PH - 1, False)

            def routing(l):
                NB = blocks_of(l)
                dve.sem_inc(g_mm[l], 2)
                dve.tensor_copy(iotar, iota[:, 0:TOPK, None].to_broadcast([P, TOPK, NR]))
                link(dve.tensor_copy(iotaq, iota[:, :, None].to_broadcast([P, NKEY, QT])))
                own.clear()

                def pairs(b, k):
                    svb = sv[:, ds(b + k), :, :, :].rearrange("p b h s t -> p (b h) s t")
                    for a0, na, nb, c0 in RECTS:
                        last = tt(cand[:, :, c0:c0 + na * nb].rearrange("p h (a b) -> p h a b", a=na),
                                  svb[:, :, 0, a0:a0 + na][:, :, :, None].to_broadcast([P, PH, na, nb]),
                                  svb[:, :, 1, 0:nb][:, :, None, :].to_broadcast([P, PH, na, nb]), ALU.add)
                    link(last)
                    for h in range(PH):
                        last = dve.max(cv[:, h, 0:8], cand[:, h, :])
                    link(last)
                    for h in range(PH):
                        dve.max_index(ci[:, h, 0:8], cv[:, h, 0:8], cand[:, h, :])
                    for h in range(PH):
                        last = dve.match_replace(cand2[:, h, :], cv[:, h, 0:8], cand[:, h, :], NEG)
                    link(last)
                    for h in range(PH):
                        last = dve.max(cv[:, h, 8:16], cand2[:, h, :])
                    link(last)
                    for h in range(PH):
                        last = dve.max_index(ci[:, h, 8:16], cv[:, h, 8:16], cand2[:, h, :])
                    gat = expo.rearrange("p (h t) -> p h t", h=PH)
                    link(last)
                    tt(gat, cv, cv[:, :, 0:1].to_broadcast([P, PH, TOPK]), ALU.subtract).then_inc(expo_in[l], 1)
                    cif = ci.rearrange("p h t -> p (h t)")
                    dve.tensor_scalar(shifted[:, 0, :], cif, 3, None, ALU.logical_shift_right)
                    dve.tensor_scalar(shifted[:, 1, :], cif, 2, None, ALU.logical_shift_right)
                    link(dve.tensor_copy(pos[:, 0, :], cif))
                    link(dve.tensor_copy(pos[:, 1:3, :], shifted[:, :, :]))
                    p0, p3, p2 = pos[:, 0, :], pos[:, 1, :], pos[:, 2, :]
                    for r in range(3):
                        dve.tensor_scalar(inrect[:, r, :], p0, float(RECTS[r + 1][3]), None, ALU.is_ge)
                    tt(part[:, 0, :], p2, p3, ALU.subtract)
                    link(tt(part[:, 1, :], p0, p2, ALU.subtract))
                    m1, m2, m3 = inrect[:, 0, :], inrect[:, 1, :], inrect[:, 2, :]
                    stt = dve.scalar_tensor_tensor
                    stt(rank[:, 0, :], p3, -1.0, m1, ALU.add, ALU.mult)
                    stt(part[:, 0, :], part[:, 0, :], -5.0, m2, ALU.add, ALU.mult)
                    stt(part[:, 1, :], part[:, 1, :], -42.0, m3, ALU.add, ALU.mult)
                    stt(part[:, 2, :], p3, 8.0, m1, ALU.mult, ALU.mult)
                    stt(part[:, 3, :], p3, -2.0, p2, ALU.mult, ALU.add)
                    link(stt(part[:, 4, :], p2, -4.0, p0, ALU.mult, ALU.add))
                    tt(rank[:, 0, :], rank[:, 0, :], part[:, 0, :], ALU.add)
                    stt(part[:, 3, :], part[:, 3, :], 4.0, m2, ALU.mult, ALU.mult)
                    tt(part[:, 4, :], part[:, 4, :], m3, ALU.mult)
                    link(tt(rank[:, 1, :], p0, part[:, 2, :], ALU.subtract))
                    tt(rankh[:, 0, :], rank[:, 0, :], part[:, 1, :], ALU.add)
                    link(tt(rank[:, 1, :], rank[:, 1, :], part[:, 3, :], ALU.subtract))
                    link(tt(rankh[:, 1, :], rank[:, 1, :], part[:, 4, :], ALU.subtract))
                    dve.wait_ge(expo_ok[l], b + (k + 1))
                    link(dve.reduce_sum(gsum, gat, axis=AX.X))
                    link(dve.reciprocal(gsum, gsum))
                    link(tt(gaten.rearrange("p (h t) -> p h t", h=PH), gat, gsum[:, :, None].to_broadcast([P, PH, TOPK]), ALU.mult))

                def one_hot_ranks(b, k):
                    if k:
                        dve.wait_ge(route_ok[l], b + k)
                        dve.wait_ge(routeT_mm[l], b + k)
                    for s in range(2):
                        tt(hot[:, s, :, :], iotar, rankh[:, s, None, :].to_broadcast([P, TOPK, NR]), ALU.is_equal).then_inc(rank_ok[l], 1)
                    link(dve.tensor_copy(route[:, 2, :], gaten))

                def indices(b, k):
                    dve.wait_ge(rank_idx[l], b * 2 + (2 * k + 2))
                    n = TOPK // 2
                    while n > 1:
                        link(tt(hot[:, :, 0:n, :], hot[:, :, 0:n, :], hot[:, :, n:2 * n, :], ALU.add))
                        n //= 2
                    tt(route[:, 0:2, :], hot[:, :, 0, :], hot[:, :, 1, :], ALU.add).then_inc(route_ok[l], 1)

                def matrices(b):
                    dve.wait_ge(routeT_ok[l], b + 1)
                    dve.scalar_tensor_tensor(glowT, ps[0][:, 2 * P:3 * P], S_G, routeT[:, 2, :], ALU.mult, ALU.subtract)
                    dve.scalar_tensor_tensor(routeT[:, 3, :], ps[0][:, 2 * P:3 * P], S_G, routeT[:, 2, :], ALU.mult, ALU.subtract).then_inc(glo_ok[l], 1)
                    with dve.Fori(0, P // (2 * QT)) as i:
                        for h in range(2):
                            n = b * (P // QT) + i * 2

                            def of_tokens(j):
                                return routeT[:, j, ds(i * (2 * QT) + h * QT, QT)][:, None, :].to_broadcast([P, NKEY, QT])

                            dve.wait_ge(g_mm[l], n + (h + 1))
                            tt(oh1[h], iotaq, of_tokens(0), ALU.is_equal).then_inc(hot_ok[l], 1)
                            tt(oh2[h], iotaq, of_tokens(1), ALU.is_equal)
                            dve.wait_ge(hot_ok[l], n + (h + 1))
                            tt(oh1h[h], oh1[h], of_tokens(2), ALU.mult).then_inc(hot2_ok[l], 1)

                def new_chain():
                    hold()
                    own.clear()

                pairs(0, 0)
                one_hot_ranks(0, 0)
                new_chain()
                pairs(1, 0)
                indices(0, 0)
                new_chain()
                with dve.Fori(0, NB - 2) as b:
                    matrices(b)
                    one_hot_ranks(b, 1)
                    new_chain()
                    pairs(b, 2)
                    indices(b, 1)
                    new_chain()
                matrices(NB - 2)
                one_hot_ranks(NB - 2, 1)
                indices(NB - 2, 1)
                new_chain()
                matrices(NB - 1)

            def affine2(l, b):
                xb = x[:, b, :]
                dve.wait_ge(lnx_ok[1][l], b + 1)
                link(tt(xb, xb, lng[:, :], ALU.mult))
                tt(xb, xb, lnb[:, :], ALU.add).then_inc(x2last_ok[l], 1)

            def norm2(l, b):
                link(dve.scalar_tensor_tensor(ftmp, facc[:, b, :], 1.0 / (S_W * S_V), gate[:, b // LAT_B, :], ALU.mult, ALU.mult))
                link(dve.scalar_tensor_tensor(x[:, b, :], x[:, b, :], ALPHA, ftmp, ALU.mult, ALU.add))
                stats(l, 1, b)

            def experts(l):
                NB = blocks_of(l)
                T = NB * P
                outs = [(b, half) for b in range(NB) for half in range(2)]
                dve.sem_inc(ul_ok[l], 2)
                dve.sem_inc(vl_ok[l], 2)
                dve.sem_inc(wf_ok[l], GRP)
                dve.sem_inc(f_ok[l], 4)

                def u_split(n, s):
                    dve.wait_ge(uh_ok[l], n + 1)
                    dve.scalar_tensor_tensor(usl[s], uraw[s], S_U, ush[s], ALU.mult, ALU.subtract).then_inc(ul_ok[l], 1)

                def group(g, more, mod):
                    for e in range(GRP):
                        if mod and e == 2:
                            for s in range(MS):
                                mod_rows(l + 1, g * MS + s, s)
                        s = e % 2
                        n = g * GRP + e
                        if e < GRP - 1 or more:
                            u_split(n + 1, (e + 1) % 2)
                        dve.wait_ge(vh_ok[l], n + 1)
                        dve.scalar_tensor_tensor(vsl[:, e, :], vraw[s], S_V, vsh[:, e, :], ALU.mult, ALU.subtract).then_inc(vl_ok[l], 1)
                        dve.wait_ge(gelu_ok[l], n + 3)
                        dve.wait_ge(g_in[e // 2][l], g * 16 + 16)
                        a3 = actb[s][:, 0:T].rearrange("p (b c) -> p b c", c=HT)
                        w3 = wf[s][:, 0:T].rearrange("p (b c) -> p b c", c=HT)
                        tt(w3, a3, graw[:, e // 2, 0:2 * NB, e % 2, :], ALU.mult).then_inc(wf_ok[l], 1)
                        dve.wait_ge(wh_ok[l], n + 1)
                        dve.scalar_tensor_tensor(wtl[:, e, 0:T], wf[s][:, 0:T], S_W, wth[:, e, 0:T], ALU.mult, ALU.subtract).then_inc(wl_ok[l], 1)
                    for j, (b, half) in enumerate(outs):
                        dve.wait_ge(v_mm[l], g * len(outs) + (j + 2))
                        f = facc[:, b, half * 512:(half + 1) * 512]
                        tt(f, f, ps[4 + j % 4][:, :], ALU.add).then_inc(f_ok[l], 1)
                        if not more and j % 4 == 3:
                            dve.wait_ge(f_ok[l], g * len(outs) + (j + 5))
                            if j == 3:
                                dve.wait_ge(rows2_in[l], 64 if NB > LAT_B else 48)
                            for m in (b - 1, b):
                                norm2(l, m)
                                if m:
                                    factors(l, 1, m - 1)
                    if not more:
                        factors(l, 1, NB - 1)
                        affine2(l, NB - 1)
                    dve.wait_ge(f_ok[l], g * len(outs) + (len(outs) + 4))

                u_split(0, 0)
                own.clear()
                link(dve.memset(facc[:, 0:NB, :], 0.0))
                for lo, hi, mod in group_runs(l, NGRP - 1):
                    with dve.Fori(lo, hi) as g:
                        group(g, True, mod)
                group(NGRP - 1, False, False)

            for l in range(DEPTH):
                for stage in (modulation, columns, mixer, project, queries, routing, experts):
                    stage(l)
                    stages.end()
                if l < DEPTH - 1:
                    stages.begin()


def layouts(inputs):
    import numpy as np

    a = {k: np.asarray(v) for k, v in inputs.items()}
    L = DEPTH
    out = {
        "x": np.concatenate([a["x"][0], a["ctx"][0]], 0),
        "c2": np.stack([a["c"][0], a["c_ctx"]], -1).reshape(KC, P, 2).transpose(1, 0, 2),
        "b_mod": a["b_mod"].reshape(L, NMG, MODW),
        "w_mod": a["w_mod"].reshape(L, KC, P, NMG, MODW).transpose(0, 3, 2, 1, 4),
        "w_in": a["w_in"].reshape(L, KC, P, NCOL, P).transpose(0, 3, 2, 1, 4),
        "w_v": a["w_in"][:, :, 5 * CONV:6 * CONV].reshape(L, KC, P, CONV).transpose(0, 2, 1, 3),
        "w_g": a["w_in"][:, :, 6 * CONV:].reshape(L, KC, P, CONV).transpose(0, 2, 1, 3),
        "conv_w": a["conv_w"].reshape(L, CCT, P, 3).transpose(0, 2, 1, 3),
        "w_out": a["w_out"].reshape(L, KC, P, D),
        "ln": np.stack([a["ln1_g"], a["ln1_b"], a["ln2_g"], a["ln2_b"]], 1),
        "w_q": a["peer_wq"].reshape(L, KC, P, 2 * PH, P).transpose(0, 3, 2, 1, 4),
        "keys": a["peer_keys"].transpose(0, 3, 1, 2),
        "peer_u": a["peer_u"].reshape(L, NKEY, P, KC, P).transpose(0, 1, 4, 3, 2),
        "peer_v": a["peer_v"].reshape(L, NKEY, P, D),
        "ident": np.eye(P),
        "iota": np.tile(np.arange(P), (P, 1)),
    }
    nf = P // 4
    d = np.arange(P)
    where = np.arange(SEQ)
    ang = np.where(d[:, None] < P // 2, where // GRID, where % GRID) * 10000.0 ** (-(d[:, None] % nf) / nf)
    out["ropeC"], out["ropeS"] = np.cos(ang), np.sin(ang)
    perm = np.zeros((P, P))
    for i in d:
        if i % (P // 2) < nf:
            perm[i + nf, i] = -1.0
        else:
            perm[i - nf, i] = 1.0
    out["perm"] = perm
    h = np.arange(HEADS)
    lf = np.log1p(-np.exp2(-(5.0 + h)))[:, None, None]
    lb = np.log1p(-np.exp2(-(5.5 + h)))[:, None, None]
    u = (np.arange(STRIP1)[None, :] - 384 - d[:, None])[None]
    out["strip1"] = np.where(u >= 0, np.exp(np.abs(u) * lf), np.exp(np.abs(u) * lb)) * P ** -0.5
    u = (np.arange(STRIP2)[None, :] - P - d[:, None])[None]
    out["strip2"] = (np.exp((u + CTX) * lf) + np.exp((SEQ - u) * lb)) * P ** -0.5
    return {k: np.ascontiguousarray(v, np.float32) for k, v in out.items()}


def kernel(**inputs):
    import concourse.bacc as bacc
    from concourse.bass_utils import run_bass_kernel_spmd

    arrays = layouts(inputs)
    nc = bacc.Bacc("TRN2", target_bir_lowering=False, num_devices=1)
    t = {k: nc.dram_tensor(f"in_{k}", v.shape, F32, kind="ExternalInput").ap() for k, v in arrays.items()}
    t["gates"] = nc.dram_tensor("gates", [2 * NBLK, P, NKEY, HT], F32, kind="Internal").ap()
    t["mod"] = nc.dram_tensor("mod", [DEPTH, 2, 6 * D], F32, kind="Internal").ap()
    t["out"] = nc.dram_tensor("out", [SEQ, D], F32, kind="ExternalOutput").ap()
    build(nc, t)
    r = run_bass_kernel_spmd(nc, [{f"in_{k}": v for k, v in arrays.items()}], core_ids=[0])
    return r.results[0]["out"].reshape(1, SEQ, D)
```
